# Optimizing a Trainium2 kernel written in Bass

```python
import numpy as np
import jax, jax.numpy as jnp
from jax import lax
import math

D_MODEL = 1024
BATCH = 1
SEQ = 512
DEPTH = 1

POOL_WINDOWS = (2, 4, 8, 16)
N_POOL_GROUPS = len(POOL_WINDOWS)
POOL_GROUP = D_MODEL // 8
POOL_WIDTH = POOL_GROUP * N_POOL_GROUPS
HEAD_DIM = 64
N_HEADS = D_MODEL // HEAD_DIM
N_KV_GROUPS = 2
HEADS_PER_GROUP = N_HEADS // N_KV_GROUPS
ATTN_WIDTH = N_HEADS * HEAD_DIM
N_NSA_BRANCHES = 3
KV_WIDTH = N_NSA_BRANCHES * 2 * N_KV_GROUPS * HEAD_DIM
CMP_BLOCK = 32
CMP_STRIDE = 16
CMP_HIDDEN = 128
SLC_BLOCK = 64
SLC_TOP_N = 8
WINDOW = 512
Q_BLOCK = 32
ROPE_THETA = 10000.0
SCALE = HEAD_DIM ** -0.5
FORCE_BONUS = 1000.0
NEG_INF = -1e30
N_MERGE = 2
OFF_Q = POOL_WIDTH
OFF_KV = OFF_Q + ATTN_WIDTH
OFF_NSA_G = OFF_KV + KV_WIDTH
OFF_MERGE_G = OFF_NSA_G + N_NSA_BRANCHES * N_HEADS
IN_WIDTH = OFF_MERGE_G + N_MERGE * D_MODEL
D_FF = 2752
CONV_WIDTH = 3
EPS = 1e-6


def rms_norm(x, w):
    xf = x.astype(jnp.float32)
    y = xf * lax.rsqrt(jnp.mean(xf * xf, axis=-1, keepdims=True) + EPS)
    return (y * w.astype(jnp.float32)).astype(x.dtype)

def rope(x, pos):
    half = HEAD_DIM // 2
    freqs = ROPE_THETA ** (-jnp.arange(half, dtype=jnp.float32) / half)
    ang = pos.astype(jnp.float32)[:, None] * freqs[None, :]
    shp = (1, pos.shape[0]) + (1,) * (x.ndim - 3) + (half,)
    cos = jnp.cos(ang).reshape(shp)
    sin = jnp.sin(ang).reshape(shp)
    xf = x.astype(jnp.float32)
    x1, x2 = xf[..., :half], xf[..., half:]
    return jnp.concatenate([x1 * cos - x2 * sin, x2 * cos + x1 * sin], axis=-1).astype(x.dtype)

def masked_softmax(s, mask):
    s = jnp.where(mask, s.astype(jnp.float32), NEG_INF)
    p = jax.nn.softmax(s, axis=-1)
    return jnp.where(mask, p, 0.0)

def pool_mixer(u, pool_w, pool_scale):
    B, S, _ = u.shape
    ug = u.reshape(B, S, N_POOL_GROUPS, POOL_GROUP).astype(jnp.float32)
    c = jnp.pad(jnp.cumsum(ug, axis=1), ((0, 0), (1, 0), (0, 0), (0, 0)))
    t = jnp.arange(S)
    outs = []
    for gi, w in enumerate(POOL_WINDOWS):
        lo = jnp.maximum(t + 1 - w, 0)
        cnt = jnp.minimum(t + 1, w).astype(jnp.float32)
        outs.append((c[:, 1:, gi] - c[:, lo, gi]) / cnt[None, :, None])
    pooled = jnp.stack(outs, axis=2) - ug
    y = jnp.einsum('bsgc,gcd->bsgd', pooled.astype(u.dtype), pool_w)
    return y.reshape(B, S, POOL_WIDTH) * pool_scale

def compress(k, pos_emb, w1, b1, w2):
    B, S = k.shape[0], k.shape[1]
    n_cmp = (S - CMP_BLOCK) // CMP_STRIDE + 1
    idx = np.arange(n_cmp)[:, None] * CMP_STRIDE + np.arange(CMP_BLOCK)[None, :]
    blk = k[:, idx] + pos_emb[None, None, :, None, :]
    flat = jnp.moveaxis(blk, 3, 2).reshape(B, n_cmp, N_KV_GROUPS, CMP_BLOCK * HEAD_DIM)
    hid = jax.nn.gelu(flat @ w1 + b1)
    return hid @ w2

def nsa_attention(q, k, v, nsa_g, cmp_pos, cmp_w1, cmp_b1, cmp_w2):
    B, S = q.shape[0], q.shape[1]
    k_c, k_s, k_w = k[:, :, 0], k[:, :, 1], k[:, :, 2]
    v_c, v_s, v_w = v[:, :, 0], v[:, :, 1], v[:, :, 2]
    k_cmp = compress(k_c, cmp_pos[0], cmp_w1[0], cmp_b1[0], cmp_w2[0])
    v_cmp = compress(v_c, cmp_pos[1], cmp_w1[1], cmp_b1[1], cmp_w2[1])
    n_cmp = k_cmp.shape[1]
    cmp_end = jnp.asarray(np.arange(n_cmp) * CMP_STRIDE + CMP_BLOCK - 1, dtype=jnp.int32)
    n_slc = S // SLC_BLOCK
    n_sel = min(SLC_TOP_N, n_slc)
    ci = np.arange(n_cmp)[:, None]
    sj = np.arange(n_slc)[None, :]
    overlap = jnp.asarray(((ci * CMP_STRIDE < (sj + 1) * SLC_BLOCK) &
                           (ci * CMP_STRIDE + CMP_BLOCK > sj * SLC_BLOCK)).astype(np.float32))
    ks_blk = k_s.reshape(B, n_slc, SLC_BLOCK, N_KV_GROUPS, HEAD_DIM).transpose(0, 3, 1, 2, 4)
    vs_blk = v_s.reshape(B, n_slc, SLC_BLOCK, N_KV_GROUPS, HEAD_DIM).transpose(0, 3, 1, 2, 4)
    pad = ((0, 0), (WINDOW, 0), (0, 0), (0, 0))
    kw_pad = jnp.pad(k_w, pad)
    vw_pad = jnp.pad(v_w, pad)
    b_ix = jnp.arange(B)[:, None, None, None]
    g_ix = jnp.arange(N_KV_GROUPS)[None, :, None, None]
    blk_ids = jnp.arange(n_slc)

    def chunk(args):
        qc, gc, start = args
        tq = start + jnp.arange(Q_BLOCK)
        qg = qc.reshape(B, Q_BLOCK, N_KV_GROUPS, HEADS_PER_GROUP, HEAD_DIM)
        s_c = jnp.einsum('bqghd,bngd->bghqn', qg, k_cmp)
        p_c = masked_softmax(s_c, cmp_end[None, :] <= tq[:, None])
        o_c = jnp.einsum('bghqn,bngd->bqghd', p_c.astype(v_cmp.dtype), v_cmp)
        imp = jnp.einsum('bghqn,nj->bgqj', p_c, overlap)
        cur = tq // SLC_BLOCK
        forced = ((blk_ids[None] == 0) | (blk_ids[None] == cur[:, None]) |
                  (blk_ids[None] == cur[:, None] - 1)).astype(jnp.float32)
        valid_b = blk_ids[None] * SLC_BLOCK <= tq[:, None]
        score = jnp.where(valid_b, imp + FORCE_BONUS * forced, NEG_INF)
        _, idx = lax.top_k(score, n_sel)
        kg = ks_blk[b_ix, g_ix, idx]
        vg = vs_blk[b_ix, g_ix, idx]
        m_tok = n_sel * SLC_BLOCK
        kpos = idx[..., None] * SLC_BLOCK + jnp.arange(SLC_BLOCK)
        mask_s = (kpos <= tq[None, None, :, None, None]).reshape(B, N_KV_GROUPS, 1, Q_BLOCK, m_tok)
        s_s = jnp.einsum('bqghd,bgqnld->bghqnl', qg, kg).reshape(B, N_KV_GROUPS, HEADS_PER_GROUP, Q_BLOCK, m_tok)
        p_s = masked_softmax(s_s, mask_s)
        o_s = jnp.einsum('bghqm,bgqmd->bqghd', p_s.astype(vg.dtype),
                         vg.reshape(B, N_KV_GROUPS, Q_BLOCK, m_tok, HEAD_DIM))
        kw = lax.dynamic_slice_in_dim(kw_pad, start, Q_BLOCK + WINDOW, axis=1)
        vw = lax.dynamic_slice_in_dim(vw_pad, start, Q_BLOCK + WINDOW, axis=1)
        kp = start - WINDOW + jnp.arange(Q_BLOCK + WINDOW)
        dist = tq[:, None] - kp[None, :]
        mask_w = (dist >= 0) & (dist < WINDOW) & (kp[None, :] >= 0)
        s_w = jnp.einsum('bqghd,bkgd->bghqk', qg, kw)
        p_w = masked_softmax(s_w, mask_w)
        o_w = jnp.einsum('bghqk,bkgd->bqghd', p_w.astype(vw.dtype), vw)
        gc = gc.reshape(B, Q_BLOCK, N_KV_GROUPS, HEADS_PER_GROUP, N_NSA_BRANCHES)
        o = gc[..., 0:1] * o_c + gc[..., 1:2] * o_s + gc[..., 2:3] * o_w
        return o.reshape(B, Q_BLOCK, ATTN_WIDTH)

    n_q = S // Q_BLOCK
    q_chunks = q.reshape(B, n_q, Q_BLOCK, N_HEADS, HEAD_DIM).transpose(1, 0, 2, 3, 4)
    g_chunks = nsa_g.reshape(B, n_q, Q_BLOCK, N_HEADS, N_NSA_BRANCHES).transpose(1, 0, 2, 3, 4)
    starts = jnp.arange(n_q, dtype=jnp.int32) * Q_BLOCK
    out = lax.map(chunk, (q_chunks, g_chunks, starts))
    return out.transpose(1, 0, 2, 3).reshape(B, S, ATTN_WIDTH)

def token_mixer(h, w_in, pool_w, pool_scale, q_norm_w, k_norm_w, cmp_pos, cmp_w1, cmp_b1,
                cmp_w2, w_pool_br, w_attn_br, w_o):
    B, S, _ = h.shape
    z = h @ w_in
    u_pool = z[..., :OFF_Q]
    q = z[..., OFF_Q:OFF_KV].reshape(B, S, N_HEADS, HEAD_DIM)
    kv = z[..., OFF_KV:OFF_NSA_G].reshape(B, S, N_NSA_BRANCHES, 2, N_KV_GROUPS, HEAD_DIM)
    nsa_g = jax.nn.sigmoid(z[..., OFF_NSA_G:OFF_MERGE_G].astype(jnp.float32)).astype(h.dtype)
    nsa_g = nsa_g.reshape(B, S, N_HEADS, N_NSA_BRANCHES)
    merge_g = jax.nn.sigmoid(z[..., OFF_MERGE_G:].astype(jnp.float32)).astype(h.dtype)
    merge_g = merge_g.reshape(B, S, N_MERGE, D_MODEL)
    pos = jnp.arange(S)
    q = rope(rms_norm(q, q_norm_w), pos) * SCALE
    k = rope(rms_norm(kv[:, :, :, 0], k_norm_w[:, None, :]), pos)
    v = kv[:, :, :, 1]
    y_pool = pool_mixer(u_pool, pool_w, pool_scale) @ w_pool_br
    y_attn = nsa_attention(q, k, v, nsa_g, cmp_pos, cmp_w1, cmp_b1, cmp_w2) @ w_attn_br
    merged = merge_g[:, :, 0] * y_pool + merge_g[:, :, 1] * y_attn
    return merged @ w_o

def conv_ffn(h, w_up, conv_w, conv_b, w_down):
    S = h.shape[1]
    u = h @ w_up
    up = jnp.pad(u, ((0, 0), (CONV_WIDTH - 1, 0), (0, 0)))
    c = conv_b + conv_w[0] * up[:, 0:S]
    for tap in range(1, CONV_WIDTH):
        c = c + conv_w[tap] * up[:, tap:tap + S]
    gate, val = jnp.split(c, 2, axis=-1)
    return (jax.nn.silu(gate) * val) @ w_down

def first_inputs(seed: int = 0) -> dict:
    key = jax.random.key(seed)
    ks = jax.random.split(key, 20)
    f32 = jnp.float32
    nrm = lambda k, shape, s: jax.random.normal(k, shape, f32) * s
    L = DEPTH
    return {
        "x": jax.random.normal(ks[0], (BATCH, SEQ, D_MODEL), f32),
        "attn_norm_w": 1.0 + nrm(ks[1], (L, D_MODEL), 0.05),
        "w_in": nrm(ks[2], (L, D_MODEL, IN_WIDTH), D_MODEL ** -0.5),
        "pool_w": nrm(ks[3], (L, N_POOL_GROUPS, POOL_GROUP, POOL_GROUP), POOL_GROUP ** -0.5),
        "pool_scale": 1.0 + nrm(ks[4], (L, POOL_WIDTH), 0.1),
        "q_norm_w": 1.0 + nrm(ks[5], (L, HEAD_DIM), 0.05),
        "k_norm_w": 1.0 + nrm(ks[6], (L, N_NSA_BRANCHES, HEAD_DIM), 0.05),
        "cmp_pos": nrm(ks[7], (L, 2, CMP_BLOCK, HEAD_DIM), 0.5),
        "cmp_w1": nrm(ks[8], (L, 2, CMP_BLOCK * HEAD_DIM, CMP_HIDDEN), (CMP_BLOCK * HEAD_DIM) ** -0.5),
        "cmp_b1": nrm(ks[9], (L, 2, CMP_HIDDEN), 0.02),
        "cmp_w2": nrm(ks[10], (L, 2, CMP_HIDDEN, HEAD_DIM), CMP_HIDDEN ** -0.5),
        "w_pool_br": nrm(ks[11], (L, POOL_WIDTH, D_MODEL), POOL_WIDTH ** -0.5),
        "w_attn_br": nrm(ks[12], (L, ATTN_WIDTH, D_MODEL), ATTN_WIDTH ** -0.5),
        "w_o": nrm(ks[13], (L, D_MODEL, D_MODEL), D_MODEL ** -0.5),
        "ffn_norm_w": 1.0 + nrm(ks[14], (L, D_MODEL), 0.05),
        "w_up": nrm(ks[15], (L, D_MODEL, 2 * D_FF), D_MODEL ** -0.5),
        "conv_w": nrm(ks[16], (L, CONV_WIDTH, 2 * D_FF), CONV_WIDTH ** -0.5),
        "conv_b": nrm(ks[17], (L, 2 * D_FF), 0.02),
        "w_down": nrm(ks[18], (L, D_FF, D_MODEL), D_FF ** -0.5),
    }

def first_block(x, attn_norm_w, w_in, pool_w, pool_scale, q_norm_w, k_norm_w, cmp_pos, cmp_w1,
              cmp_b1, cmp_w2, w_pool_br, w_attn_br, w_o, ffn_norm_w, w_up, conv_w, conv_b, w_down):
    for l in range(DEPTH):
        h = rms_norm(x, attn_norm_w[l])
        x = x + token_mixer(h, w_in[l], pool_w[l], pool_scale[l], q_norm_w[l], k_norm_w[l],
                            cmp_pos[l], cmp_w1[l], cmp_b1[l], cmp_w2[l], w_pool_br[l],
                            w_attn_br[l], w_o[l])
        h = rms_norm(x, ffn_norm_w[l])
        x = x + conv_ffn(h, w_up[l], conv_w[l], conv_b[l], w_down[l])
    return x


DEPTH_2 = 2

DA_HEADS = 8
DA_HEAD_DIM = 64
DA_WIDTH = DA_HEADS * 2 * DA_HEAD_DIM
SSD_WIDTH = D_MODEL
SSD_HEAD_DIM = 64
SSD_HEADS = SSD_WIDTH // SSD_HEAD_DIM
SSD_GROUPS = 2
SSD_STATE = 128
SSD_CONV = 4
SSD_CHUNK = 128
SSD_CONV_DIM = SSD_WIDTH + 2 * SSD_GROUPS * SSD_STATE
SW_HEADS = 16
SW_KV_HEADS = 2
SW_GQ = SW_HEADS // SW_KV_HEADS
SW_HEAD_DIM = 64
SW_WIDTH = SW_HEADS * SW_HEAD_DIM
SW_KV_WIDTH = SW_KV_HEADS * SW_HEAD_DIM
WINDOW_2 = 128
Q_BLOCK_2 = 128
EPS_2 = 1e-5

N_EVEN = (DEPTH_2 + 1) // 2
N_ODD = DEPTH_2 // 2
EVEN_IN = 4 * DA_WIDTH + SSD_WIDTH + SSD_CONV_DIM + SSD_HEADS
EVEN_SPLITS = [DA_WIDTH, 2 * DA_WIDTH, 3 * DA_WIDTH, 4 * DA_WIDTH,
               4 * DA_WIDTH + SSD_WIDTH, 4 * DA_WIDTH + SSD_WIDTH + SSD_CONV_DIM]
ODD_IN = 2 * SW_WIDTH + 2 * SW_KV_WIDTH
ODD_SPLITS = [SW_WIDTH, SW_WIDTH + SW_KV_WIDTH, SW_WIDTH + 2 * SW_KV_WIDTH]


def rmsnorm(x, w):
    xf = x.astype(jnp.float32)
    y = xf * lax.rsqrt(jnp.mean(xf * xf, axis=-1, keepdims=True) + EPS_2)
    return (y * w.astype(jnp.float32)).astype(x.dtype)

def alibi_slopes(n):
    return jnp.exp2(-8.0 * jnp.arange(1, n + 1, dtype=jnp.float32) / n)

def diff_attention(q, k, v, lam, slopes):
    b, s = q.shape[:2]
    nb = s // Q_BLOCK_2
    scale = DA_HEAD_DIM ** -0.5
    qb = q.reshape(b, nb, Q_BLOCK_2, DA_HEADS, 2, DA_HEAD_DIM).transpose(1, 0, 2, 3, 4, 5)
    kpos = jnp.arange(s)

    def block(args):
        qi, n = args
        qpos = n * Q_BLOCK_2 + jnp.arange(Q_BLOCK_2)
        dist = qpos[:, None] - kpos[None, :]
        logits = jnp.einsum('bqhmd,bshmd->bhmqs', qi, k).astype(jnp.float32) * scale
        logits = logits - slopes[None, :, None, None, None] * dist.astype(jnp.float32)[None, None, None]
        logits = jnp.where((dist >= 0)[None, None, None], logits, -jnp.inf)
        p = jax.nn.softmax(logits, axis=-1)
        attn = p[:, :, 0] - lam * p[:, :, 1]
        return jnp.einsum('bhqs,bshe->bqhe', attn.astype(v.dtype), v)

    out = lax.map(block, (qb, jnp.arange(nb)))
    return out.transpose(1, 0, 2, 3, 4).reshape(b, s, DA_HEADS, 2 * DA_HEAD_DIM)

def causal_dwconv(x, w, bias):
    c = x.shape[-1]
    y = lax.conv_general_dilated(x, w[:, None, :].astype(x.dtype), window_strides=(1,),
                                 padding=[(SSD_CONV - 1, 0)],
                                 dimension_numbers=('NWC', 'WIO', 'NWC'),
                                 feature_group_count=c)
    return y + bias.astype(x.dtype)

def segsum(a):
    cs = jnp.cumsum(a, axis=-1)
    diff = cs[..., :, None] - cs[..., None, :]
    n = a.shape[-1]
    mask = jnp.tril(jnp.ones((n, n), dtype=bool))
    return jnp.where(mask, diff, -jnp.inf)

def ssd_scan(xh, dt, A, bm, cm):
    b, s = xh.shape[:2]
    nc = s // SSD_CHUNK
    hpg = SSD_HEADS // SSD_GROUPS
    dtype = xh.dtype
    xdt = (xh * dt[..., None].astype(dtype)).reshape(b, nc, SSD_CHUNK, SSD_GROUPS, hpg, SSD_HEAD_DIM)
    bc = bm.reshape(b, nc, SSD_CHUNK, SSD_GROUPS, SSD_STATE)
    cc = cm.reshape(b, nc, SSD_CHUNK, SSD_GROUPS, SSD_STATE)
    dA = (dt * A).reshape(b, nc, SSD_CHUNK, SSD_GROUPS, hpg).transpose(0, 1, 3, 4, 2)
    cs = jnp.cumsum(dA, axis=-1)
    lmat = jnp.exp(segsum(dA)).astype(dtype)
    cb = jnp.einsum('bclgn,bcsgn->bcgls', cc, bc)
    y_diag = jnp.einsum('bcgjls,bcsgjp->bclgjp', cb[:, :, :, None] * lmat, xdt)
    decay_states = jnp.exp(cs[..., -1:] - cs).astype(dtype)
    states = jnp.einsum('bclgn,bcgjl,bclgjp->bcgjpn', bc, decay_states, xdt)
    chunk_decay = jnp.exp(cs[..., -1]).astype(dtype)

    def step(h, inp):
        st, dec = inp
        return h * dec[..., None, None] + st, h

    h0 = jnp.zeros((b, SSD_GROUPS, hpg, SSD_HEAD_DIM, SSD_STATE), dtype)
    _, prev = lax.scan(step, h0, (states.transpose(1, 0, 2, 3, 4, 5), chunk_decay.transpose(1, 0, 2, 3)))
    prev = prev.transpose(1, 0, 2, 3, 4, 5)
    y_off = jnp.einsum('bclgn,bcgjpn,bcgjl->bclgjp', cc, prev, jnp.exp(cs).astype(dtype))
    return (y_diag + y_off).reshape(b, s, SSD_HEADS, SSD_HEAD_DIM)

def sliding_window_attention(q, k, v, sinks, slopes):
    b, s = q.shape[:2]
    nb = s // WINDOW_2
    scale = SW_HEAD_DIM ** -0.5
    qb = q.reshape(b, nb, WINDOW_2, SW_KV_HEADS, SW_GQ, SW_HEAD_DIM)
    kb = k.reshape(b, nb, WINDOW_2, SW_KV_HEADS, SW_HEAD_DIM)
    vb = v.reshape(b, nb, WINDOW_2, SW_KV_HEADS, SW_HEAD_DIM)
    pad = ((0, 0), (1, 0), (0, 0), (0, 0), (0, 0))
    kk = jnp.concatenate([jnp.pad(kb, pad)[:, :-1], kb], axis=2)
    vv = jnp.concatenate([jnp.pad(vb, pad)[:, :-1], vb], axis=2)
    logits = jnp.einsum('bnqkgd,bnskd->bnkgqs', qb, kk).astype(jnp.float32) * scale
    qrel = jnp.arange(WINDOW_2) + WINDOW_2
    krel = jnp.arange(2 * WINDOW_2)
    dist = qrel[:, None] - krel[None, :]
    key_abs = (jnp.arange(nb) * WINDOW_2 - WINDOW_2)[:, None] + krel[None, :]
    valid = ((dist >= 0) & (dist < WINDOW_2))[None] & (key_abs >= 0)[:, None, :]
    sl = slopes.reshape(SW_KV_HEADS, SW_GQ)[None, None, :, :, None, None]
    logits = logits - sl * dist.astype(jnp.float32)
    logits = jnp.where(valid[None, :, None, None], logits, -jnp.inf)
    sink = jnp.broadcast_to(sinks.astype(jnp.float32).reshape(SW_KV_HEADS, SW_GQ)[None, None, :, :, None, None],
                            logits.shape[:-1] + (1,))
    p = jax.nn.softmax(jnp.concatenate([logits, sink], axis=-1), axis=-1)[..., :-1]
    out = jnp.einsum('bnkgqs,bnskd->bnqkgd', p.astype(v.dtype), vv)
    return out.reshape(b, s, SW_WIDTH)

def even_layer(h, w_in, conv_w, conv_b, dt_bias, a_log, d_skip, ssd_norm_w,
               lq1, lk1, lq2, lk2, subln_w, w_out, lambda_init):
    b, s, _ = h.shape
    proj = h @ w_in
    q, k, v, g_a, z, xbc, dt_raw = jnp.split(proj, EVEN_SPLITS, axis=-1)
    q = q.reshape(b, s, DA_HEADS, 2, DA_HEAD_DIM)
    k = k.reshape(b, s, DA_HEADS, 2, DA_HEAD_DIM)
    v = v.reshape(b, s, DA_HEADS, 2 * DA_HEAD_DIM)
    f32 = jnp.float32
    lam = (jnp.exp(jnp.sum(lq1.astype(f32) * lk1.astype(f32)))
           - jnp.exp(jnp.sum(lq2.astype(f32) * lk2.astype(f32))) + lambda_init)
    attn = diff_attention(q, k, v, lam, alibi_slopes(DA_HEADS))
    attn = rmsnorm(attn, subln_w) * (1.0 - lambda_init)
    y_a = attn.reshape(b, s, DA_WIDTH) * jax.nn.silu(g_a)
    xbc = jax.nn.silu(causal_dwconv(xbc, conv_w, conv_b))
    xs, bm, cm = jnp.split(xbc, [SSD_WIDTH, SSD_WIDTH + SSD_GROUPS * SSD_STATE], axis=-1)
    xh = xs.reshape(b, s, SSD_HEADS, SSD_HEAD_DIM)
    dt = jax.nn.softplus(dt_raw.astype(f32) + dt_bias.astype(f32))
    A = -jnp.exp(a_log.astype(f32))
    y = ssd_scan(xh, dt, A, bm.reshape(b, s, SSD_GROUPS, SSD_STATE), cm.reshape(b, s, SSD_GROUPS, SSD_STATE))
    y = y + xh * d_skip[:, None].astype(xh.dtype)
    y = y.reshape(b, s, SSD_WIDTH) * jax.nn.silu(z)
    y_b = rmsnorm(y.reshape(b, s, SSD_GROUPS, SSD_WIDTH // SSD_GROUPS),
                  ssd_norm_w.reshape(SSD_GROUPS, SSD_WIDTH // SSD_GROUPS)).reshape(b, s, SSD_WIDTH)
    return jnp.concatenate([y_a, y_b], axis=-1) @ w_out

def odd_layer(h, w_in, b_in, sinks, w_out):
    b, s, _ = h.shape
    proj = h @ w_in + b_in
    q, k, v, g = jnp.split(proj, ODD_SPLITS, axis=-1)
    q = q.reshape(b, s, SW_KV_HEADS, SW_GQ, SW_HEAD_DIM)
    k = k.reshape(b, s, SW_KV_HEADS, SW_HEAD_DIM)
    v = v.reshape(b, s, SW_KV_HEADS, SW_HEAD_DIM)
    o = sliding_window_attention(q, k, v, sinks, alibi_slopes(SW_HEADS))
    return (o * jax.nn.silu(g)) @ w_out

def second_inputs(seed: int = 0) -> dict:
    key = jax.random.key(seed)
    ks = jax.random.split(key, 24)
    f32 = jnp.float32

    def nrm(k, shape, scale):
        return jax.random.normal(k, shape, f32) * scale

    dt0 = jnp.exp(jax.random.uniform(ks[5], (N_EVEN, SSD_HEADS), f32, math.log(1e-3), math.log(1e-1)))
    return {
        "x": nrm(ks[0], (BATCH, SEQ, D_MODEL), 1.0),
        "norm_a": 1.0 + nrm(ks[1], (N_EVEN, D_MODEL), 0.02),
        "w_in_a": nrm(ks[2], (N_EVEN, D_MODEL, EVEN_IN), D_MODEL ** -0.5),
        "conv_w_a": nrm(ks[3], (N_EVEN, SSD_CONV, SSD_CONV_DIM), SSD_CONV ** -0.5),
        "conv_b_a": nrm(ks[4], (N_EVEN, SSD_CONV_DIM), 0.02),
        "dt_bias_a": dt0 + jnp.log(-jnp.expm1(-dt0)),
        "a_log_a": jnp.log(jax.random.uniform(ks[6], (N_EVEN, SSD_HEADS), f32, 1.0, 16.0)),
        "d_skip_a": 1.0 + nrm(ks[7], (N_EVEN, SSD_HEADS), 0.1),
        "ssd_norm_a": 1.0 + nrm(ks[8], (N_EVEN, SSD_WIDTH), 0.02),
        "lambda_q1_a": nrm(ks[9], (N_EVEN, DA_HEAD_DIM), 0.1),
        "lambda_k1_a": nrm(ks[10], (N_EVEN, DA_HEAD_DIM), 0.1),
        "lambda_q2_a": nrm(ks[11], (N_EVEN, DA_HEAD_DIM), 0.1),
        "lambda_k2_a": nrm(ks[12], (N_EVEN, DA_HEAD_DIM), 0.1),
        "subln_a": 1.0 + nrm(ks[13], (N_EVEN, 2 * DA_HEAD_DIM), 0.02),
        "w_out_a": nrm(ks[14], (N_EVEN, DA_WIDTH + SSD_WIDTH, D_MODEL), (DA_WIDTH + SSD_WIDTH) ** -0.5),
        "norm_c": 1.0 + nrm(ks[15], (N_ODD, D_MODEL), 0.02),
        "w_in_c": nrm(ks[16], (N_ODD, D_MODEL, ODD_IN), D_MODEL ** -0.5),
        "b_in_c": nrm(ks[17], (N_ODD, ODD_IN), 0.02),
        "sinks_c": nrm(ks[18], (N_ODD, SW_HEADS), 1.0),
        "w_out_c": nrm(ks[19], (N_ODD, SW_WIDTH, D_MODEL), SW_WIDTH ** -0.5),
        "final_norm": 1.0 + nrm(ks[20], (D_MODEL,), 0.02),
    }

def second_block(x, norm_a, w_in_a, conv_w_a, conv_b_a, dt_bias_a, a_log_a, d_skip_a, ssd_norm_a,
              lambda_q1_a, lambda_k1_a, lambda_q2_a, lambda_k2_a, subln_a, w_out_a,
              norm_c, w_in_c, b_in_c, sinks_c, w_out_c, final_norm):
    for i in range(DEPTH_2):
        j = i // 2
        if i % 2 == 0:
            lambda_init = 0.8 - 0.6 * math.exp(-0.3 * i)
            x = x + even_layer(rmsnorm(x, norm_a[j]), w_in_a[j], conv_w_a[j], conv_b_a[j],
                               dt_bias_a[j], a_log_a[j], d_skip_a[j], ssd_norm_a[j],
                               lambda_q1_a[j], lambda_k1_a[j], lambda_q2_a[j], lambda_k2_a[j],
                               subln_a[j], w_out_a[j], lambda_init)
        else:
            x = x + odd_layer(rmsnorm(x, norm_c[j]), w_in_c[j], b_in_c[j], sinks_c[j], w_out_c[j])
    return rmsnorm(x, final_norm)


def setup_inputs(seed=0):
    out = dict(first_inputs(seed))
    for name, value in second_inputs(seed + 1).items():
        if name != "x":
            out[name + "_2"] = value
    return out


def reference(
    x, attn_norm_w, w_in, pool_w, pool_scale, q_norm_w, k_norm_w, cmp_pos, cmp_w1, cmp_b1,
    cmp_w2, w_pool_br, w_attn_br, w_o, ffn_norm_w, w_up, conv_w, conv_b, w_down, norm_a_2,
    w_in_a_2, conv_w_a_2, conv_b_a_2, dt_bias_a_2, a_log_a_2, d_skip_a_2, ssd_norm_a_2,
    lambda_q1_a_2, lambda_k1_a_2, lambda_q2_a_2, lambda_k2_a_2, subln_a_2, w_out_a_2, norm_c_2,
    w_in_c_2, b_in_c_2, sinks_c_2, w_out_c_2, final_norm_2,
):
    x = first_block(
        x, attn_norm_w, w_in, pool_w, pool_scale, q_norm_w, k_norm_w, cmp_pos, cmp_w1, cmp_b1,
        cmp_w2, w_pool_br, w_attn_br, w_o, ffn_norm_w, w_up, conv_w, conv_b, w_down,
    )
    return second_block(
        x, norm_a_2, w_in_a_2, conv_w_a_2, conv_b_a_2, dt_bias_a_2, a_log_a_2, d_skip_a_2,
        ssd_norm_a_2, lambda_q1_a_2, lambda_k1_a_2, lambda_q2_a_2, lambda_k2_a_2, subln_a_2,
        w_out_a_2, norm_c_2, w_in_c_2, b_in_c_2, sinks_c_2, w_out_c_2, final_norm_2,
    )


_drawn_inputs = setup_inputs


def setup_inputs(seed=0):
    import zlib

    import numpy as np

    out = dict(_drawn_inputs(seed))
    spreads = {}
    factors = {'q_norm_w': 8.0,
     'k_norm_w': 8.0,
     'cmp_b1': 8.0,
     'conv_b': 3.392,
     'norm_a_2': 3.36,
     'conv_b_a_2': 4.269,
     'ssd_norm_a_2': 5.769,
     'lambda_q1_a_2': 5.325,
     'lambda_k1_a_2': 8.0,
     'subln_a_2': 8.0,
     'norm_c_2': 8.0,
     'b_in_c_2': 6.68,
     'sinks_c_2': 21.776,
     'final_norm_2': 7.983,
     'd_skip_a_2': 8.0}
    for name, (base, spread) in spreads.items():
        noise = np.random.default_rng([zlib.crc32(name.encode()), seed]).standard_normal(out[name].shape)
        drawn = base * np.exp(spread * noise) if base else spread * noise
        out[name] = __import__('jax').numpy.asarray(drawn.astype(out[name].dtype))
    for name, factor in factors.items():
        out[name] = (out[name] * factor).astype(out[name].dtype)
    return out
```

```python
from contextlib import ExitStack

import numpy as np

import concourse.bass as bass
from concourse import mybir

F32 = mybir.dt.float32
F32R = mybir.dt.float32r
ACT = mybir.ActivationFunctionType
ALU = mybir.AluOpType
AX = mybir.AxisListType.X

P = 128
S = 512
D = 1024
TT = S // P
KT = D // P
IC = 256
NEG = -1e30

POOL_W = 512
POOL_WINDOWS = (2, 4, 8, 16)
HD = 64
NH = 16
OFF_Q = POOL_W
OFF_KV = OFF_Q + NH * HD
OFF_G = OFF_KV + 3 * 2 * 2 * HD
OFF_MG = OFF_G + 3 * NH
DFF = 2752
FT = DFF // P
FREST = DFF - FT * P
CMP_BLOCK, CMP_STRIDE = 32, 16
NCMP = (S - CMP_BLOCK) // CMP_STRIDE + 1
EPS1, EPS2 = 1e-6, 1e-5
SCALE = HD ** -0.5
DA_H = 8
OFF_K2, OFF_V2, OFF_GA, OFF_Z, OFF_XBC, OFF_DT = 1024, 2048, 3072, 4096, 5120, 6656
SSD_H = 16
CH = S // P
LAMBDA_INIT = 0.8 - 0.6 * float(np.exp(-0.3 * 0))
WIN2 = 128
OFF_KV_C, OFF_G_C = 1024, 1280


def slopes(n):
    return [float(np.float32(2.0 ** (-8.0 * (i + 1) / n))) for i in range(n)]


def high_part(v):
    m, e = np.frexp(np.float64(v))
    return float(np.ldexp(np.round(m * 4096) / 4096, e))


PARAMS = [("attn_norm", 8), ("ffn_norm", 8), ("q_norm", 1), ("k_norm", 3), ("pool_scale", 4), ("cmp_b1", 2),
          ("pos", 64), ("convw_g", 66), ("convw_v", 66), ("convb_g", 22), ("convb_v", 22),
          ("norm_a", 8), ("conv_a", 48), ("convb_a", 12), ("dt_bias", 1), ("a_log", 1), ("d_skip", 8),
          ("ssd_norm", 8), ("lam", 4), ("subln", 1), ("norm_c", 8), ("b_q", 8), ("b_k", 1), ("b_g", 8),
          ("sinks", 16), ("final", 8)]
PCOL, _o = {}, 0
for _n, _c in PARAMS:
    PCOL[_n] = _o
    _o += _c
NPAR = _o


def pack_params(a):
    f = np.float32

    def tiles(v, n=None):
        v = np.asarray(v).reshape(-1)
        n = n or -(-v.size // P)
        out = np.zeros(n * P, f)
        out[:v.size] = v
        return out.reshape(n, P).T

    def rows(v):
        out = np.zeros((P, v.shape[1]), f)
        out[:v.shape[0]] = v
        return out

    def twice(v):
        return np.concatenate([v, v], axis=0)

    cw, cb = a["conv_w"][0], a["conv_b"][0]
    b_in = a["b_in_c_2"][0]
    got = {
        "attn_norm": tiles(a["attn_norm_w"]), "ffn_norm": tiles(a["ffn_norm_w"]),
        "q_norm": twice(a["q_norm_w"][0][:, None]),
        "k_norm": twice(a["k_norm_w"][0].T), "pool_scale": tiles(a["pool_scale"]),
        "cmp_b1": a["cmp_b1"][0].T,
        "pos": twice(np.concatenate([a["cmp_pos"][0, 0].T, a["cmp_pos"][0, 1].T], axis=1)),
        "convw_g": np.concatenate([tiles(cw[t, :DFF]) for t in range(3)], axis=1),
        "convw_v": np.concatenate([tiles(cw[t, DFF:]) for t in range(3)], axis=1),
        "convb_g": tiles(cb[:DFF]), "convb_v": tiles(cb[DFF:]),
        "norm_a": tiles(a["norm_a_2"]),
        "conv_a": np.concatenate([tiles(a["conv_w_a_2"][0, t]) for t in range(4)], axis=1),
        "convb_a": tiles(a["conv_b_a_2"]),
        "dt_bias": rows(a["dt_bias_a_2"].T), "a_log": rows(a["a_log_a_2"].T),
        "d_skip": tiles(np.repeat(a["d_skip_a_2"][0], HD)),
        "ssd_norm": tiles(a["ssd_norm_a_2"]),
        "lam": rows(np.stack([a["lambda_q1_a_2"][0], a["lambda_k1_a_2"][0],
                              a["lambda_q2_a_2"][0], a["lambda_k2_a_2"][0]], axis=1)),
        "subln": tiles(a["subln_a_2"]), "norm_c": tiles(a["norm_c_2"]),
        "b_q": tiles(b_in[:1024]), "b_k": tiles(b_in[1024:1152]), "b_g": tiles(b_in[OFF_G_C:]),
        "sinks": np.tile(a["sinks_c_2"][0][None, :], (P, 1)),
        "final": tiles(a["final_norm_2"]),
    }
    return np.ascontiguousarray(np.concatenate([got[n] for n, _ in PARAMS], axis=1), dtype=f)


CONSTS = [("ident", 128), ("ones", 128), ("eps1", 1), ("eps2", 1), ("halves", 2), ("maskc", 4 * NCMP), ("keepc", 4 * NCMP),
          ("cos", 512), ("sin", 512), ("perm", 128), ("blk", 128), ("dup0", 128), ("dup1", 128),
          ("causal", 128), ("rcnt", 4 * 16), ("causal_t", 512), ("sel", SSD_H * 128), ("selp", 8 * 128),
          ("dist", 512), ("dist2", 256)]
CCOL, _o = {}, 0
for _n, _c in CONSTS:
    CCOL[_n] = _o
    _o += _c
NCON = _o


def make_consts():
    f = np.float32
    i = np.arange(P)
    freqs = (f(10000.0) ** (-np.arange(32, dtype=f) / f(32))).astype(f)
    ang = (np.arange(S, dtype=f)[:, None] * freqs[None, :]).astype(f)
    cos = np.cos(ang.astype(np.float64)).T
    sin = np.sin(ang.astype(np.float64)).T
    perm = np.zeros((P, P), f)
    for j in range(P):
        perm[j ^ 32, j] = 1.0
    dup = []
    for g in range(2):
        m = np.zeros((P, P), f)
        for j in range(P):
            m[64 * g + j % 64, j] = 1.0
        dup.append(m)
    t = np.arange(S).reshape(TT, P).T
    end = np.arange(NCMP) * CMP_STRIDE + CMP_BLOCK - 1
    ok = end[None, None, :] <= t[:, :, None]
    rc = np.zeros((P, 4, 16), f)
    for g, w in enumerate(POOL_WINDOWS):
        rc[:, g, :] = 1.0 / np.minimum(np.arange(16) + 1, w)
    sel = np.zeros((P, SSD_H, P), f)
    selp = np.zeros((P, 8, P), f)
    for h in range(SSD_H):
        sel[h, h, :] = 1.0
        selp[h, h // 2, 64 * (h % 2):64 * (h % 2) + 64] = 1.0
    c = np.arange(512)
    rel = (c[None, :] - 384) - i[:, None]
    c2 = np.arange(256)
    rel2 = (c2[None, :] - 128) - i[:, None]
    got = {
        "ident": np.eye(P), "ones": np.ones((P, P)), "eps1": np.full((P, 1), EPS1), "eps2": np.full((P, 1), EPS2),
        "halves": (i[:, None] // 64 == np.arange(2)[None, :]).astype(f),
        "maskc": np.where(ok, 0.0, NEG).reshape(P, -1), "keepc": ok.reshape(P, -1).astype(f),
        "cos": np.concatenate([cos] * 4), "sin": np.concatenate([-sin, sin] * 2),
        "perm": perm, "blk": (i[:, None] // 64 == i[None, :] // 64).astype(f),
        "dup0": dup[0], "dup1": dup[1],
        "causal": np.where(i[None, :] <= i[:, None], 0.0, NEG),
        "rcnt": rc.reshape(P, -1),
        "causal_t": np.tile(np.where(i[None, :] >= i[:, None], 0.0, NEG), (1, 4)),
        "sel": sel.reshape(P, -1), "selp": selp.reshape(P, -1),
        "dist": np.where(rel <= 0, rel, NEG), "dist2": np.where((rel2 <= 0) & (rel2 > -WIN2), rel2, NEG),
    }
    return np.ascontiguousarray(np.concatenate([got[n] for n, _ in CONSTS], axis=1), dtype=f)


WEIGHTS = ["w_in", "pool_w", "cmp_w1", "cmp_w2", "w_pool_br", "w_attn_br", "w_o", "w_up", "w_down",
           "w_in_a_2", "w_out_a_2", "w_in_c_2", "w_out_c_2"]


AHEAD = 2
TOTAL_ITEMS = 112


def two_blocks(nc, x, par, con, bvc, w, out):
    ctx = ExitStack()
    K = 1024
    base = nc.sbuf_base
    base += -base % 64
    room = nc.sbuf_usable_end - base

    def at(name, offset, shape, dt=F32):
        size = 4 * int(np.prod(shape))
        assert offset + size <= room, (name, offset + size, room)
        return nc.alloc_sbuf_tensor_at(name, [P] + list(shape), dt, offset=base + offset)

    def sem(name):
        return ctx.enter_context(nc.semaphore(name))

    W_RAW, W_HI, W_LO, X_AT, H_HI, H_LO, Y, PAR_AT, CON_AT = (0, 16 * K, 32 * K, 48 * K, 64 * K, 80 * K, 96 * K,
                                                            184 * K, 186 * K)
    SC_AT = CON_AT + 1600
    SC_AT += -SC_AT % 64
    wraw = at("wraw", W_RAW, [2, KT, IC])
    whi = at("whi", W_HI, [2, KT, IC], F32R)
    wlo = at("wlo", W_LO, [2, KT, IC], F32R)
    xt = at("xt", X_AT, [KT, S])
    hh = at("hh", H_HI, [KT, S], F32R)
    hl = at("hl", H_LO, [KT, S], F32R)
    parm = at("parm", PAR_AT, [NPAR])
    ident = at("ident", CON_AT, [128])
    ones = at("ones", CON_AT + 512, [128])
    identr = at("identr", CON_AT + 1024, [128], F32R)
    eps = at("eps", CON_AT + 1536, [2])
    halves = at("halves", CON_AT + 1568, [2])

    causf = at("causf", Y + 80 * K, [128])

    def pcol(name, t=0, rows=P, n=1):
        return parm[0:rows, PCOL[name] + t:PCOL[name] + t + n]

    def pcol_at(name, t, rows=P):
        return parm[0:rows, bass.ds(PCOL[name] + t, 1)]

    bank = [ctx.enter_context(nc.psum_tensor(f"bank{i}", [P, S], F32)) for i in range(8)]

    block = ctx.enter_context(nc.Block())

    w_landed = [sem("w_landed0"), sem("w_landed1")]
    w_hi_done = sem("w_hi_done")
    w_lo_done = sem("w_lo_done")
    tiles = sem("tiles")
    drained = sem("drained")
    count = {"item": 0, "tile": 0}

    def new_items(n):
        n0 = count["item"]
        count["item"] += n
        return n0

    def new_tiles(n):
        m0 = count["tile"]
        count["tile"] += n
        return m0

    def load_item(sp, b, i, pairs):
        assert len(pairs) == 2
        if b >= 2:
            sp.wait_ge(w_lo_done, b - 1 + 2 * i)
            sp.sem_inc(w_free, 1)
        for dst, src in pairs:
            sp.dma_start(dst, src).then_inc(w_landed[b % 2], 16)

    def full_item(b, mat, r0, c0):
        v = mat[r0:r0 + D, :].rearrange("(k p) n -> p k n", p=P)
        s = wraw[:, b % 2]
        return [(s[:, 0:4, :], v[:, 0:4, bass.ds(c0, IC)]), (s[:, 4:8, :], v[:, 4:8, bass.ds(c0, IC)])]

    def split_hi(act, b, i=0):
        if isinstance(i, int) and b + 2 * i >= TOTAL_ITEMS:
            return
        p = b % 2
        act.wait_ge(w_landed[p], 32 * (b // 2 + 1) + 32 * i)
        if b >= 2:
            act.wait_ge(tiles, 2 * (b - 1) + 4 * i)
        act.activation(whi[:, p], wraw[:, p], ACT.Copy).then_inc(w_hi_done, 1)

    def split_lo(dve, b, i=0):
        if isinstance(i, int) and b + 2 * i >= TOTAL_ITEMS:
            return
        p = b % 2
        dve.wait_ge(w_hi_done, b + 1 + 2 * i)
        dve.tensor_tensor(wlo[:, p], wraw[:, p], whi[:, p].bitcast(F32), ALU.subtract).then_inc(w_lo_done, 1)

    def item_ready(pe, b, i=0):
        pe.wait_ge(w_lo_done, b + 1 + 2 * i)

    def passes(pe, out, ws, hs, first, last):
        pe.matmul(out, ws[0], hs[0], start=first, stop=False)
        pe.matmul(out, ws[0], hs[1], start=False, stop=False)
        return pe.matmul(out, ws[1], hs[0], start=False, stop=last)

    def tile_of(pe, b, t, out, rhs, kts=KT, k0=0, w0=0, cols=P, c0=None, first=True, last=True, ready=None):
        p = b % 2
        c0 = P * t if c0 is None else c0
        for k in range(kts):
            if ready:
                pe.wait_ge(ready[0], ready[1] + k + 1)
            mm = passes(pe, out, (whi[:, p, w0 + k, c0:c0 + cols], wlo[:, p, w0 + k, c0:c0 + cols]),
                        (rhs[0][:, k0 + k, :], rhs[1][:, k0 + k, :]), first and k == 0, last and k == kts - 1)
        return mm

    def rows_of(pe, b, tt, out, cols, c0=0):
        p = b % 2
        for k in range(KT):
            mm = passes(pe, out, (hh[:, k, P * tt:P * tt + P], hl[:, k, P * tt:P * tt + P]),
                        (whi[:, p, k, c0:c0 + cols], wlo[:, p, k, c0:c0 + cols]), k == 0, k == KT - 1)
        return mm

    class Chain:

        def __init__(self, name):
            self.sem, self.n, self.off = sem(name), 0, 0

        def __call__(self, eng, ins):
            ins.then_inc(self.sem, 1)
            self.n += 1
            eng.wait_ge(self.sem, self.n + self.off)

        def loop(self, i, per, times):
            self.n0, self.off, self.per, self.times = self.n, per * i, per, times

        def done(self):
            assert self.n - self.n0 == self.per, (self.n - self.n0, self.per)
            self.n, self.off = self.n0 + self.per * self.times, 0

    dch = Chain("dve_own")
    ach = Chain("act_own")

    xr = at("xr", Y, [TT, D])
    CON1 = 16 * 6
    CON_K, CON_P = CON1 + 16 * 13, CON1 + 16 * 15
    CON2, CON3, CON4 = CON_P + 16, CON_P + 16 * 4, CON_P + 16 * 7
    w_free = sem("w_free")
    got_x, got_con, con_ready = sem("got_x"), sem("got_con"), sem("con_ready")
    x_turned = sem("x_turned")

    def load_x():
        n0 = 0

        @block.sync
        def _(sp):
            sp.dma_start(parm[:, :], par).then_inc(got_con, 16)
            sp.dma_start(ident[:, :], con[:, CCOL["ident"]:CCOL["ident"] + 128]).then_inc(got_con, 16)
            sp.dma_start(ones[:, :], con[:, CCOL["ones"]:CCOL["ones"] + 128]).then_inc(got_con, 16)
            sp.dma_start(eps[:, :], con[:, CCOL["eps1"]:CCOL["eps1"] + 2]).then_inc(got_con, 16)
            sp.dma_start(halves[:, :], con[:, CCOL["halves"]:CCOL["halves"] + 2]).then_inc(got_con, 16)
            sp.dma_start(causf[:, :], con[:, CCOL["causal"]:CCOL["causal"] + 128]).then_inc(got_con, 16)
            v = x.rearrange("(t p) n -> p t n", p=P)
            for t in range(TT):
                sp.dma_start(xr[:, t, :], v[:, t, :]).then_inc(got_x, 16)

        @block.scalar
        def _(act):
            for early in (g_sig, b_silu):
                act.sem_inc(early, AHEAD)
            split_hi(act, 0)
            split_hi(act, 1)
            act.wait_ge(got_con, CON1)
            act.activation(identr[:, :], ident[:, :], ACT.Copy).then_inc(con_ready, 1)

        @block.tensor
        def _(pe):
            pe.wait_ge(got_con, CON1)
            pe.wait_ge(got_x, 16 * TT)
            pe.wait_ge(con_ready, 1)
            for k in range(KT):
                if k >= 4:
                    pe.wait_ge(drained, k - 3)
                for t in range(TT):
                    mm = pe.transpose(bank[k % 4][:, P * t:P * t + P], xr[:, t, P * k:P * k + P], ident[:, :])
                mm.then_inc(x_turned, 1)

        @block.vector
        def _(dve):
            for early in (g_pool, g_full, g_low, f_act, f_low, e_prod, e_low):
                dve.sem_inc(early, AHEAD)
            for k in range(KT):
                dve.wait_ge(x_turned, k + 1)
                dve.tensor_copy(xt[:, k, :], bank[k % 4][:, :]).then_inc(drained, 1)
            split_lo(dve, 0)
            split_lo(dve, 1)

        return new_tiles(KT)

    sqn = at("sqn", SC_AT, [2, S])
    ssn = at("ssn", SC_AT + 4 * K, [S])
    rtn = at("rtn", SC_AT + 6 * K, [TT])
    rrn = at("rrn", SC_AT + 6 * K + 64, [TT])
    hfn = at("hfn", SC_AT + 7 * K, [2, S])
    n_sq, n_add, n_sum, n_root, n_rec = sem("n_sq"), sem("n_add"), sem("n_sum"), sem("n_root"), sem("n_rec")
    n_spread, n_full, n_high, n_low = sem("n_spread"), sem("n_full"), sem("n_high"), sem("n_low")
    norms = [0]

    def norm(m0, weight, eps_col):
        c = norms[0]
        norms[0] += 1

        def norm_low(dve, c, k):
            dve.wait_ge(n_high, KT * c + k + 1)
            dve.tensor_tensor(hl[:, k, :], hfn[:, k % 2, :], hh[:, k, :].bitcast(F32),
                              ALU.subtract).then_inc(n_low, 1)

        @block.scalar
        def _(act):
            for k in range(KT):
                act.wait_ge(drained, m0 + k + 1)
                if k >= 2 or c:
                    act.wait_ge(n_add, KT * c + k - 1)
                act.activation(sqn[:, k % 2, :], xt[:, k, :], ACT.Square).then_inc(n_sq, 1)
            act.wait_ge(n_sum, c + 1)
            act.activation(rtn[:, :], bank[4][:, 0:TT], ACT.Sqrt, bias=eps[:, eps_col:eps_col + 1],
                           scale=1.0 / D).then_inc(n_root, 1)
            for k in range(KT):
                act.wait_ge(n_full, KT * c + k + 1)
                act.activation(hh[:, k, :], hfn[:, k % 2, :], ACT.Copy).then_inc(n_high, 1)

        @block.vector
        def _(dve):
            dve.wait_ge(n_sq, KT * c + 1)
            if c:
                dve.wait_ge(n_sum, c)
            dve.tensor_copy(ssn[:, :], sqn[:, 0, :]).then_inc(n_add, 1)
            for k in range(1, KT):
                dve.wait_ge(n_sq, KT * c + k + 1)
                dve.wait_ge(n_add, KT * c + k)
                dve.tensor_tensor(ssn[:, :], ssn[:, :], sqn[:, k % 2, :], ALU.add).then_inc(n_add, 1)
            dve.wait_ge(n_root, c + 1)
            dve.reciprocal(rrn[:, :], rtn[:, :]).then_inc(n_rec, 1)
            dve.wait_ge(n_spread, c + 1)
            for k in range(KT):
                if k >= 2:
                    dve.wait_ge(n_low, KT * c + k - 1)
                dve.scalar_tensor_tensor(out=hfn[:, k % 2, :], in0=xt[:, k, :], scalar=pcol(weight, k),
                                         in1=bank[5][:, :], op0=ALU.mult, op1=ALU.mult).then_inc(n_full, 1)
                if k >= 1:
                    norm_low(dve, c, k - 1)
            norm_low(dve, c, KT - 1)

        @block.tensor
        def _(pe):
            pe.wait_ge(n_add, KT * c + KT)
            pe.wait_ge(drained, m0 + KT)
            for t in range(TT):
                mm = pe.matmul(bank[4][:, t:t + 1], ssn[:, P * t:P * t + P], ones[:, 0:1], start=True, stop=True)
            mm.then_inc(n_sum, 1)
            pe.wait_ge(n_rec, c + 1)
            spread(pe, bank[5], lambda t: rrn[:, t:t + 1].to_broadcast([P, P])).then_inc(n_spread, 1)
            pe.wait_ge(n_low, KT * c + KT)

    def spread(pe, out, col):
        for t in range(TT):
            mm = pe.matmul(out[:, P * t:P * t + P], col(t), ident[:, :], start=True, stop=True)
        return mm

    H = (hh, hl)

    cosr = at("cosr", Y + 66 * K, [S])
    sinr = at("sinr", Y + 68 * K, [S])
    perm = at("perm", Y + 70 * K, [128])
    dup = at("dup", Y + 71 * K, [2, 128])
    kr = at("kr", Y + 72 * K, [3, S])
    vcz = at("vcz", Y + 78 * K, [S])
    qt = at("qt", Y + 32 * K, [KT, S])
    kdh = at("kdh", Y + 48 * K, [2, 2, S], F32R)
    kdl = at("kdl", Y + 16 * K, [2, 2, S], F32R)
    qs = at("qs", Y + 24 * K, [2, 2, S], F32R)
    vp = at("vp", Y + 56 * K, [TT, 2, 320])
    pt = at("pt", Y + 66 * K, [2, TT, S])
    gt = at("gt", Y + 82 * K, [TT, 3 * NH])
    kc = at("kc", Y + 83 * K, [2, NCMP])
    mc = at("mc", Y + 83 * K + 256, [TT, NCMP])
    keep = at("keep", Y + 83 * K + 768, [TT, NCMP])
    SM = Y + 84 * K + 512
    rtq = at("rtq", SM, [TT, 22])
    rq = at("rq", SM + 352, [TT, 22])
    cmx = at("cmx", SM + 704, [TT, NH])
    csm = at("csm", SM + 960, [TT, NH])
    crs = at("crs", SM + 1216, [TT, NH])
    nm = at("nm", SM + 1472, [2, TT])
    sm = at("sm", SM + 1504, [2, TT])
    rs = at("rs", SM + 1536, [2, TT])
    gel = at("gel", SM + 1600, [2, 2, NCMP])
    w2d = at("w2d", SM + 2112, [128])
    w2v = at("w2v", SM + 2624, [64])
    caus = at("caus", SM + 2880, [128], F32R)
    w1 = at("w1", Y, [2, 32, 128])
    hs = at("hs", Y + 66 * K, [2 * P])
    oh = at("oh", Y + 32 * K, [KT, S], F32R)
    ol = at("ol", Y, [KT, S], F32R)
    kw = at("kw", SC_AT, [2, S])
    sq = at("sq", SC_AT + 4 * K, [2, S])
    ta = at("ta", SC_AT + 8 * K, [S])
    tb = at("tb", SC_AT + 10 * K, [S])
    rwide = at("rwide", SC_AT, [2, TT, P])
    f_wide = sem("f_wide")
    win = at("win", SC_AT + 4 * K, [2, 32, 2 * NCMP])
    sc = at("sc", SC_AT + 8 * K, [TT, NH, 32])
    pct = at("pct", SC_AT, [4, S])
    pr = at("pr", SC_AT + 8 * K, [2, 1280])
    vc = at("vc", SC_AT + 18 * K, [2, 2, 128])
    r_z, r_mm, r_done = sem("r_z"), sem("r_mm"), sem("r_done")

    def rope_in(act, r, src, weight):
        n, p = r
        if not (isinstance(n, int) and n < 2):
            act.wait_ge(r_done, n - 1)
        act.activation(kw[:, p, :], src, ACT.Copy, scale=weight)
        act.activation(sq[:, p, :], src, ACT.Square).then_inc(r_z, 1)

    def rope_mm(pe, r):
        n, p = r
        pe.wait_ge(r_z, n + 1)
        if not (isinstance(n, int) and n < 2):
            pe.wait_ge(r_done, n - 1)
        for t in range(TT):
            out = bank[6][:, 44 * t + 2 * n:44 * t + 2 * n + 2] if isinstance(n, int) else \
                bank[6][:, bass.ds(44 * t + 2 * n, 2)]
            pe.matmul(out, sq[:, p, P * t:P * t + P], halves[:, :], start=True, stop=True)
        pe.matmul(bank[4 + p][:, :], perm[:, :], kw[:, p, :], start=True, stop=True).then_inc(r_mm, 1)

    def rope_out(dve, r, dst):
        n, p = r
        dve.wait_ge(r_mm, n + 1)
        if not (isinstance(n, int) and n < 1):
            dve.wait_ge(r_done, n)
        dve.tensor_tensor(ta[:, :], kw[:, p, :], cosr[:, :], ALU.mult)
        dch(dve, dve.tensor_tensor(tb[:, :], bank[4 + p][:, :], sinr[:, :], ALU.mult))
        dve.tensor_tensor(dst, ta[:, :], tb[:, :], ALU.add).then_inc(r_done, 1)

    vcz_ready, gates_ready = sem("vcz_ready"), sem("gates_ready")
    pads_ready = sem("pads_ready")

    def block1_kv():
        n0, m0 = new_items(4), new_tiles(7)
        w_in = w["w_in"]
        v = w_in.rearrange("(k p) n -> p k n", p=P)

        @block.sync
        def _(sp):
            load_item(sp, n0, 0, full_item(n0, w_in, 0, OFF_KV))
            for b, (c0, c1) in ((n0 + 1, (256, 512)), (n0 + 2, (384, 640))):
                s = wraw[:, b % 2]
                load_item(sp, b, 0, [(s[:, :, 0:P], v[:, :, OFF_KV + c0:OFF_KV + c0 + P]),
                                     (s[:, :, P:IC], v[:, :, OFF_KV + c1:OFF_KV + c1 + P])])
            b = n0 + 3
            s = wraw[:, b % 2]
            g = 3 * NH
            load_item(sp, b, 0, [(s[:, 0:4, 0:g], v[:, 0:4, OFF_G:OFF_G + g]),
                                 (s[:, 4:8, 0:g], v[:, 4:8, OFF_G:OFF_G + g])])
            sp.wait_ge(x_turned, KT)
            for dst, name in ((cosr, "cos"), (sinr, "sin"), (perm, "perm")):
                n = dst.shape[1]
                sp.dma_start(dst[:, :], con[:, CCOL[name]:CCOL[name] + n]).then_inc(got_con, 16)
            sp.dma_start(dup[:, :, :], con[:, CCOL["dup0"]:CCOL["dup0"] + 256].rearrange(
                "p (g n) -> p g n", g=2)).then_inc(got_con, 16)
            for dst, name in ((mc, "maskc"), (keep, "keepc")):
                sp.dma_start(dst[:, :, :], con[:, CCOL[name]:CCOL[name] + TT * NCMP].rearrange(
                    "p (t n) -> p t n", t=TT)).then_inc(got_con, 16)
            w1v = w["cmp_w1"].rearrange("a (l d) h -> d a l h", d=HD)
            for half in range(2):
                for a in range(2):
                    sp.dma_start(w1[HD * half:HD * half + HD, a], w1v[:, a]).then_inc(got_con, 16)
                sp.dma_start(w2d[:, HD * half:HD * half + HD], w["cmp_w2"][0]).then_inc(got_con, 16)
            sp.dma_start(w2v[:, :], w["cmp_w2"][1]).then_inc(got_con, 16)

        @block.gpsimd
        def _(pool):
            pool.wait_ge(x_turned, KT)
            pool.memset(vp[:, :, :, :], 0.0).then_inc(pads_ready, 1)

        @block.tensor
        def _(pe):
            item_ready(pe, n0)
            tile_of(pe, n0, 0, bank[0][:, :], H).then_inc(tiles, 1)
            tile_of(pe, n0, 1, bank[1][:, :], H).then_inc(tiles, 1)
            item_ready(pe, n0 + 1)
            tile_of(pe, n0 + 1, 0, bank[2][:, :], H).then_inc(tiles, 1)
            pe.wait_ge(got_con, CON_K)
            rope_mm(pe, (0, 0))
            tile_of(pe, n0 + 1, 1, bank[3][:, :], H).then_inc(tiles, 1)
            rope_mm(pe, (1, 1))
            item_ready(pe, n0 + 2)
            for half in range(2):
                pe.wait_ge(drained, m0 + 1 + half)
                for j in range(2):
                    mm = rows_of(pe, n0 + 2, 2 * half + j, bank[half][:, IC * j:IC * j + IC], IC)
                mm.then_inc(tiles, 1)
            rope_mm(pe, (2, 0))
            item_ready(pe, n0 + 3)
            g = 3 * NH
            pe.wait_ge(drained, m0 + 3)
            for half in range(2):
                for j in range(2):
                    tt = 2 * half + j
                    mm = rows_of(pe, n0 + 3, tt, bank[2][:, g * tt:g * tt + g], g)
                mm.then_inc(tiles, 1)

        @block.scalar
        def _(act):
            act.wait_ge(tiles, 2 * n0 + 1)
            rope_in(act, (0, 0), bank[0][:, :], pcol("k_norm", 0))
            act.wait_ge(tiles, 2 * n0 + 2)
            act.wait_ge(x_turned, KT)
            act.activation(vcz[:, :], bank[1][:, :], ACT.Copy).then_inc(vcz_ready, 1)
            split_hi(act, n0 + 2)
            act.wait_ge(tiles, 2 * n0 + 3)
            rope_in(act, (1, 1), bank[2][:, :], pcol("k_norm", 1))
            act.wait_ge(tiles, 2 * n0 + 4)
            rope_in(act, (2, 0), bank[3][:, :], pcol("k_norm", 2))
            split_hi(act, n0 + 3)
            split_hi(act, n0 + 4)
            act.wait_ge(tiles, 2 * n0 + 8)
            act.activation(gt[:, :, :], bank[2][:, 0:TT * 3 * NH].rearrange("p (t g) -> p t g", t=TT),
                           ACT.Sigmoid).then_inc(gates_ready, 1)
            split_hi(act, n0 + 5)

        @block.vector
        def _(dve):
            dve.wait_ge(r_z, 1)
            dve.sem_inc(drained, 1)
            dve.wait_ge(vcz_ready, 1)
            dve.sem_inc(drained, 1)
            split_lo(dve, n0 + 2)
            dve.wait_ge(got_con, 16 * 13)
            rope_out(dve, (0, 0), kr[:, 0, :])
            dve.wait_ge(r_z, 2)
            dve.sem_inc(drained, 1)
            rope_out(dve, (1, 1), kr[:, 1, :])
            dve.wait_ge(r_z, 3)
            dve.sem_inc(drained, 1)
            split_lo(dve, n0 + 3)
            dve.wait_ge(pads_ready, 1)
            for half in range(2):
                dve.wait_ge(tiles, 2 * n0 + 5 + half)
                for j in range(2):
                    tt = 2 * half + j
                    src = bank[half][:, IC * j:IC * j + IC].rearrange("p (b g d) -> p b g d", b=2, g=2)
                    dst = vp[:, tt, :, HD:HD + 256].rearrange("p b (g e) -> p b g e", g=2)[:, :, :, 0:HD]
                    ins = dve.tensor_copy(dst, src)
                ins.then_inc(drained, 1)
            split_lo(dve, n0 + 4)
            rope_out(dve, (2, 0), kr[:, 2, :])
            dve.wait_ge(gates_ready, 1)
            dve.sem_inc(drained, 1)
            split_lo(dve, n0 + 5)

    def block1_q():
        n0, m0, r0 = new_items(4), new_tiles(8), 3

        @block.sync
        def _(sp):
            with sp.Fori(0, 2) as i:
                for j in range(2):
                    load_item(sp, n0 + j, i, full_item(n0 + j, w["w_in"], 0, OFF_Q + IC * j + 2 * IC * i))

        @block.tensor
        def _(pe):
            pe.wait_ge(drained, m0)
            with pe.Fori(0, 2) as i:
                for t in range(4):
                    if t % 2 == 0:
                        item_ready(pe, n0 + t // 2, i)
                    pe.wait_ge(drained, m0 - 4 + t + 1 + 4 * i)
                    tile_of(pe, n0 + t // 2, t % 2, bank[t][:, :], H).then_inc(tiles, 1)
                    if t:
                        rope_mm(pe, (r0 + t - 1 + 4 * i, (r0 + t - 1) % 2))
                rope_mm(pe, (r0 + 3 + 4 * i, (r0 + 3) % 2))

        @block.scalar
        def _(act):
            with act.Fori(0, 2) as i:
                for t in range(4):
                    act.wait_ge(tiles, 2 * n0 + t + 1 + 4 * i)
                    rope_in(act, (r0 + t + 4 * i, (r0 + t) % 2), bank[t][:, :], pcol("q_norm"))
                    if t % 2:
                        split_hi(act, n0 + 2 + t // 2, i)

        @block.vector
        def _(dve):
            with dve.Fori(0, 2) as i:
                dch.loop(i, 4, 2)
                for t in range(4):
                    dve.wait_ge(r_z, r0 + t + 1 + 4 * i)
                    dve.sem_inc(drained, 1)
                    if t % 2:
                        split_lo(dve, n0 + 2 + t // 2, i)
                    rope_out(dve, (r0 + t + 4 * i, (r0 + t) % 2), flat(qt[:, bass.ds(4 * i + t, 1), :]))
            dch.done()
        return m0 + 8

    def flat(ap):
        return ap.rearrange("p a n -> p (a n)")

    f_root, f_rec, f_spread, f_used, kd_mm, kd_done = (sem("f_root"), sem("f_rec"), sem("f_spread"), sem("f_used"),
                                                       sem("kd_mm"), sem("kd_done"))
    c_win, c_mm1, c_gelu, c_mm2, c_out = sem("c_win"), sem("c_mm1"), sem("c_gelu"), sem("c_mm2"), sem("c_out")
    kd_low, q_hi, q_lo = sem("kd_low"), sem("q_hi"), sem("q_lo")
    c_pad, c_s, c_sub, c_exp, c_p, c_t, c_done = (sem("c_pad"), sem("c_s"), sem("c_sub"), sem("c_exp"), sem("c_p"),
                                                  sem("c_t"), sem("c_done"))

    def block1_finish_qk(m1):

        @block.scalar
        def _(act):
            act.wait_ge(r_mm, 11)
            act.activation(rtq[:, :, :], bank[6][:, 0:44 * TT].rearrange("p (t g) -> p t g", t=TT)[:, :, 0:22],
                           ACT.Sqrt, bias=eps[:, 0:1], scale=1.0 / HD).then_inc(f_root, 1)
            act.wait_ge(f_rec, 1)
            act.wait_ge(r_done, 11)
            for n in range(11):
                if n >= 2:
                    act.wait_ge(f_spread, n - 1)
                act.activation(rwide[:, n % 2, :, :].rearrange("p t (h d) -> p t h d", h=2),
                               rq[:, :, 2 * n:2 * n + 2].unsqueeze(3).to_broadcast([P, TT, 2, HD]),
                               ACT.Copy).then_inc(f_wide, 1)
            act.activation(caus[:, :], causf[:, :], ACT.Copy).then_inc(kd_done, 1)
            act.wait_ge(c_mm1, 2)
            act.activation(hs[0:2 * NCMP, :], bank[0][0:2 * NCMP, 0:2 * P], ACT.Copy).then_inc(c_gelu, 1)
            act.wait_ge(c_mm1, 3)
            for a in range(2):
                ins = act.activation(gel[:, a, :, :], bank[1][:, 64 * a:64 * a + 2 * NCMP].rearrange(
                    "p (g n) -> p g n", g=2), ACT.Gelu_apprx_tanh, bias=pcol("cmp_b1", a))
            ins.then_inc(c_gelu, 1)
            for b in range(2):
                for g in range(2):
                    n = 2 * b + g
                    act.wait_ge(kd_mm, n + 1)
                    act.activation(kdh[:, b, g, :], bank[4 + n][:, :], ACT.Copy).then_inc(kd_done, 1)

        @block.vector
        def _(dve):
            dve.wait_ge(f_root, 1)
            dve.reciprocal(rq[:, :, :], rtq[:, :, :]).then_inc(f_rec, 1)
            for n in range(11):
                dve.wait_ge(f_spread, n + 1)
                dst = kr[:, n, :] if n < 3 else qt[:, n - 3, :]
                dve.scalar_tensor_tensor(out=dst, in0=dst, scalar=1.0 if n < 3 else SCALE, in1=bank[4 + n % 2][:, :],
                                         op0=ALU.mult, op1=ALU.mult).then_inc(f_used, 1)
            dve.wait_ge(f_used, 11)
            dve.wait_ge(vcz_ready, 1)
            for a, src in ((0, kr[:, 0, :]), (1, vcz[:, :])):
                v = src.rearrange("p (m b) -> p b m", b=CMP_STRIDE)
                for half in range(2):
                    for g in range(2):
                        rows = slice(HD * g, HD * g + HD)
                        pos = parm[rows, PCOL["pos"] + 32 * a + 16 * half:PCOL["pos"] + 32 * a + 16 * half + 16]
                        dve.tensor_tensor(win[rows, a, 16 * half:16 * half + 16, NCMP * g:NCMP * g + NCMP],
                                          v[rows, :, half:half + NCMP],
                                          pos.unsqueeze(2).to_broadcast([HD, 16, NCMP]), ALU.add).then_inc(c_win, 1)
            for n in range(4):
                dve.wait_ge(kd_done, n + 2)
                dve.tensor_tensor(kdl[:, n // 2, n % 2, :], bank[4 + n][:, :], kdh[:, n // 2, n % 2, :].bitcast(F32),
                                  ALU.subtract).then_inc(kd_low, 1)
            dve.wait_ge(c_mm2, 1)
            dve.wait_ge(c_pad, 3)
            dve.tensor_copy(kc[:, :, :], bank[2][:, 0:2 * NCMP].rearrange("p (g n) -> p g n", g=2))
            for g in range(2):
                for hq in range(4):
                    ins = dve.tensor_copy(vc[32 * hq:32 * hq + NCMP, g, hq // 2, HD * (hq % 2):HD * (hq % 2) + HD],
                                          bank[3][0:NCMP, HD * g:HD * g + HD])
            dch(dve, ins)
            dve.sem_inc(c_out, 1)
            for b in range(4):
                i2, e = b // 2, b % 2
                view = sc[:, 2 * i2:2 * i2 + 2, e::2, 0:NCMP]
                src = bank[b][:, :].rearrange("p (i h n) -> p i h n", i=2, h=8)[:, :, :, 0:NCMP]
                dve.wait_ge(c_s, b + 1)
                for ii in range(2):
                    i = 2 * i2 + ii
                    v1 = sc[:, i, e::2, 0:NCMP]
                    dve.tensor_tensor(v1, src[:, ii], mc[:, i:i + 1, :].to_broadcast([P, 8, NCMP]), ALU.add) \
                        .then_inc(c_sub, 1)
            dve.wait_ge(c_sub, 8)
            dch(dve, dve.tensor_reduce(cmx[:, :, :], sc[:, :, :, 0:NCMP], AX, ALU.max))
            for i in range(TT):
                dve.tensor_tensor(sc[:, i, :, 0:NCMP], sc[:, i, :, 0:NCMP],
                                  cmx[:, i, :].unsqueeze(2).to_broadcast([P, NH, NCMP]), ALU.subtract) \
                    .then_inc(c_sub, 1)
            dve.wait_ge(c_exp, TT)
            dch(dve, dve.tensor_reduce(csm[:, :, :], sc[:, :, :, 0:NCMP], AX, ALU.add))
            dch(dve, dve.reciprocal(crs[:, :, :], csm[:, :, :]))
            dch(dve, dve.tensor_tensor(crs[:, :, :], crs[:, :, :],
                                       gt[:, :, :].rearrange("p t (h b) -> p t h b", b=3)[:, :, :, 0], ALU.mult))
            for i in range(TT):
                v1 = sc[:, i, :, 0:NCMP]
                dch(dve, dve.tensor_tensor(v1, v1, crs[:, i, :].unsqueeze(2).to_broadcast([P, NH, NCMP]), ALU.mult))
                dve.tensor_tensor(v1, v1, keep[:, i:i + 1, :].to_broadcast([P, NH, NCMP]), ALU.mult) \
                    .then_inc(c_p, 1)
            for q4 in range(4):
                dve.wait_ge(c_t, q4 + 1)
                dve.tensor_copy(pct[:, q4, :], bank[4 + q4 % 2][:, :]).then_inc(c_done, 1)

        @block.gpsimd
        def _(pool):
            pool.wait_ge(r_done, 11)
            pool.wait_ge(r_mm, 11)
            for g in range(2):
                ins = pool.memset(win[HD * g:HD * g + HD, :, :, NCMP * (1 - g):NCMP * (2 - g)], 0.0)
            ins.then_inc(c_pad, 1)
            pool.wait_ge(c_mm1, 2)
            pool.memset(vc[:, :, :, :], 0.0).then_inc(c_pad, 1)
            pool.memset(sc[:, :, :, :], 0.0).then_inc(c_pad, 1)

        @block.scalar
        def _(act):
            for i in range(TT):
                act.wait_ge(c_sub, 8 + i + 1)
                act.activation(sc[:, i, :, 0:NCMP], sc[:, i, :, 0:NCMP], ACT.Exp).then_inc(c_exp, 1)

        @block.tensor
        def _(pe):
            pe.wait_ge(f_rec, 1)
            pe.wait_ge(r_done, 11)
            for n in range(11):
                if n >= 2:
                    pe.wait_ge(f_used, n - 1)
                pe.wait_ge(f_wide, n + 1)
                spread(pe, bank[4 + n % 2], lambda t: rwide[:, n % 2, t, :]).then_inc(f_spread, 1)
            pe.wait_ge(drained, m1)
            pe.wait_ge(c_pad, 1)
            for a in range(2):
                pe.wait_ge(c_win, 4 * a + 4)
                for pos in range(CMP_BLOCK):
                    mm = pe.matmul(bank[0][0:2 * NCMP, P * a:P * a + P], win[:, a, pos, :], w1[:, a, pos, :],
                                   start=(pos == 0), stop=(pos == CMP_BLOCK - 1))
                mm.then_inc(c_mm1, 1)
            pe.wait_ge(f_used, 11)
            for b in range(2):
                for g in range(2):
                    pe.matmul(bank[4 + 2 * b + g][:, :], dup[:, g, :], kr[:, 1 + b, :], start=True, stop=True) \
                        .then_inc(kd_mm, 1)
            pe.wait_ge(c_gelu, 1)
            for a in range(2):
                mm = pe.transpose(bank[1][:, 64 * a:64 * a + 2 * NCMP], hs[0:2 * NCMP, P * a:P * a + P],
                                  ident[0:2 * NCMP, 0:2 * NCMP])
            mm.then_inc(c_mm1, 1)
            pe.wait_ge(c_gelu, 2)
            pe.matmul(bank[2][:, 0:2 * NCMP], w2d[:, :], gel[:, 0, :, :].rearrange("p g n -> p (g n)"),
                      start=True, stop=True)
            for g in range(2):
                mm = pe.matmul(bank[3][0:NCMP, HD * g:HD * g + HD], gel[:, 1, g, :], w2v[:, :], start=True, stop=True)
            mm.then_inc(c_mm2, 1)
            pe.wait_ge(c_out, 1)
            for b in range(4):
                i2, e = b // 2, b % 2
                for ii in range(2):
                    i = 2 * i2 + ii
                    for hp in range(8):
                        mm = pe.matmul(bank[b][:, 256 * ii + 32 * hp:256 * ii + 32 * hp + NCMP],
                                       qt[HD * e:HD * e + HD, hp, P * i:P * i + P],
                                       kc[HD * e:HD * e + HD, hp // 4, :], start=True, stop=True)
                mm.then_inc(c_s, 1)
            pe.wait_ge(c_p, TT)
            pe.wait_ge(kd_low, 4)
            for q4 in range(4):
                if q4 >= 2:
                    pe.wait_ge(c_done, q4 - 1)
                for i in range(TT):
                    mm = pe.transpose(bank[4 + q4 % 2][:, P * i:P * i + P],
                                      sc[:, i, 4 * q4:4 * q4 + 4, :].rearrange("p h n -> p (h n)"), ident[:, :])
                mm.then_inc(c_t, 1)

    s_done, s_max, p_exp, p_scaled = sem("s_done"), sem("s_max"), sem("p_exp"), sem("p_scaled")
    t_done, t_act, t_dve, pv_done = sem("t_done"), sem("t_act"), sem("t_dve"), sem("pv_done")
    o_high, o_out = sem("o_high"), sem("o_out")
    UNITS = 4 * (NH // 2)
    POFF = [0, 128, 384, 768]

    def block1_attention():

        def scores(pe, u):
            p, e, b = u // 4, u // 2 % 2, u % 2
            if u % 4 == 0:
                pe.wait_ge(q_lo, p + 1)
            for i in range(TT):
                wd = P * (i + 1)
                if u:
                    pe.wait_ge(p_exp, 4 * (u - 1) + i + 1)
                for part in (kdh, kdl):
                    pe.matmul(bank[i][:, 0:wd], qs[:, p % 2, e, P * i:P * i + P], part[:, b, p // 4, 0:wd],
                              start=(part is kdh), stop=False)
                pe.matmul(bank[i][:, P * i:wd], identr[:, :], caus[:, :], start=False, stop=True).then_inc(s_done, 1)

        def turn(pe, u):
            for i in range(TT):
                pe.wait_ge(p_scaled, 4 * u + i + 1)
                k = 2 * u + i // 2
                if k:
                    pe.wait_ge(t_dve if i % 2 else t_act, k)
                for j in range(i + 1):
                    mm = pe.transpose(bank[4 + i % 2][:, P * j:P * j + P],
                                      pr[:, u % 2, POFF[i] + P * j:POFF[i] + P * j + P], ident[:, :])
                mm.then_inc(t_done, 1)

        def values(pe, u):
            p, e, b = u // 4, u // 2 % 2, u % 2
            out = bank[6 + p % 2]
            if u % 4 == 0:
                if p >= 2:
                    pe.wait_ge(o_out, p - 1)
                pe.matmul(out[:, :], vc[:, p // 4, p % 2, :], pct[:, p // 2, :], start=True, stop=False)
            pe.wait_ge(t_act, 2 * u + 2)
            pe.wait_ge(t_dve, 2 * u + 2)
            g = p // 4
            c0 = HD + P * g if e == 0 else P * g
            for j in range(TT):
                mm = pe.matmul(out[:, P * j:S], vp[:, j, b, c0:c0 + P], pt[:, u % 2, j, P * j:S],
                               start=False, stop=(u % 4 == 3 and j == TT - 1))
            mm.then_inc(pv_done, 1)

        @block.tensor
        def _(pe):
            pe.wait_ge(c_done, 4)
            pe.wait_ge(kd_done, 5)
            scores(pe, 0)
            for u in range(UNITS + 1):
                if u:
                    turn(pe, u - 1)
                if u + 1 < UNITS:
                    scores(pe, u + 1)
                if u:
                    values(pe, u - 1)

        def turned(eng, u, i, signal, copy):
            eng.wait_ge(t_done, 4 * u + i + 1)
            if u >= 2:
                eng.wait_ge(pv_done, u - 1)
            copy(pt[:, u % 2, 0:i + 1, P * i:P * i + P],
                 bank[4 + i % 2][:, 0:P * (i + 1)].rearrange("p (j q) -> p j q", j=i + 1)).then_inc(signal, 1)

        @block.scalar
        def _(act):
            def expo(u, i):
                wd = P * (i + 1)
                act.wait_ge(s_max, 4 * u + i + 1)
                if u >= 2 and i == 0:
                    act.wait_ge(t_done, 4 * (u - 1))
                act.activation(pr[:, u % 2, POFF[i]:POFF[i] + wd], bank[i][:, 0:wd], ACT.Exp,
                               bias=nm[:, u % 2, i:i + 1], accum_out=sm[:, u % 2, i:i + 1]).then_inc(p_exp, 1)

            def queries_high(p):
                if p >= 2:
                    act.wait_ge(s_done, 16 * (p - 1))
                for e in range(2):
                    rows = slice(HD * e, HD * e + HD)
                    ins = act.activation(qs[rows, p % 2, e, :], qt[rows, p, :], ACT.Copy)
                ins.then_inc(q_hi, 1)

            queries_high(0)
            act.wait_ge(c_t, 4)
            for u in range(UNITS + 2):
                if u % 4 == 1 and u // 4 + 1 < NH // 2:
                    queries_high(u // 4 + 1)
                if u >= 2 and u % 4 == 1:
                    p = u // 4 - 1
                    act.wait_ge(pv_done, u - 1)
                    act.activation(oh[:, p, :], bank[6 + p % 2][:, :], ACT.Copy).then_inc(o_high, 1)
                if u < UNITS:
                    for i in range(TT):
                        expo(u, i)
                if 1 <= u <= UNITS:
                    for i in (0, 2):
                        turned(act, u - 1, i, t_act, lambda o, s: act.activation(o, s, ACT.Copy))

        @block.vector
        def _(dve):
            def queries_low(p):
                dve.wait_ge(q_hi, p + 1)
                for e in range(2):
                    rows, other = slice(HD * e, HD * e + HD), slice(HD - HD * e, P - HD * e)
                    ins = dve.tensor_tensor(qs[other, p % 2, e, :], qt[rows, p, :],
                                            qs[rows, p % 2, e, :].bitcast(F32), ALU.subtract)
                ins.then_inc(q_lo, 1)

            queries_low(0)
            for u in range(UNITS + 2):
                if u % 4 == 2 and u // 4 + 1 < NH // 2:
                    queries_low(u // 4 + 1)
                if u < UNITS:
                    for i in range(TT):
                        dve.wait_ge(s_done, 4 * u + i + 1)
                        if u >= 2:
                            dve.wait_ge(p_exp, 4 * (u - 1) - 3 + i)
                        dve.tensor_reduce(nm[:, u % 2, i:i + 1], bank[i][:, 0:P * (i + 1)], AX, ALU.max,
                                          negate=True).then_inc(s_max, 1)
                if 1 <= u <= UNITS:
                    v = u - 1
                    h, b = v // 2, v % 2
                    dve.wait_ge(p_exp, 4 * v + 4)
                    if v >= 2:
                        dve.wait_ge(p_scaled, 4 * (v - 1))
                    dch(dve, dve.reciprocal(rs[:, v % 2, :], sm[:, v % 2, :]))
                    dch(dve, dve.tensor_tensor(rs[:, v % 2, :], rs[:, v % 2, :], gt[:, :, 3 * h + 1 + b], ALU.mult))
                    for i in range(TT):
                        part = pr[:, v % 2, POFF[i]:POFF[i] + P * (i + 1)]
                        dve.tensor_scalar(part, part, rs[:, v % 2, i:i + 1], None, ALU.mult).then_inc(p_scaled, 1)
                if 1 <= u <= UNITS:
                    for i in (1, 3):
                        turned(dve, u - 1, i, t_dve, dve.tensor_copy)
                if u >= 2 and u % 4 == 1:
                    p = u // 4 - 1
                    dve.wait_ge(o_high, p + 1)
                    dve.tensor_tensor(ol[:, p, :], bank[6 + p % 2][:, :], oh[:, p, :].bitcast(F32),
                                      ALU.subtract).then_inc(o_out, 1)

    pu = at("pu", Y + 16 * K, [4, 16 + S])
    pa = at("pa", Y + 25 * K, [2, 16 + S])
    pm = at("pm", Y + 48 * K, [4, S])
    pmh = at("pmh", Y + 64 * K, [4, S], F32R)
    pml = at("pml", Y + 72 * K, [4, S], F32R)
    pw = at("pw", Y + 80 * K, [4, P])
    rc = at("rc", Y + 82 * K, [4, 16])
    p_pad, p_mean, p_mm, p_high, p_out = (sem("p_pad"), sem("p_mean"), sem("p_mm"),
                                                  sem("p_high"), sem("p_out"))

    def block1_pool():
        n0, m0 = new_items(2), new_tiles(4)

        @block.sync
        def _(sp):
            for j in range(2):
                load_item(sp, n0 + j, 0, full_item(n0 + j, w["w_in"], 0, IC * j))
            sp.wait_ge(pv_done, UNITS)
            sp.dma_start(pw[:, :, :], w["pool_w"].rearrange("g c d -> c g d")).then_inc(got_con, 16)
            sp.dma_start(rc[:, :, :], con[:, CCOL["rcnt"]:CCOL["rcnt"] + 64].rearrange(
                "p (g n) -> p g n", g=4)).then_inc(got_con, 16)

        @block.gpsimd
        def _(pool):
            pool.wait_ge(pv_done, UNITS)
            pool.memset(pu[:, :, 0:16], 0.0)
            pool.memset(pa[:, :, 0:16], 0.0).then_inc(p_pad, 1)

        @block.tensor
        def _(pe):
            for t in range(4):
                if t % 2 == 0:
                    item_ready(pe, n0 + t // 2)
                pe.wait_ge(p_exp, 4 * (UNITS - 1) + t + 1)
                tile_of(pe, n0 + t // 2, t % 2, bank[t][:, :], H).then_inc(tiles, 1)
            pe.wait_ge(got_con, CON_P)
            pe.wait_ge(t_act, 2 * UNITS)
            pe.wait_ge(t_dve, 2 * UNITS)
            for g in range(4):
                pe.wait_ge(p_mean, g + 1)
                if g >= 2:
                    pe.wait_ge(p_out, g - 1)
                pe.matmul(bank[4 + g % 2][:, :], pw[:, g, :], pm[:, g, :], start=True, stop=True).then_inc(p_mm, 1)

        @block.scalar
        def _(act):
            for b in (n0, n0 + 1):
                split_hi(act, b + 2)
            for g in range(4):
                act.wait_ge(p_mm, g + 1)
                act.activation(pmh[:, g, :], bank[4 + g % 2][:, :], ACT.Copy, scale=pcol("pool_scale", g)) \
                    .then_inc(p_high, 1)

        @block.vector
        def _(dve):
            dve.wait_ge(pv_done, UNITS)
            for t in range(4):
                dve.wait_ge(tiles, 2 * n0 + t + 1)
                dve.tensor_copy(pu[:, t, 16:16 + S], bank[t][:, :]).then_inc(drained, 1)
                if t % 2:
                    split_lo(dve, n0 + 2 + t // 2)
            dve.wait_ge(drained, m0 + 4)
            dve.wait_ge(p_pad, 1)
            dve.wait_ge(got_con, CON_P)
            for g, wd in enumerate(POOL_WINDOWS):
                src, step, flip = pu[:, g, :], 1, 0
                while step < wd:
                    dst = pa[:, flip, :]
                    dch(dve, dve.tensor_tensor(dst[:, 16:16 + S], src[:, 16:16 + S], src[:, 16 - step:16 + S - step],
                                               ALU.add))
                    src, step, flip = dst, 2 * step, 1 - flip
                dch(dve, dve.tensor_tensor(pm[:, g, 0:16], src[:, 16:32], rc[:, g, :], ALU.mult))
                dch(dve, dve.tensor_tensor(pm[:, g, 0:16], pm[:, g, 0:16], pu[:, g, 16:32], ALU.subtract))
                dch(dve, dve.scalar_tensor_tensor(out=pm[:, g, 16:S], in0=src[:, 32:16 + S], scalar=1.0 / wd,
                                                  in1=pu[:, g, 32:16 + S], op0=ALU.mult, op1=ALU.subtract))
                dve.sem_inc(p_mean, 1)
            for g in range(4):
                dve.wait_ge(p_high, g + 1)
                dve.scalar_tensor_tensor(out=pml[:, g, :], in0=bank[4 + g % 2][:, :], scalar=pcol("pool_scale", g),
                                         in1=pmh[:, g, :].bitcast(F32), op0=ALU.mult,
                                         op1=ALU.subtract).then_inc(p_out, 1)

    mh = at("mh", Y + 16 * K, [KT, S], F32R)
    ml = at("ml", Y + 48 * K, [KT, S], F32R)
    gs = at("gs", SC_AT, [4, S])
    mt = at("mt", SC_AT + 8 * K, [2, S])
    mu = at("mu", SC_AT + 12 * K, [2, S])
    g_sig, g_pool, g_full, g_high, g_low = sem("g_sig"), sem("g_pool"), sem("g_full"), sem("g_high"), sem("g_low")
    MI = D // IC

    def block1_merge():
        n0 = new_items(4 * MI)

        @block.sync
        def _(sp):
            with sp.Fori(0, MI) as i:
                for j in range(4):
                    b = n0 + j
                    if j == 2:
                        v = w["w_pool_br"].rearrange("(k p) n -> p k n", p=P)
                        s = wraw[:, b % 2]
                        pairs = [(s[:, k:k + 2, :], v[:, k:k + 2, bass.ds(IC * i, IC)]) for k in (0, 2)]
                    elif j == 3:
                        pairs = full_item(b, w["w_attn_br"], 0, IC * i)
                    else:
                        pairs = full_item(b, w["w_in"], 0, OFF_MG + D * j + IC * i)
                    load_item(sp, b, 2 * i, pairs)

        @block.tensor
        def _(pe):
            pe.wait_ge(drained, count_before_merge)
            with pe.Fori(0, MI) as i:
                for j in range(4):
                    if j < 2:
                        pe.wait_ge(g_sig, AHEAD + 4 * i)
                    elif j == 2:
                        pe.wait_ge(p_out, 4)
                        pe.wait_ge(g_pool, AHEAD + 2 * i)
                    else:
                        pe.wait_ge(o_out, NH // 2)
                        pe.wait_ge(g_full, AHEAD + 4 * i)
                    item_ready(pe, n0 + j, 2 * i)
                    for t in range(2):
                        rhs, kts = ((H, KT), (H, KT), ((pmh, pml), 4), ((oh, ol), KT))[j]
                        tile_of(pe, n0 + j, t, bank[2 * j + t][:, :], rhs, kts=kts).then_inc(tiles, 1)
            pe.wait_ge(g_low, AHEAD + KT)

        @block.scalar
        def _(act):
            with act.Fori(0, MI) as i:
                for j in range(4):
                    if j < 2:
                        for t in range(2):
                            act.wait_ge(tiles, 2 * (n0 + j) + t + 1 + 8 * i)
                            act.wait_ge(g_full, AHEAD + 4 * i)
                            act.activation(gs[:, 2 * j + t, :], bank[2 * j + t][:, :], ACT.Sigmoid).then_inc(g_sig, 1)
                    split_hi(act, n0 + 2 + j, 2 * i)
                for t in range(2):
                    act.wait_ge(g_full, AHEAD + 2 * t + 2 + 4 * i)
                    act.activation(flat(mh[:, bass.ds(2 * i + t, 1), :]), mt[:, t, :], ACT.Copy).then_inc(g_high, 1)

        @block.vector
        def _(dve):
            with dve.Fori(0, MI) as i:
                split_lo(dve, n0 + 2, 2 * i)
                split_lo(dve, n0 + 3, 2 * i)
                for t in range(2):
                    dve.wait_ge(tiles, 2 * (n0 + 2) + t + 1 + 8 * i)
                    dve.wait_ge(g_sig, AHEAD + 4 * i + 4)
                    dve.wait_ge(g_low, AHEAD + 2 * i)
                    dve.tensor_tensor(mt[:, t, :], gs[:, t, :], bank[4 + t][:, :], ALU.mult).then_inc(g_pool, 1)
                split_lo(dve, n0 + 4, 2 * i)
                for t in range(2):
                    dve.wait_ge(tiles, 2 * (n0 + 3) + t + 1 + 8 * i)
                    dve.tensor_tensor(mu[:, t, :], gs[:, 2 + t, :], bank[6 + t][:, :], ALU.mult).then_inc(g_full, 1)
                    dve.wait_ge(g_full, AHEAD + 2 * t + 1 + 4 * i)
                    dve.wait_ge(g_pool, AHEAD + 2 * i + t + 1)
                    dve.tensor_tensor(mt[:, t, :], mt[:, t, :], mu[:, t, :], ALU.add).then_inc(g_full, 1)
                split_lo(dve, n0 + 5, 2 * i)
                for t in range(2):
                    dve.wait_ge(g_high, 2 * i + t + 1)
                    dve.tensor_tensor(flat(ml[:, bass.ds(2 * i + t, 1), :]), mt[:, t, :],
                                      flat(mh[:, bass.ds(2 * i + t, 1), :]).bitcast(F32),
                                      ALU.subtract).then_inc(g_low, 1)

    def residual(mat, rhs, r0=0, last=False, ready=None):
        n0, m0 = new_items(4), new_tiles(KT)

        @block.sync
        def _(sp):
            with sp.Fori(0, 2) as i:
                for j in range(2):
                    load_item(sp, n0 + j, i, full_item(n0 + j, mat, r0, IC * j + 2 * IC * i))

        @block.tensor
        def _(pe):
            pe.wait_ge(drained, m0)
            with pe.Fori(0, 2) as i:
                for t in range(4):
                    if t % 2 == 0:
                        item_ready(pe, n0 + t // 2, i)
                    pe.wait_ge(drained, m0 - 4 + t + 1 + 4 * i)
                    tile_of(pe, n0 + t // 2, t % 2, bank[t][:, :], rhs, ready=ready if t == 0 else None) \
                        .then_inc(tiles, 1)

        @block.scalar
        def _(act):
            if last:
                split_hi(act, n0 + 2)
                split_hi(act, n0 + 3)
                return
            with act.Fori(0, 2) as i:
                for j in range(2):
                    split_hi(act, n0 + 2 + j, i)

        @block.vector
        def _(dve):
            def part(i):
                for t in range(4):
                    dve.wait_ge(tiles, 2 * n0 + t + 1 + 4 * i)
                    x_t = flat(xt[:, bass.ds(4 * i + t, 1), :])
                    dve.tensor_tensor(x_t, x_t, bank[t][:, :], ALU.add).then_inc(drained, 1)
                    if t % 2:
                        split_lo(dve, n0 + 2 + t // 2, i)

            if last:
                part(0)
                part(1)
                return
            with dve.Fori(0, 2) as i:
                part(i)
        return m0

    yh = at("yh", Y, [FT + 1, S], F32R)
    yl = at("yl", Y + 44 * K, [FT + 1, S], F32R)
    cg = at("cg", SC_AT, [2, S])
    cv = at("cv", SC_AT + 4 * K, [2, S])
    fa = at("fa", SC_AT + 8 * K, [2, S])
    f_id, f_conv, f_silu, f_act, f_high, f_low = (sem("f_id"), sem("f_conv"), sem("f_silu"), sem("f_act"),
                                                  sem("f_high"), sem("f_low"))

    def ffn_up():
        n0, m0 = new_items(FT + 1), new_tiles(2 * (FT + 1))
        v = w["w_up"].rearrange("(k p) n -> p k n", p=P)
        LOOPS = FT // 2
        rest = [FT - 1, FT] if FT % 2 else [FT]

        def pairs(b, c0, cols):
            s = wraw[:, b % 2]
            return [(s[:, :, 0:cols], v[:, :, bass.ds(c0, cols)]), (s[:, :, P:P + cols], v[:, :, bass.ds(c0 + DFF, cols)])]

        @block.sync
        def _(sp):
            with sp.Fori(0, LOOPS) as i:
                for j in range(2):
                    load_item(sp, n0 + j, i, pairs(n0 + j, P * j + IC * i, P))
            for f in rest:
                load_item(sp, n0 + f, 0, pairs(n0 + f, P * f, P if f < FT else FREST))

        def products(pe, b, j, i, f, cols):
            item_ready(pe, b, i)
            for t in range(2):
                pe.wait_ge(drained, m0 - 4 + 2 * f + t + 1)
                tile_of(pe, b, t, bank[2 * j + t][0:cols, :], H, cols=cols).then_inc(tiles, 1)

        def straight(act, b, j, i, f, n):
            for t, (wn, bn, dst) in enumerate((("convw_g", "convb_g", cg), ("convw_v", "convb_v", cv))):
                act.wait_ge(tiles, 2 * b + 4 * i + t + 1)
                if not (isinstance(f, int) and f < 2):
                    act.wait_ge(f_act, AHEAD + f - 1)
                act.activation(dst[0:n, j, :], bank[2 * j + t][0:n, :], ACT.Identity,
                               scale=pcol_at(wn, 2 * (FT + 1) + f, n), bias=pcol_at(bn, f, n)).then_inc(f_id, 1)

        def conv(dve, b, j, i, f, n):
            for t, (wn, dst) in enumerate((("convw_g", cg), ("convw_v", cv))):
                src = bank[2 * j + t]
                dve.wait_ge(f_id, 2 * f + t + 1)
                dve.scalar_tensor_tensor(out=dst[0:n, j, 1:S], in0=src[0:n, 0:S - 1],
                                         scalar=pcol_at(wn, FT + 1 + f, n), in1=dst[0:n, j, 1:S],
                                         op0=ALU.mult, op1=ALU.add).then_inc(f_conv, 1)
                dve.wait_ge(f_conv, 4 * f + 2 * t + 1)
                dve.scalar_tensor_tensor(out=dst[0:n, j, 2:S], in0=src[0:n, 0:S - 2],
                                         scalar=pcol_at(wn, f, n), in1=dst[0:n, j, 2:S],
                                         op0=ALU.mult, op1=ALU.add).then_inc(f_conv, 1)
                dve.wait_ge(f_conv, 4 * f + 2 * t + 2)
                dve.sem_inc(drained, 1)

        def gate(act, j, f, n):
            act.wait_ge(f_conv, 4 * f + 2)
            act.activation(cg[0:n, j, :], cg[0:n, j, :], ACT.Silu).then_inc(f_silu, 1)

        def product(dve, j, f, n):
            dve.wait_ge(f_silu, f + 1)
            if not (isinstance(f, int) and f < 2):
                dve.wait_ge(f_low, AHEAD + f - 1)
            dve.tensor_tensor(fa[0:n, j, :], cg[0:n, j, :], cv[0:n, j, :], ALU.mult).then_inc(f_act, 1)

        def high(act, j, f, n):
            act.wait_ge(f_act, AHEAD + f + 1)
            act.activation(flat(yh[0:n, bass.ds(f, 1), :]), fa[0:n, j, :], ACT.Copy).then_inc(f_high, 1)

        def low(dve, j, f, n):
            dve.wait_ge(f_high, f + 1)
            dve.tensor_tensor(flat(yl[0:n, bass.ds(f, 1), :]), fa[0:n, j, :],
                              flat(yh[0:n, bass.ds(f, 1), :]).bitcast(F32), ALU.subtract).then_inc(f_low, 1)

        def each(loop, eng, body):
            with eng.Fori(0, LOOPS) as i:
                for j in range(2):
                    body(n0 + j, j, i, 2 * i + j, P)
            for f in rest:
                body(n0 + f, f % 2, 0, f, P if f < FT else FREST)

        @block.tensor
        def _(pe):
            pe.wait_ge(drained, m0)
            each(None, pe, lambda b, j, i, f, n: products(pe, b, j, i, f, n))

        @block.scalar
        def _(act):
            def body(b, j, i, f, n):
                straight(act, b, j, i, f, n)
                split_hi(act, b + 2, i)
                gate(act, j, f, n)
                high(act, j, f, n)
            act.wait_ge(g_low, AHEAD + KT)
            each(None, act, body)

        @block.vector
        def _(dve):
            def body(b, j, i, f, n):
                conv(dve, b, j, i, f, n)
                product(dve, j, f, n)
                split_lo(dve, b + 2, i)
                low(dve, j, f, n)
            each(None, dve, body)

    def ffn_down():
        PER = 3
        n0, m0 = new_items(PER * MI), new_tiles(KT)
        mat = w["w_down"]
        v = mat[0:FT * P, :].rearrange("(k p) n -> p k n", p=P)

        @block.sync
        def _(sp):
            with sp.Fori(0, MI // 2) as i:
                for c in range(2):
                    for part in range(PER):
                        b = n0 + PER * c + part
                        s = wraw[:, b % 2]
                        cols = bass.ds(IC * c + 2 * IC * i, IC)
                        if part < 2:
                            pr_ = [(s[:, 0:4, :], v[:, 8 * part:8 * part + 4, cols]),
                                   (s[:, 4:8, :], v[:, 8 * part + 4:8 * part + 8, cols])]
                        else:
                            pr_ = [(s[:, 0:FT - 16, :], v[:, 16:FT, cols]),
                                   (s[0:FREST, FT - 16, :], mat[FT * P:DFF, cols])]
                        load_item(sp, b, PER * i, pr_)

        @block.tensor
        def _(pe):
            pe.wait_ge(f_low, AHEAD + FT + 1)
            pe.wait_ge(drained, m0)
            with pe.Fori(0, MI // 2) as i:
                for c in range(2):
                    for part in range(PER):
                        b = n0 + PER * c + part
                        item_ready(pe, b, PER * i)
                        p = b % 2
                        for t in range(2):
                            if part == 0:
                                pe.wait_ge(drained, m0 - 4 + 2 * c + t + 1 + 4 * i)
                            out = bank[2 * c + t][:, :]
                            if part < 2:
                                mm = tile_of(pe, b, t, out, (yh, yl), k0=8 * part, first=part == 0, last=False)
                            else:
                                tile_of(pe, b, t, out, (yh, yl), kts=FT - 16, k0=16, first=False, last=False)
                                k, cs = FT - 16, slice(P * t, P * t + P)
                                mm = passes(pe, out, (whi[0:FREST, p, k, cs], wlo[0:FREST, p, k, cs]),
                                            (yh[0:FREST, FT, :], yl[0:FREST, FT, :]), False, True)
                            mm.then_inc(tiles, 1)

        @block.scalar
        def _(act):
            with act.Fori(0, MI // 2) as i:
                for j in range(2 * PER):
                    split_hi(act, n0 + 2 + j, PER * i)

        @block.vector
        def _(dve):
            with dve.Fori(0, MI // 2) as i:
                for c in range(2):
                    for part in range(PER):
                        b = n0 + PER * c + part
                        if part == PER - 1:
                            for t in range(2):
                                dve.wait_ge(tiles, 2 * b + t + 1 + 4 * PER * i // 1)
                                x_t = flat(xt[:, bass.ds(4 * i + 2 * c + t, 1), :])
                                dve.tensor_tensor(x_t, x_t, bank[2 * c + t][:, :], ALU.add).then_inc(drained, 1)
                        split_lo(dve, b + 2, PER * i)
        return m0

    def project(mat, c0, dst, scale=1.0, bias=None, wait=None):
        n0, m0 = new_items(4), new_tiles(KT)

        @block.sync
        def _(sp):
            with sp.Fori(0, 2) as i:
                for j in range(2):
                    load_item(sp, n0 + j, i, full_item(n0 + j, mat, 0, c0 + IC * j + 2 * IC * i))

        @block.tensor
        def _(pe):
            pe.wait_ge(drained, m0)
            with pe.Fori(0, 2) as i:
                for t in range(4):
                    if t % 2 == 0:
                        item_ready(pe, n0 + t // 2, i)
                    pe.wait_ge(drained, m0 - 4 + t + 1 + 4 * i)
                    tile_of(pe, n0 + t // 2, t % 2, bank[t][:, :], H).then_inc(tiles, 1)

        @block.scalar
        def _(act):
            with act.Fori(0, 2) as i:
                for j in range(2):
                    split_hi(act, n0 + 2 + j, i)

        @block.vector
        def _(dve):
            if wait:
                dve.wait_ge(*wait)
            with dve.Fori(0, 2) as i:
                for t in range(4):
                    dve.wait_ge(tiles, 2 * n0 + t + 1 + 4 * i)
                    out_t = flat(dst[:, bass.ds(4 * i + t, 1), :])
                    if bias:
                        ins = dve.tensor_scalar(out_t, bank[t][:, :], pcol_at(bias, 4 * i + t), scale,
                                                ALU.add, ALU.mult)
                    else:
                        ins = dve.tensor_scalar(out_t, bank[t][:, :], scale, None, ALU.mult)
                    ins.then_inc(drained, 1)
                    if t % 2:
                        split_lo(dve, n0 + 2 + t // 2, i)
        return m0

    e_silu, e_prod, e_high, e_low = sem("e_silu"), sem("e_prod"), sem("e_high"), sem("e_low")
    sg = at("sg", SC_AT, [2, S])
    ep = at("ep", SC_AT + 4 * K, [2, S])
    gated = [0]

    def gate_and_split(mat, c0, src, dst, bias=None, wait=None):
        n0, m0, q0 = new_items(4), new_tiles(KT), KT * gated[0]
        gated[0] += 1

        @block.sync
        def _(sp):
            with sp.Fori(0, 2) as i:
                for j in range(2):
                    load_item(sp, n0 + j, i, full_item(n0 + j, mat, 0, c0 + IC * j + 2 * IC * i))

        @block.tensor
        def _(pe):
            pe.wait_ge(drained, m0)
            with pe.Fori(0, 2) as i:
                for t in range(4):
                    if t % 2 == 0:
                        item_ready(pe, n0 + t // 2, i)
                    pe.wait_ge(drained, m0 - 4 + t + 1 + 4 * i)
                    tile_of(pe, n0 + t // 2, t % 2, bank[t][:, :], H).then_inc(tiles, 1)
            pe.wait_ge(e_low, AHEAD + q0 + KT)

        @block.scalar
        def _(act):
            if wait:
                act.wait_ge(*wait)
            if q0:
                act.wait_ge(e_low, AHEAD + q0)
            with act.Fori(0, 2) as i:
                for t in range(4):
                    act.wait_ge(tiles, 2 * n0 + t + 1 + 4 * i)
                    if t >= 2:
                        act.wait_ge(e_prod, AHEAD + q0 + t - 1 + 4 * i)
                    else:
                        act.wait_ge(e_prod, AHEAD + q0 + 4 * i)
                    b = pcol_at(bias, 4 * i + t) if bias else 0.0
                    act.activation(sg[:, t % 2, :], bank[t][:, :], ACT.Silu, bias=b).then_inc(e_silu, 1)
                    act.wait_ge(e_prod, AHEAD + q0 + t + 1 + 4 * i)
                    act.activation(flat(dst[0][:, bass.ds(4 * i + t, 1), :]), ep[:, t % 2, :],
                                   ACT.Copy).then_inc(e_high, 1)
                    if t % 2:
                        split_hi(act, n0 + 2 + t // 2, i)

        @block.vector
        def _(dve):
            with dve.Fori(0, 2) as i:
                for t in range(4):
                    dve.wait_ge(e_silu, q0 + t + 1 + 4 * i)
                    dve.sem_inc(drained, 1)
                    if t >= 2:
                        dve.wait_ge(e_low, AHEAD + q0 + t - 1 + 4 * i)
                    else:
                        dve.wait_ge(e_low, AHEAD + q0 + 4 * i)
                    dve.tensor_tensor(ep[:, t % 2, :], sg[:, t % 2, :], flat(src[:, bass.ds(4 * i + t, 1), :]),
                                      ALU.mult).then_inc(e_prod, 1)
                    if t % 2:
                        split_lo(dve, n0 + 2 + t // 2, i)
                    dve.wait_ge(e_high, q0 + t + 1 + 4 * i)
                    dve.tensor_tensor(flat(dst[1][:, bass.ds(4 * i + t, 1), :]), ep[:, t % 2, :],
                                      flat(dst[0][:, bass.ds(4 * i + t, 1), :]).bitcast(F32),
                                      ALU.subtract).then_inc(e_low, 1)
        return m0

    ah = at("ah", Y, [KT, S], F32R)
    al = at("al", Y + 16 * K, [KT, S], F32R)
    q2 = at("q2", Y + 32 * K, [KT, S])
    k2 = at("k2", Y + 48 * K, [KT, S])
    v2 = at("v2", Y + 64 * K, [TT, D])
    pt2 = [at("pt2a", Y + 80 * K, [TT, S]), at("pt2b", SC_AT + 8 * K, [TT, S])]
    pr2 = at("pr2", SC_AT, [2, 2, S])
    dist = at("dist", SC_AT + 16 * K, [S], F32R)
    dg2 = at("dg2", SC_AT + 18 * K, [2, P], F32R)
    S2 = SC_AT + 19 * K
    nm2 = at("nm2", S2, [2, 2])
    sm2 = at("sm2", S2 + 32, [2, 2])
    rs2 = at("rs2", S2 + 64, [2, 2])
    nlam = at("nlam", S2 + 96, [4])
    lprod = at("lprod", S2 + 128, [2])
    rta = at("rta", S2 + 160, [TT, DA_H])
    rra = at("rra", S2 + 288, [TT, DA_H])
    distf = at("distf", SC_AT, [S])
    d_ready, l_prod, l_sum, l_exp, l_lam = (sem("d_ready"), sem("l_prod"), sem("l_sum"),
                                                    sem("l_exp"), sem("l_lam"))
    dg_done, s2_done, s2_max, p2_exp, p2_done = sem("dg_done"), sem("s2_done"), sem("s2_max"), sem("p2_exp"), sem("p2_done")
    t2_done, t2_act, t2_dve, pv2_done, o2_out = (sem("t2_done"), sem("t2_act"), sem("t2_dve"), sem("pv2_done"),
                                                 sem("o2_out"))
    a_sq, a_used, a_root, a_rec, a_spread, a_out = (sem("a_sq"), sem("a_used"), sem("a_root"), sem("a_rec"),
                                                    sem("a_spread"), sem("a_out"))
    sqa = at("sqa", SC_AT, [2, S])

    def diff_values():
        n0, m0 = new_items(4), new_tiles(KT)
        mat = w["w_in_a_2"]

        @block.sync
        def _(sp):
            with sp.Fori(0, 2) as i:
                for j in range(2):
                    load_item(sp, n0 + j, i, full_item(n0 + j, mat, 0, OFF_V2 + IC * j + 2 * IC * i))

        @block.tensor
        def _(pe):
            pe.wait_ge(drained, m0)
            with pe.Fori(0, 2) as i:
                for j in range(2):
                    item_ready(pe, n0 + j, i)
                    for half in range(2):
                        pe.wait_ge(drained, m0 - 4 + 2 * j + half + 1 + 4 * i)
                        for t in range(2):
                            mm = rows_of(pe, n0 + j, 2 * half + t, bank[2 * j + half][:, IC * t:IC * t + IC], IC)
                        mm.then_inc(tiles, 1)

        @block.scalar
        def _(act):
            with act.Fori(0, 2) as i:
                for j in range(2):
                    split_hi(act, n0 + 2 + j, i)

        @block.vector
        def _(dve):
            with dve.Fori(0, 2) as i:
                for j in range(2):
                    for half in range(2):
                        dve.wait_ge(tiles, 2 * n0 + 2 * j + half + 1 + 4 * i)
                        dve.tensor_copy(v2[:, 2 * half:2 * half + 2, bass.ds(IC * j + 2 * IC * i, IC)],
                                        bank[2 * j + half][:, :].rearrange("p (t n) -> p t n", t=2)) \
                            .then_inc(drained, 1)
                    split_lo(dve, n0 + 2 + j, i)
        return m0

    STEPS = DA_H * TT
    k2r = at("k2r", Y + 48 * K, [KT, S], F32R)
    qs2 = at("qs2", Y + 16 * K, [2, 2, S], F32R)
    kh2 = at("kh2", Y + 24 * K, [2, 2, S], F32R)
    sga = at("sga", Y, [KT, S])

    def diff_attention(m1):
        sl = slopes(DA_H)
        n0, m0, q0 = new_items(4), new_tiles(KT), KT * gated[0]
        gated[0] += 1
        QB = NH // 2

        @block.sync
        def _(sp):
            with sp.Fori(0, 2) as i:
                for j in range(2):
                    load_item(sp, n0 + j, i, full_item(n0 + j, w["w_in_a_2"], 0, OFF_GA + IC * j + 2 * IC * i))

        @block.tensor
        def _(pe):
            pe.wait_ge(l_prod, 1)
            pe.matmul(bank[4][:, 0:2], ones[:, :], lprod[:, :], start=True, stop=True).then_inc(l_sum, 1)
            pe.wait_ge(l_lam, 1)
            pe.wait_ge(drained, m1)
            pe.wait_ge(d_ready, 1)

            def scores(u):
                h, i = u // TT, u % TT
                wd = P * (i + 1)
                if i == 0:
                    pe.wait_ge(dg_done, h + 1)
                    pe.wait_ge(q_lo, QB + h + 1)
                for m in range(2):
                    rows = slice(HD * m, HD * m + HD)
                    if u >= 2:
                        pe.wait_ge(p2_exp, 2 * (u - 2) + m + 1)
                    out = bank[2 * (u % 2) + m][:, 0:wd]
                    pe.matmul(out, qs2[:, h % 2, m, P * i:P * i + P], kh2[:, h % 2, m, 0:wd], start=True, stop=False)
                    pe.matmul(out, qs2[rows, h % 2, m, P * i:P * i + P], k2r[rows, h, 0:wd], start=False, stop=False)
                    pe.matmul(out, dg2[:, h % 2, :], dist[:, S - wd:S], start=False, stop=True).then_inc(s2_done, 1)

            def turn(u):
                i = u % TT
                pe.wait_ge(p2_done, u + 1)
                if u >= 2:
                    pe.wait_ge(t2_dve if u % 2 else t2_act, u // 2)
                for j in range(i + 1):
                    mm = pe.transpose(bank[4 + u % 2][:, P * j:P * j + P], pr2[:, u % 2, 0, P * j:P * j + P],
                                      ident[:, :])
                mm.then_inc(t2_done, 1)

            def values(h):
                pe.wait_ge(t2_act, 2 * h + 2)
                pe.wait_ge(t2_dve, 2 * h + 2)
                if h:
                    pe.wait_ge(o2_out, h)
                for j in range(TT):
                    mm = pe.matmul(bank[6][:, P * j:S], v2[:, j, P * h:P * h + P], pt2[h % 2][:, j, P * j:S],
                                   start=(j == 0), stop=(j == TT - 1))
                mm.then_inc(pv2_done, 1)

            def gate_part(u):
                h, i = u // TT, u % TT
                if i == 0:
                    if h % 2 == 0:
                        item_ready(pe, n0 + h // 2)
                    pe.wait_ge(drained, m0 + h)
                mm = tile_of(pe, n0 + h // 2, h % 2, bank[7][:, :], H, kts=2, k0=2 * i, w0=2 * i, first=i == 0,
                             last=i == TT - 1)
                if i == TT - 1:
                    mm.then_inc(tiles, 1)

            scores(0)
            for u in range(STEPS + 1):
                if u:
                    turn(u - 1)
                if u + 1 < STEPS:
                    scores(u + 1)
                if u < STEPS:
                    gate_part(u)
                if u > TT and (u - 2) % TT == TT - 1:
                    values((u - 2) // TT)
            values(DA_H - 1)

        def turned(eng, u, signal, copy):
            h, i = u // TT, u % TT
            eng.wait_ge(t2_done, u + 1)
            if h >= 2:
                eng.wait_ge(pv2_done, h - 1)
            copy(pt2[h % 2][:, 0:i + 1, P * i:P * i + P],
                 bank[4 + u % 2][:, 0:P * (i + 1)].rearrange("p (j q) -> p j q", j=i + 1)).then_inc(signal, 1)

        @block.scalar
        def _(act):
            act.wait_ge(drained, m1)
            act.dma_start(distf[:, :], con[:, CCOL["dist"]:CCOL["dist"] + S]).then_inc(got_con, 16)
            act.wait_ge(got_con, CON2)
            act.activation(dist[:, :], distf[:, :], ACT.Copy).then_inc(d_ready, 1)
            act.wait_ge(l_sum, 1)
            act.activation(nlam[:, 0:2], bank[4][:, 0:2], ACT.Exp).then_inc(l_exp, 1)

            def diag(h):
                if h >= 2:
                    act.wait_ge(s2_done, 8 * (h - 1))
                act.activation(dg2[:, h % 2, :], ident[:, :], ACT.Copy, scale=sl[h]).then_inc(dg_done, 1)

            def high(h, m, what):
                rows, other = slice(HD * m, HD * m + HD), slice(HD - HD * m, P - HD * m)
                if what == "q":
                    return act.activation(qs2[rows, h % 2, m, :], q2[rows, h, :], ACT.Copy)
                return act.activation(kh2[rows if what == "k" else other, h % 2, m, :], k2[rows, h, :], ACT.Copy)

            def high_parts(h, step):
                if step == 0:
                    if h >= 2:
                        act.wait_ge(s2_done, 8 * (h - 1))
                    high(h, 0, "q")
                    high(h, 1, "q")
                    high(h, 0, "k")
                else:
                    high(h, 0, "other")
                    high(h, 1, "k")
                    high(h, 1, "other").then_inc(q_hi, 1)

            def out_head(h):
                act.wait_ge(pv2_done, h + 1)
                act.activation(q2[:, h, :], bank[6][:, :], ACT.Copy).then_inc(o2_out, 1)

            diag(0)
            act.wait_ge(d_ready, 1)
            high_parts(0, 0)
            high_parts(0, 1)
            for u in range(STEPS + 3):
                h, i = u // TT, u % TT
                if u < STEPS:
                    wd = P * (i + 1)
                    for m in range(2):
                        act.wait_ge(s2_max, 2 * u + m + 1)
                        if u >= 2:
                            act.wait_ge(t2_done, u - 1)
                        act.activation(pr2[:, u % 2, m, 0:wd], bank[2 * (u % 2) + m][:, 0:wd], ACT.Exp,
                                       bias=nm2[:, u % 2, m:m + 1],
                                       accum_out=sm2[:, u % 2, m:m + 1]).then_inc(p2_exp, 1)
                if 1 <= u <= STEPS and (u - 1) % 2 == 0:
                    turned(act, u - 1, t2_act, lambda o, s_: act.activation(o, s_, ACT.Copy))
                if u < STEPS:
                    if i < 2 and h + 1 < DA_H:
                        high_parts(h + 1, i)
                        if i == 0:
                            diag(h + 1)
                    if i == 2 and h % 2 == 0 and h:
                        split_hi(act, n0 + h // 2 + 1)
                if 0 < u <= STEPS and i == 0:
                    act.wait_ge(tiles, 2 * n0 + h)
                    act.activation(sga[:, h - 1, :], bank[7][:, :], ACT.Copy).then_inc(drained, 1)
                if u > TT and (u - 3) % TT == TT - 1:
                    out_head((u - 3) // TT)
            split_hi(act, n0 + 5)

        @block.vector
        def _(dve):
            lamc = pcol("lam", 0, n=4).rearrange("p (a b) -> p a b", b=2)
            dve.tensor_tensor(lprod[:, :], lamc[:, :, 0], lamc[:, :, 1], ALU.mult).then_inc(l_prod, 1)
            dve.wait_ge(l_exp, 1)
            dve.scalar_tensor_tensor(out=nlam[:, 2:3], in0=nlam[:, 1:2], scalar=-LAMBDA_INIT, in1=nlam[:, 0:1],
                                     op0=ALU.add, op1=ALU.subtract).then_inc(l_lam, 1)
            dve.wait_ge(l_lam, 1)

            def low(h, m, what):
                rows, other = slice(HD * m, HD * m + HD), slice(HD - HD * m, P - HD * m)
                if what == "q":
                    return dve.tensor_tensor(qs2[other, h % 2, m, :], q2[rows, h, :],
                                             qs2[rows, h % 2, m, :].bitcast(F32), ALU.subtract)
                return dve.tensor_tensor(k2r[rows, h, :], k2[rows, h, :], kh2[rows, h % 2, m, :].bitcast(F32),
                                         ALU.subtract)

            def low_parts(h, what):
                dve.wait_ge(q_hi, QB + h + 1)
                low(h, 0, what)
                ins = low(h, 1, what)
                if what == "k":
                    ins.then_inc(q_lo, 1)

            low_parts(0, "q")
            low_parts(0, "k")
            for u in range(STEPS + 2):
                if u < STEPS:
                    wd = P * (u % TT + 1)
                    for m in range(2):
                        dve.wait_ge(s2_done, 2 * u + m + 1)
                        if u >= 2:
                            dve.wait_ge(p2_exp, 2 * (u - 2) + m + 1)
                        dve.tensor_reduce(nm2[:, u % 2, m:m + 1], bank[2 * (u % 2) + m][:, 0:wd], AX, ALU.max,
                                          negate=True).then_inc(s2_max, 1)
                if 1 <= u <= STEPS:
                    v = u - 1
                    wd = P * (v % TT + 1)
                    dve.wait_ge(p2_exp, 2 * v + 2)
                    r = rs2[:, v % 2, :]
                    if v:
                        dve.wait_ge(p2_done, v)
                    dch(dve, dve.reciprocal(r, sm2[:, v % 2, :]))
                    dch(dve, dve.tensor_scalar(rs2[:, v % 2, 1:2], rs2[:, v % 2, 1:2], nlam[:, 2:3], None, ALU.mult))
                    a, b = pr2[:, v % 2, 0, 0:wd], pr2[:, v % 2, 1, 0:wd]
                    dch(dve, dve.tensor_scalar(a, a, rs2[:, v % 2, 0:1], None, ALU.mult))
                    dve.scalar_tensor_tensor(out=a, in0=b, scalar=rs2[:, v % 2, 1:2], in1=a, op0=ALU.mult,
                                             op1=ALU.add).then_inc(p2_done, 1)
                if u >= 1 and (u - 1) % 2 and u <= STEPS:
                    turned(dve, u - 1, t2_dve, dve.tensor_copy)
                if u < STEPS:
                    h, i = u // TT, u % TT
                    if h + 1 < DA_H and i in (2, 3):
                        low_parts(h + 1, "q" if i == 2 else "k")
                    if i == 3 and h % 2 == 0 and h:
                        split_lo(dve, n0 + h // 2 + 1)
            split_lo(dve, n0 + 5)

        @block.scalar
        def _(act):
            act.wait_ge(t2_done, STEPS)
            act.wait_ge(o2_out, DA_H)
            act.wait_ge(drained, m0 + KT)
            for h in range(DA_H):
                act.activation(sga[:, h, :], sga[:, h, :], ACT.Silu).then_inc(e_silu, 1)
                if h >= 2:
                    act.wait_ge(a_used, h - 1)
                act.activation(sqa[:, h % 2, :], q2[:, h, :], ACT.Square).then_inc(a_sq, 1)
            act.wait_ge(a_used, DA_H)
            act.activation(rta[:, :, :], bank[4][:, 0:TT * DA_H].rearrange("p (t h) -> p t h", t=TT), ACT.Sqrt,
                           bias=eps[:, 1:2], scale=1.0 / P).then_inc(a_root, 1)
            for h in range(DA_H):
                act.wait_ge(e_prod, AHEAD + q0 + h + 1)
                act.activation(ah[:, h, :], q2[:, h, :], ACT.Copy).then_inc(e_high, 1)

        @block.tensor
        def _(pe):
            pe.wait_ge(t2_act, STEPS // 2)
            for h in range(DA_H):
                pe.wait_ge(a_sq, h + 1)
                for t in range(TT):
                    mm = pe.matmul(bank[4][:, DA_H * t + h:DA_H * t + h + 1], sqa[:, h % 2, P * t:P * t + P],
                                   ones[:, 0:1], start=True, stop=True)
                mm.then_inc(a_used, 1)
            pe.wait_ge(a_rec, 2)
            pe.wait_ge(t2_dve, STEPS // 2)
            for h in range(DA_H):
                if h >= 3:
                    pe.wait_ge(e_prod, AHEAD + q0 + h - 2)
                spread(pe, bank[5 + h % 3], lambda t: rra[:, t, h:h + 1].to_broadcast([P, P])).then_inc(a_spread, 1)

        @block.vector
        def _(dve):
            for h in range(DA_H):
                dve.wait_ge(e_silu, q0 + h + 1)
                dve.wait_ge(a_sq, h + 1)
                dve.scalar_tensor_tensor(out=q2[:, h, :], in0=q2[:, h, :], scalar=pcol("subln"), in1=sga[:, h, :],
                                         op0=ALU.mult, op1=ALU.mult).then_inc(a_out, 1)
            dve.wait_ge(a_root, 1)
            dve.reciprocal(rra[:, :, :], rta[:, :, :]).then_inc(a_rec, 1)
            dve.wait_ge(a_rec, 1)
            dve.tensor_scalar(rra[:, :, :], rra[:, :, :], 1.0 - LAMBDA_INIT, None, ALU.mult).then_inc(a_rec, 1)

            def low_out(h):
                dve.wait_ge(e_high, h + 1)
                dve.tensor_tensor(al[:, h, :], q2[:, h, :], ah[:, h, :].bitcast(F32), ALU.subtract).then_inc(e_low, 1)

            for h in range(DA_H):
                dve.wait_ge(a_spread, h + 1)
                dve.wait_ge(a_out, h + 1)
                dve.tensor_tensor(q2[:, h, :], q2[:, h, :], bank[5 + h % 3][:, :], ALU.mult).then_inc(e_prod, 1)
                if h:
                    low_out(h - 1)
            low_out(DA_H - 1)
        return (e_low, AHEAD + q0)

    xbc = at("xbc", Y + 32 * K, [12, S])
    xtok = at("xtok", Y + 56 * K, [CH, D])
    btok = at("btok", Y + 72 * K, [CH, 2, P])
    cbt = at("cbt", Y + 76 * K, [2, S])
    xpad = at("xpad", Y + 80 * K, [2, 2, CH, P])
    sel = at("sel", Y, [SSD_H, P])
    selp = at("selp", Y + 8 * K, [8, P])
    cx = at("cx", SC_AT, [2, S])
    csf = at("csf", Y + 12 * K, [S])
    dtf = at("dtf", Y + 14 * K, [S])
    caut = at("caut", Y + 16 * K, [S], F32R)
    cautf = at("cautf", Y + 18 * K, [S])
    xdec = at("xdec", Y + 20 * K, [2, D])
    daf = at("daf", Y + 28 * K, [S])
    spx = at("spx", Y + 30 * K, [S])
    prevt = at("prevt", SC_AT, [CH - 1, D])
    lm = at("lm", SC_AT + 12 * K, [2, S])
    eb = at("eb", SC_AT + 16 * K, [S])
    S3 = SC_AT + 18 * K
    cst = at("cst", S3, [CH, SSD_H])
    dtt = at("dtt", S3 + 256, [CH, SSD_H])
    ncst = at("ncst", S3 + 512, [CH, SSD_H])
    dec = at("dec", S3 + 768, [CH, SSD_H])
    wdec = at("wdec", S3 + 1024, [CH, SSD_H])
    na = at("na", S3 + 1280, [1])
    mtt = at("mtt", Y + 20 * K, [2, S])
    yo = at("yo", Y + 24 * K, [S])
    b_id, b_conv, b_silu = sem("b_id"), sem("b_conv"), sem("b_silu")
    dt_v, dt_a, cs_done, cs_t, cs_tok, cl_mm, cl_exp = (
        sem("dt_v"), sem("dt_a"), sem("cs_done"), sem("cs_t"), sem("cs_tok"), sem("cl_mm"),
        sem("cl_exp"))
    x_t, x_tok, st_w, st_mm, st_done, cb_mm, cb_done, s3_pad = (
        sem("x_t"), sem("x_tok"), sem("st_w"), sem("st_mm"), sem("st_done"), sem("cb_mm"), sem("cb_done"),
        sem("s3_pad"))
    cs_mm, cs_exp, m_done, xp_done, y_mm, y_out = (sem("cs_mm"), sem("cs_exp"), sem("m_done"), sem("xp_done"),
                                                   sem("y_mm"), sem("y_out"))

    def ssd_inputs():
        n0, m0 = new_items(7), new_tiles(13)
        mat = w["w_in_a_2"]
        v = mat.rearrange("(k p) n -> p k n", p=P)

        @block.sync
        def _(sp):
            with sp.Fori(0, 3) as i:
                for j in range(2):
                    load_item(sp, n0 + j, i, full_item(n0 + j, mat, 0, OFF_XBC + IC * j + 2 * IC * i))
            b = n0 + 6
            s_ = wraw[:, b % 2]
            load_item(sp, b, 0, [(s_[:, 0:4, 0:SSD_H], v[:, 0:4, OFF_DT:OFF_DT + SSD_H]),
                                 (s_[:, 4:8, 0:SSD_H], v[:, 4:8, OFF_DT:OFF_DT + SSD_H])])

        @block.tensor
        def _(pe):
            pe.wait_ge(drained, m0)
            with pe.Fori(0, 3) as i:
                for t in range(4):
                    if t % 2 == 0:
                        item_ready(pe, n0 + t // 2, i)
                    pe.wait_ge(drained, m0 - 4 + t + 1 + 4 * i)
                    tile_of(pe, n0 + t // 2, t % 2, bank[t][:, :], H).then_inc(tiles, 1)
            item_ready(pe, n0 + 6)
            pe.wait_ge(drained, m0 + 9)
            tile_of(pe, n0 + 6, 0, bank[0][0:SSD_H, :], H, cols=SSD_H).then_inc(tiles, 2)

        @block.scalar
        def _(act):
            act.wait_ge(tiles, 2 * n0)
            for dst, name, n in ((sel, "sel", SSD_H * P), (selp, "selp", 8 * P)):
                act.dma_start(dst[:, :, :], con[:, CCOL[name]:CCOL[name] + n].rearrange("p (h n) -> p h n", n=P)) \
                    .then_inc(got_con, 16)
            act.dma_start(cautf[:, :], con[:, CCOL["causal_t"]:CCOL["causal_t"] + S]).then_inc(got_con, 16)
            with act.Fori(0, 3) as i:
                for t in range(4):
                    act.wait_ge(tiles, 2 * n0 + t + 1 + 4 * i)
                    if t >= 2:
                        act.wait_ge(b_silu, AHEAD + t - 1 + 4 * i)
                    else:
                        act.wait_ge(b_silu, AHEAD + 4 * i)
                    act.activation(cx[:, t % 2, :], bank[t][:, :], ACT.Identity, scale=pcol_at("conv_a", 36 + t + 4 * i),
                                   bias=pcol_at("convb_a", t + 4 * i)).then_inc(b_id, 1)
                    if t % 2:
                        split_hi(act, n0 + 2 + t // 2, i)
                    act.wait_ge(b_conv, 3 * t + 3 + 12 * i)
                    act.activation(flat(xbc[:, bass.ds(4 * i + t, 1), :]), cx[:, t % 2, :],
                                   ACT.Silu).then_inc(b_silu, 1)
            split_hi(act, n0 + 8)
            act.wait_ge(got_con, CON3)
            act.activation(caut[:, :], cautf[:, :], ACT.Copy)
            act.wait_ge(dt_v, 1)
            ach(act, act.activation(spx[0:SSD_H, :], daf[0:SSD_H, :], ACT.Abs))
            ach(act, act.activation(spx[0:SSD_H, :], spx[0:SSD_H, :], ACT.Exp, scale=-1.0))
            ach(act, act.activation(spx[0:SSD_H, :], spx[0:SSD_H, :], ACT.Ln, bias=ones[0:SSD_H, 0:1]))
            act.activation(na[0:SSD_H, :], pcol("a_log", rows=SSD_H), ACT.Exp).then_inc(dt_a, 1)

        @block.vector
        def _(dve):
            with dve.Fori(0, 3) as i:
                for t in range(4):
                    dve.wait_ge(b_id, t + 1 + 4 * i)
                    for tap in range(1, 4):
                        d_ = cx[:, t % 2, tap:S]
                        dve.scalar_tensor_tensor(out=d_, in0=bank[t][:, 0:S - tap],
                                                 scalar=pcol_at("conv_a", 12 * (3 - tap) + t + 4 * i), in1=d_,
                                                 op0=ALU.mult, op1=ALU.add).then_inc(b_conv, 1)
                        dve.wait_ge(b_conv, 3 * t + tap + 12 * i)
                    dve.sem_inc(drained, 1)
                    if t % 2:
                        split_lo(dve, n0 + 2 + t // 2, i)
            split_lo(dve, n0 + 8)
            dve.wait_ge(tiles, 2 * (n0 + 7))
            dve.tensor_scalar(daf[0:SSD_H, :], bank[0][0:SSD_H, :], pcol("dt_bias", rows=SSD_H), None,
                              ALU.add).then_inc(drained, 1)
            dve.wait_ge(drained, m0 + 13)
            dve.sem_inc(dt_v, 1)
            dve.wait_ge(dt_a, 1)
            dch(dve, dve.scalar_tensor_tensor(out=dtf[0:SSD_H, :], in0=daf[0:SSD_H, :], scalar=0.0,
                                              in1=spx[0:SSD_H, :], op0=ALU.max, op1=ALU.add))
            dch(dve, dve.tensor_scalar(daf[0:SSD_H, :], dtf[0:SSD_H, :], na[0:SSD_H, :], -1.0, ALU.mult, ALU.mult))
            for c in range(CH):
                cs = slice(P * c, P * c + P)
                ins = dve.tensor_tensor_scan(csf[0:SSD_H, cs], ones[0:SSD_H, :], daf[0:SSD_H, cs], 0.0,
                                             ALU.mult, ALU.add)
            dch(dve, ins)
            dve.sem_inc(cs_done, 1)
        return m0 + 13

    def ssd_core(m1):
        XB = 40

        @block.tensor
        def _(pe):
            pe.wait_ge(drained, m1)
            pe.wait_ge(b_silu, AHEAD + 12)
            for t in range(10):
                if t >= 3:
                    pe.wait_ge(x_tok, t - 2)
                for c in range(CH):
                    mm = pe.transpose(bank[5 + t % 3][:, P * c:P * c + P], xbc[:, t, P * c:P * c + P], ident[:, :])
                mm.then_inc(x_t, 1)
            for g in range(2):
                for c in range(CH):
                    cs = slice(P * c, P * c + P)
                    mm = pe.matmul(bank[2 + g][:, cs], xbc[:, 8 + g, cs], xbc[:, 10 + g, cs], start=True, stop=True)
                mm.then_inc(cb_mm, 1)
            pe.wait_ge(cs_done, 1)
            for c in range(CH):
                cs = slice(P * c, P * c + P)
                pe.transpose(bank[4][:, SSD_H * c:SSD_H * c + SSD_H], csf[0:SSD_H, cs], ident[0:SSD_H, 0:SSD_H])
                mm = pe.transpose(bank[4][:, 64 + SSD_H * c:64 + SSD_H * c + SSD_H], dtf[0:SSD_H, cs],
                                  ident[0:SSD_H, 0:SSD_H])
            mm.then_inc(cs_t, 1)
            pe.wait_ge(cs_tok, 1)
            pe.matmul(bank[4][:, 128:192], ident[:, P - 1:P].to_broadcast([P, P]),
                      cst[:, :, :].rearrange("p c h -> p (c h)"), start=True, stop=True).then_inc(cl_mm, 1)
            pe.wait_ge(x_tok, 10)
            for c in range(CH - 1):
                pe.wait_ge(st_w, c + 2)
                for g in range(2):
                    n = 2 * c + g
                    if n >= 2:
                        pe.wait_ge(st_done, n - 1)
                    pe.matmul(bank[g][:, :], btok[:, c, g, :], xdec[:, c % 2, 512 * g:512 * g + 512],
                              start=True, stop=True).then_inc(st_mm, 1)
            pe.wait_ge(got_con, CON3)
            pe.wait_ge(st_done, 6)
            pe.wait_ge(cb_done, 2)

            def sums(t):
                if t:
                    pe.wait_ge(cs_exp, 9 * t)
                for e in range(2):
                    pe.matmul(bank[e][:, :], sel[0:SSD_H, 2 * t + e, :], csf[0:SSD_H, :], start=True, stop=False)
                    pe.matmul(bank[e][:, :], identr[:, :], caut[:, :], start=False, stop=True)
                pe.matmul(bank[2][:, :], selp[0:SSD_H, t, :], csf[0:SSD_H, :], start=True, stop=True) \
                    .then_inc(cs_mm, 1)

            def outputs(t):
                pe.wait_ge(m_done, 2 * t + 2)
                pe.wait_ge(xp_done, 2 * t + 2)
                if t >= 2:
                    pe.wait_ge(y_out, t - 1)
                a, b = bank[4 + t % 2], bank[6 + t % 2]
                for c in range(CH):
                    cs = slice(P * c, P * c + P)
                    for e in range(2):
                        pe.matmul(a[:, cs], xpad[:, t % 2, e, c, :], mtt[:, e, cs], start=(e == 0), stop=(e == 1))
                for c in range(1, CH):
                    cs = slice(P * c, P * c + P)
                    mm = pe.matmul(b[:, cs], prevt[:, c - 1, P * t:P * t + P], xbc[:, 10 + t // 4, cs],
                                   start=True, stop=True)
                mm.then_inc(y_mm, 1)

            sums(0)
            for t in range(8):
                if t + 1 < 8:
                    sums(t + 1)
                outputs(t)

        @block.scalar
        def _(act):
            for t in range(10):
                act.wait_ge(x_t, t + 1)
                src = bank[5 + t % 3][:, :].rearrange("p (c n) -> p c n", c=CH)
                dst = xtok[:, :, P * t:P * t + P] if t < 8 else btok[:, :, t - 8, :]
                act.activation(dst, src, ACT.Copy).then_inc(x_tok, 1)
            act.wait_ge(st_w, 1)
            act.activation(dec[:, :, :], bank[4][:, 128:192].rearrange("p (c h) -> p c h", c=CH), ACT.Exp) \
                .then_inc(cl_exp, 1)
            ach(act, act.activation(wdec[:, :, :], wdec[:, :, :], ACT.Exp))
            act.sem_inc(cl_exp, 1)
            for t in range(8):
                act.wait_ge(cs_mm, t + 1)
                if t:
                    act.wait_ge(m_done, 2 * t)
                    act.wait_ge(y_out, t)
                for e in range(2):
                    for c in range(CH):
                        cs = slice(P * c, P * c + P)
                        act.activation(lm[:, e, cs], bank[e][:, cs], ACT.Exp,
                                       bias=ncst[:, c, 2 * t + e:2 * t + e + 1]).then_inc(cs_exp, 1)
                act.activation(eb[:, :], bank[2][:, :], ACT.Exp).then_inc(cs_exp, 1)

        @block.gpsimd
        def _(pool):
            pool.wait_ge(y_free_for_pad[0], y_free_for_pad[1])
            pool.memset(xpad[:, :, :, :, :], 0.0).then_inc(s3_pad, 1)
            pool.wait_ge(s3_pad, 1)
            pool.wait_ge(cs_tok, 1)
            pool.wait_ge(x_tok, 8)
            for t in range(8):
                if t >= 2:
                    pool.wait_ge(y_mm, t - 1)
                for e in range(2):
                    h = 2 * t + e
                    pool.tensor_tensor(xpad[:, t % 2, e, :, HD * e:HD * e + HD], xtok[:, :, HD * h:HD * h + HD],
                                       dtt[:, :, h:h + 1].to_broadcast([P, CH, HD]), ALU.mult).then_inc(xp_done, 1)

        @block.vector
        def _(dve):
            for g in range(2):
                dve.wait_ge(cb_mm, g + 1)
                dve.tensor_copy(cbt[:, g, :], bank[2 + g][:, :]).then_inc(cb_done, 1)
            dve.wait_ge(cs_t, 1)
            t4 = lambda a: bank[4][:, a:a + 64].rearrange("p (c h) -> p c h", c=CH)
            dve.tensor_copy(cst[:, :, :], t4(0))
            dve.tensor_copy(dtt[:, :, :], t4(64))
            dch(dve, dve.tensor_scalar(ncst[:, :, :], t4(0), -1.0, None, ALU.mult))
            dve.sem_inc(cs_tok, 1)
            dve.wait_ge(cl_mm, 1)
            dch(dve, dve.tensor_tensor(wdec[:, :, :], t4(128), ncst[:, :, :], ALU.add))
            dve.sem_inc(st_w, 1)
            dve.wait_ge(cl_exp, 2)
            dch(dve, dve.tensor_tensor(wdec[:, :, :], wdec[:, :, :], dtt[:, :, :], ALU.mult))
            dve.wait_ge(x_tok, 8)

            def weighted(c):
                if c >= 2:
                    dve.wait_ge(st_mm, 2 * (c - 1))
                hv = lambda a: a.rearrange("p (h d) -> p h d", d=HD)
                dve.tensor_tensor(hv(xdec[:, c % 2, :]), hv(xtok[:, c, :]),
                                  wdec[:, c, :].unsqueeze(2).to_broadcast([P, SSD_H, HD]), ALU.mult) \
                    .then_inc(st_w, 1)

            weighted(0)
            for c in range(CH - 1):
                if c + 1 < CH - 1:
                    weighted(c + 1)
                for g in range(2):
                    gs_ = slice(512 * g, 512 * g + 512)
                    dve.wait_ge(st_mm, 2 * c + g + 1)
                    if c:
                        hv = lambda a: a.rearrange("p (h d) -> p h d", d=HD)
                        dch(dve, dve.tensor_tensor(hv(prevt[:, c, gs_]), hv(prevt[:, c - 1, gs_]),
                                                   dec[:, c, 8 * g:8 * g + 8].unsqueeze(2).to_broadcast([P, 8, HD]),
                                                   ALU.mult))
                        dve.tensor_tensor(prevt[:, c, gs_], prevt[:, c, gs_], bank[g][:, :], ALU.add) \
                            .then_inc(st_done, 1)
                    else:
                        dve.tensor_copy(prevt[:, 0, gs_], bank[g][:, :]).then_inc(st_done, 1)
                dve.wait_ge(st_done, 2 * c + 2)
            dve.wait_ge(st_mm, 6)

            def masked(t):
                for e in range(2):
                    dve.wait_ge(cs_exp, 9 * t + 4 * e + 4)
                    if t:
                        dve.wait_ge(y_mm, t)
                    dve.tensor_tensor(mtt[:, e, :], lm[:, e, :], cbt[:, t // 4, :], ALU.mult).then_inc(m_done, 1)

            def combine(t):
                dve.wait_ge(y_mm, t + 1)
                dve.wait_ge(cs_exp, 9 * t + 9)
                a, b = bank[4 + t % 2], bank[6 + t % 2]
                if t:
                    dve.wait_ge(y_out, t)
                dve.tensor_tensor(yo[:, P:S], b[:, P:S], eb[:, P:S], ALU.mult)
                dch(dve, dve.scalar_tensor_tensor(out=xbc[:, t, :], in0=xbc[:, t, :], scalar=pcol("d_skip", t),
                                                  in1=a[:, :], op0=ALU.mult, op1=ALU.add))
                dve.tensor_tensor(xbc[:, t, P:S], xbc[:, t, P:S], yo[:, P:S], ALU.add).then_inc(y_out, 1)

            for t in range(8):
                masked(t)
                combine(t)

    bh, bl = ah, al
    sz = at("sz", SC_AT, [2, S])
    sqb = at("sqb", SC_AT + 4 * K, [2, S])
    ssb = at("ssb", SC_AT + 8 * K, [2, S])
    rtb = at("rtb", SC_AT + 12 * K, [2, TT])
    rrb = at("rrb", SC_AT + 12 * K + 64, [2, TT])
    hfb = at("hfb", SC_AT + 14 * K, [2, S])
    z_silu, z_prod, z_sq, z_add, z_sum, z_root, z_rec, z_spread, z_full, z_high, z_low = (
        sem(n_) for n_ in ("z_silu", "z_prod", "z_sq", "z_add", "z_sum", "z_root", "z_rec", "z_spread", "z_full",
                           "z_high", "z_low"))

    def ssd_gate_norm():
        n0, m0 = new_items(4), new_tiles(KT)
        mat = w["w_in_a_2"]

        @block.sync
        def _(sp):
            for j in range(4):
                load_item(sp, n0 + j, 0, full_item(n0 + j, mat, 0, OFF_Z + IC * j))

        @block.tensor
        def _(pe):
            pe.wait_ge(y_out, 8)
            for t in range(KT):
                if t % 2 == 0:
                    item_ready(pe, n0 + t // 2)
                if t >= 4:
                    pe.wait_ge(drained, m0 + t - 3)
                tile_of(pe, n0 + t // 2, t % 2, bank[t % 4][:, :], H).then_inc(tiles, 1)
            pe.wait_ge(z_add, KT)
            for g in range(2):
                for t in range(TT):
                    mm = pe.matmul(bank[4][:, TT * g + t:TT * g + t + 1], ssb[:, g, P * t:P * t + P], ones[:, 0:1],
                                   start=True, stop=True)
            mm.then_inc(z_sum, 1)
            pe.wait_ge(z_rec, 1)
            for g in range(2):
                spread(pe, bank[5 + g], lambda t: rrb[:, g, t:t + 1].to_broadcast([P, P])).then_inc(z_spread, 1)
            pe.wait_ge(z_low, KT)

        @block.scalar
        def _(act):
            act.wait_ge(y_out, 8)
            for t in range(KT):
                act.wait_ge(tiles, 2 * n0 + t + 1)
                if t >= 2:
                    act.wait_ge(z_prod, t - 1)
                act.activation(sz[:, t % 2, :], bank[t % 4][:, :], ACT.Silu).then_inc(z_silu, 1)
                if t % 2:
                    split_hi(act, n0 + 2 + t // 2)
                act.wait_ge(z_prod, t + 1)
                if t >= 2:
                    act.wait_ge(z_add, t - 1)
                act.activation(sqb[:, t % 2, :], xbc[:, t, :], ACT.Square).then_inc(z_sq, 1)
            act.wait_ge(z_sum, 1)
            act.activation(rtb[:, :, :], bank[4][:, 0:2 * TT].rearrange("p (g t) -> p g t", g=2), ACT.Sqrt,
                           bias=eps[:, 1:2], scale=2.0 / D).then_inc(z_root, 1)
            for k in range(KT):
                act.wait_ge(z_full, k + 1)
                act.activation(bh[:, k, :], hfb[:, k % 2, :], ACT.Copy).then_inc(z_high, 1)

        @block.vector
        def _(dve):
            def add(t):
                g = t // 4
                dve.wait_ge(z_sq, t + 1)
                if t % 4 == 0:
                    dve.tensor_copy(ssb[:, g, :], sqb[:, t % 2, :]).then_inc(z_add, 1)
                else:
                    dve.wait_ge(z_add, t)
                    dve.tensor_tensor(ssb[:, g, :], ssb[:, g, :], sqb[:, t % 2, :], ALU.add).then_inc(z_add, 1)

            for t in range(KT):
                dve.wait_ge(z_silu, t + 1)
                dve.sem_inc(drained, 1)
                dve.tensor_tensor(xbc[:, t, :], xbc[:, t, :], sz[:, t % 2, :], ALU.mult).then_inc(z_prod, 1)
                if t % 2:
                    split_lo(dve, n0 + 2 + t // 2)
                if t:
                    add(t - 1)
            add(KT - 1)
            dve.wait_ge(z_root, 1)
            dve.reciprocal(rrb[:, :, :], rtb[:, :, :]).then_inc(z_rec, 1)

            def low(k):
                dve.wait_ge(z_high, k + 1)
                dve.tensor_tensor(bl[:, k, :], hfb[:, k % 2, :], bh[:, k, :].bitcast(F32),
                                  ALU.subtract).then_inc(z_low, 1)

            for k in range(KT):
                dve.wait_ge(z_spread, k // 4 + 1)
                if k >= 2:
                    dve.wait_ge(z_low, k - 1)
                dve.scalar_tensor_tensor(out=hfb[:, k % 2, :], in0=xbc[:, k, :], scalar=pcol("ssd_norm", k),
                                         in1=bank[5 + k // 4][:, :], op0=ALU.mult, op1=ALU.mult).then_inc(z_full, 1)
                if k:
                    low(k - 1)
            low(KT - 1)

    q3 = at("q3", Y + 32 * K, [KT, S])
    kd3 = at("kd3", Y + 48 * K, [2, S])
    vp3 = at("vp3", Y + 52 * K, [TT, 320])
    pt3 = at("pt3", Y + 58 * K, [2, 7 * P])
    bv3 = at("bv3", Y + 66 * K, [P])
    dup3 = at("dup3", Y + 67 * K, [2, P])
    k3 = at("k3", Y + 68 * K, [S])
    dist3 = at("dist3", Y + 70 * K, [2 * P], F32R)
    dist3f = at("dist3f", Y + 71 * K, [2 * P])
    dg3 = at("dg3", Y + 72 * K, [2, 2, P], F32R)
    pr3 = at("pr3", Y + 74 * K, [2, TT, 2 * P])
    S4 = Y + 82 * K
    nm3 = at("nm3", S4, [2, TT])
    sm3 = at("sm3", S4 + 32, [2, TT])
    es3 = at("es3", S4 + 64, [2, TT])
    rs3 = at("rs3", S4 + 96, [2, TT])
    nsink = at("nsink", S4 + 128, [NH])
    k3_done, kd3_mm, kd3_done, v3_pad, c4_ready, ns_done = (
        sem(n_) for n_ in ("k3_done", "kd3_mm", "kd3_done", "v3_pad", "c4_ready", "ns_done"))
    dg3_done, s3_done, s3_max, p3_exp, p3_done, t3_done, t3_act, t3_dve, pv3_done, o3_out = (
        sem(n_) for n_ in ("dg3_done", "s3_done", "s3_max", "p3_exp", "p3_done", "t3_done", "t3_act", "t3_dve",
                           "pv3_done", "o3_out"))

    def window_kv():
        n0, m0 = new_items(1), new_tiles(2)

        @block.sync
        def _(sp):
            load_item(sp, n0, 0, full_item(n0, w["w_in_c_2"], 0, OFF_KV_C))
            sp.wait_ge(z_low, KT)
            sp.dma_start(bv3[:, :], bvc.to_broadcast([P, P])).then_inc(got_con, 16)
            sp.dma_start(dup3[:, :, :], con[:, CCOL["dup0"]:CCOL["dup0"] + 256].rearrange(
                "p (g n) -> p g n", g=2)).then_inc(got_con, 16)
            sp.dma_start(dist3f[:, :], con[:, CCOL["dist2"]:CCOL["dist2"] + 256]).then_inc(got_con, 16)

        @block.gpsimd
        def _(pool):
            pool.wait_ge(z_low, KT)
            pool.memset(vp3[:, :, :], 0.0).then_inc(v3_pad, 1)

        @block.tensor
        def _(pe):
            item_ready(pe, n0)
            pe.wait_ge(drained, m0)
            tile_of(pe, n0, 0, bank[0][:, :], H).then_inc(tiles, 1)
            for tt in range(TT):
                mm = rows_of(pe, n0, tt, bank[1][:, P * tt:P * tt + P], P, c0=P)
            mm.then_inc(tiles, 1)
            pe.wait_ge(got_con, CON4)
            pe.wait_ge(k3_done, 1)
            for g in range(2):
                pe.matmul(bank[4 + g][:, :], dup3[:, g, :], k3[:, :], start=True, stop=True).then_inc(kd3_mm, 1)

        @block.scalar
        def _(act):
            split_hi(act, n0 + 2)
            act.wait_ge(got_con, CON4)
            act.activation(dist3[:, :], dist3f[:, :], ACT.Copy).then_inc(c4_ready, 1)
            for g in range(2):
                act.wait_ge(kd3_mm, g + 1)
                act.activation(kd3[:, g, :], bank[4 + g][:, :], ACT.Copy).then_inc(kd3_done, 1)

        @block.vector
        def _(dve):
            dve.wait_ge(tiles, 2 * n0 + 1)
            dve.tensor_scalar(k3[:, :], bank[0][:, :], pcol("b_k"), None, ALU.add).then_inc(drained, 1)
            dve.wait_ge(drained, m0 + 1)
            dve.sem_inc(k3_done, 1)
            split_lo(dve, n0 + 2)
            dve.wait_ge(tiles, 2 * n0 + 2)
            dve.wait_ge(v3_pad, 1)
            dve.wait_ge(got_con, CON4)
            for tt in range(TT):
                dst = vp3[:, tt, HD:HD + 256].rearrange("p (g e) -> p g e", g=2)[:, :, 0:HD]
                ins = dve.tensor_tensor(dst, bank[1][:, P * tt:P * tt + P].rearrange("p (g d) -> p g d", g=2),
                                        bv3[:, :].rearrange("p (g d) -> p g d", g=2), ALU.add)
            ins.then_inc(drained, 1)
            dve.tensor_scalar(nsink[:, :], pcol("sinks", n=NH), -1.0, None, ALU.mult).then_inc(ns_done, 1)

    def window_attention(m1):
        sl = slopes(NH)

        def out_pair(act, hp):
            act.wait_ge(pv3_done, 2 * hp + 2)
            act.activation(q3[:, hp, :], bank[6 + hp % 2][:, :], ACT.Copy).then_inc(o3_out, 1)

        @block.tensor
        def _(pe):
            pe.wait_ge(c4_ready, 1)
            pe.wait_ge(kd3_done, 2)
            pe.wait_ge(drained, m1)

            def scores(h):
                e, hp, g = h % 2, h // 2, h // 8
                pe.wait_ge(dg3_done, h + 1)
                for i in range(TT):
                    lo = P if i == 0 else 0
                    if h >= 2:
                        pe.wait_ge(p3_exp, 5 * (h - 2) + i + 1)
                    out = bank[2 * (h % 2) + i // 2][:, 2 * P * (i % 2) + lo:2 * P * (i % 2) + 2 * P]
                    pe.matmul(out, q3[HD * e:HD * e + HD, hp, P * i:P * i + P],
                              kd3[HD * e:HD * e + HD, g, P * (i - 1) + lo:P * (i + 1)], start=True, stop=False)
                    pe.matmul(out, dg3[:, h % 2, 0, :], dist3[:, lo:2 * P], start=False, stop=False)
                    pe.matmul(out, dg3[:, h % 2, 1, :], dist3[:, lo:2 * P], start=False, stop=True).then_inc(s3_done, 1)

            def values(h):
                e, hp, g = h % 2, h // 2, h // 8
                pe.wait_ge(p3_done, 4 * h + 4)
                n = 0
                for i in range(TT):
                    if i % 2 == 0 and h:
                        pe.wait_ge(t3_dve if i else t3_act, h)
                    for j in ([0] if i == 0 else [i - 1, i]):
                        slot = n if n < 3 else n - 3
                        mm = pe.transpose(bank[4 + i // 2][:, P * slot:P * slot + P],
                                          pr3[:, h % 2, i, P * (j - i + 1):P * (j - i + 2)], ident[:, :])
                        n += 1
                    if i % 2:
                        mm.then_inc(t3_done, 1)
                pe.wait_ge(t3_act, h + 1)
                pe.wait_ge(t3_dve, h + 1)
                out = bank[6 + hp % 2]
                if e == 0 and hp >= 2:
                    pe.wait_ge(o3_out, hp - 1)
                c0 = HD + P * g if e == 0 else P * g
                for j in range(TT):
                    n = 2 * P if j < TT - 1 else P
                    mm = pe.matmul(out[:, P * j:P * j + n], vp3[:, j, c0:c0 + P],
                                   pt3[:, h % 2, 2 * P * j:2 * P * j + n], start=(e == 0 and j == 0),
                                   stop=(e == 1 and j == TT - 1), skip_group_check=True)
                mm.then_inc(pv3_done, 1)

            for h in range(NH + 1):
                if h < NH:
                    scores(h)
                if h:
                    values(h - 1)

        @block.scalar
        def _(act):
            def diag(h):
                if h >= 2:
                    act.wait_ge(s3_done, 4 * (h - 1))
                hi_ = high_part(sl[h])
                act.activation(dg3[:, h % 2, 0, :], ident[:, :], ACT.Copy, scale=hi_)
                act.activation(dg3[:, h % 2, 1, :], ident[:, :], ACT.Copy, scale=sl[h] - hi_).then_inc(dg3_done, 1)

            diag(0)
            for h in range(NH + 1):
                if h + 1 < NH:
                    diag(h + 1)
                if h < NH:
                    act.wait_ge(s3_max, h + 1)
                    if h >= 2:
                        act.wait_ge(t3_done, 2 * (h - 1))
                    for i in range(TT):
                        lo = P if i == 0 else 0
                        act.activation(pr3[:, h % 2, i, lo:2 * P],
                                       bank[2 * (h % 2) + i // 2][:, 2 * P * (i % 2) + lo:2 * P * (i % 2) + 2 * P],
                                       ACT.Exp, bias=nm3[:, h % 2, i:i + 1],
                                       accum_out=sm3[:, h % 2, i:i + 1]).then_inc(p3_exp, 1)
                    act.activation(es3[:, h % 2, :], nm3[:, h % 2, :], ACT.Exp,
                                   bias=pcol("sinks", h)).then_inc(p3_exp, 1)
                if h:
                    v = h - 1
                    act.wait_ge(t3_done, 2 * v + 1)
                    if v >= 2:
                        act.wait_ge(pv3_done, v - 1)
                    act.activation(pt3[:, v % 2, 0:3 * P], bank[4][:, 0:3 * P], ACT.Copy).then_inc(t3_act, 1)
                    if v % 2 == 0 and v >= 2:
                        out_pair(act, v // 2 - 1)
            out_pair(act, NH // 2 - 1)

        @block.vector
        def _(dve):
            dve.wait_ge(ns_done, 1)
            for h in range(NH + 1):
                if h:
                    v = h - 1
                    dve.wait_ge(p3_exp, 5 * v + 5)
                    if v:
                        dve.wait_ge(p3_done, 4 * v)
                    dch(dve, dve.tensor_tensor(sm3[:, v % 2, :], sm3[:, v % 2, :], es3[:, v % 2, :], ALU.add))
                    dch(dve, dve.reciprocal(rs3[:, v % 2, :], sm3[:, v % 2, :]))
                    for i in range(TT):
                        part = pr3[:, v % 2, i, (P if i == 0 else 0):2 * P]
                        dve.tensor_scalar(part, part, rs3[:, v % 2, i:i + 1], None, ALU.mult).then_inc(p3_done, 1)
                if h < NH:
                    if h >= 2:
                        dve.wait_ge(p3_exp, 5 * (h - 1))
                    b0, b1 = bank[2 * (h % 2)], bank[2 * (h % 2) + 1]
                    dve.wait_ge(s3_done, 4 * h + 2)
                    dve.tensor_reduce(nm3[:, h % 2, 0:1], b0[:, P:2 * P], AX, ALU.max, negate=True)
                    dve.tensor_reduce(nm3[:, h % 2, 1:2], b0[:, 2 * P:4 * P], AX, ALU.max, negate=True)
                    dve.wait_ge(s3_done, 4 * h + 4)
                    dch(dve, dve.tensor_reduce(nm3[:, h % 2, 2:4], b1[:, :].rearrange("p (i n) -> p i n", i=2), AX,
                                               ALU.max, negate=True))
                    dve.tensor_scalar(nm3[:, h % 2, :], nm3[:, h % 2, :], nsink[:, h:h + 1], None,
                                      ALU.min).then_inc(s3_max, 1)
                if h:
                    v = h - 1
                    dve.wait_ge(t3_done, 2 * v + 2)
                    if v >= 2:
                        dve.wait_ge(pv3_done, v - 1)
                    dve.tensor_copy(pt3[:, v % 2, 3 * P:7 * P], bank[5][:, :]).then_inc(t3_dve, 1)

    xw = at("xw", Y, [KT, S])
    orow = at("orow", Y + 16 * K, [TT, D])
    x_w, y_turned, y_row = sem("x_w"), sem("y_turned"), sem("y_row")

    def final_norm(m0):
        c = norms[0]

        @block.scalar
        def _(act):
            for k in range(KT):
                act.wait_ge(drained, m0 + k + 1)
                act.wait_ge(n_add, KT * c + k - 1)
                act.activation(sqn[:, k % 2, :], xt[:, k, :], ACT.Square).then_inc(n_sq, 1)
            act.wait_ge(n_sum, c + 1)
            act.activation(rtn[:, :], bank[4][:, 0:TT], ACT.Sqrt, bias=eps[:, 1:2], scale=1.0 / D).then_inc(n_root, 1)

        @block.gpsimd
        def _(pool):
            pool.wait_ge(tiles, 2 * TOTAL_ITEMS)
            for k in range(KT):
                pool.wait_ge(drained, m0 + k + 1)
                pool.tensor_scalar(xw[:, k, :], xt[:, k, :], pcol("final", k), 1.0, ALU.mult, ALU.mult) \
                    .then_inc(x_w, 1)

        @block.tensor
        def _(pe):
            pe.wait_ge(n_add, KT * c + KT)
            pe.wait_ge(drained, m0 + KT)
            for t in range(TT):
                mm = pe.matmul(bank[4][:, t:t + 1], ssn[:, P * t:P * t + P], ones[:, 0:1], start=True, stop=True)
            mm.then_inc(n_sum, 1)
            pe.wait_ge(x_w, KT)
            for t in range(TT):
                for half in range(2):
                    n = 2 * t + half
                    if n >= 4:
                        pe.wait_ge(y_row, n - 3)
                    for k in range(4):
                        mm = pe.transpose(bank[n % 4][:, P * k:P * k + P], xw[:, 4 * half + k, P * t:P * t + P],
                                          ident[:, :])
                    mm.then_inc(y_turned, 1)

        @block.vector
        def _(dve):
            dve.wait_ge(n_sq, KT * c + 1)
            dve.wait_ge(n_sum, c)
            dve.tensor_copy(ssn[:, :], sqn[:, 0, :]).then_inc(n_add, 1)
            for k in range(1, KT):
                dve.wait_ge(n_sq, KT * c + k + 1)
                dve.wait_ge(n_add, KT * c + k)
                dve.tensor_tensor(ssn[:, :], ssn[:, :], sqn[:, k % 2, :], ALU.add).then_inc(n_add, 1)
            dve.wait_ge(n_root, c + 1)
            dve.reciprocal(rrn[:, :], rtn[:, :]).then_inc(n_rec, 1)
            dve.wait_ge(n_rec, c + 1)
            for t in range(TT):
                for half in range(2):
                    n = 2 * t + half
                    dve.wait_ge(y_turned, n + 1)
                    dve.tensor_scalar(orow[:, t, 512 * half:512 * half + 512], bank[n % 4][:, :], rrn[:, t:t + 1],
                                      None, ALU.mult).then_inc(y_row, 1)

        @block.sync
        def _(sp):
            for t in range(TT):
                sp.wait_ge(y_row, 2 * t + 2)
                sp.dma_start(out[P * t:P * t + P, :], orow[:, t, :]).then_inc(stored, 16)
            sp.wait_ge(stored, 16 * TT)

    stored = sem("stored")

    mx = load_x()
    norm(mx, "attn_norm", 0)
    block1_kv()
    m1 = block1_q()
    block1_finish_qk(m1)
    block1_attention()
    block1_pool()
    count_before_merge = count["tile"]
    block1_merge()
    mx = residual(w["w_o"], (mh, ml))
    norm(mx, "ffn_norm", 0)
    ffn_up()
    mx = ffn_down()
    wa = w["w_in_a_2"]
    norm(mx, "norm_a", 1)
    project(wa, 0, q2, SCALE)
    project(wa, OFF_K2, k2)
    m1 = diff_values() + KT
    ready = diff_attention(m1)
    mx = residual(w["w_out_a_2"], (ah, al), ready=ready)
    y_free_for_pad = (tiles, 2 * count["item"])
    ssd_core(ssd_inputs())
    ssd_gate_norm()
    mx = residual(w["w_out_a_2"], (bh, bl), r0=D)
    norm(mx, "norm_c", 1)
    window_kv()
    m1 = project(w["w_in_c_2"], 0, q3, SCALE, bias="b_q") + KT
    window_attention(m1)
    gate_and_split(w["w_in_c_2"], OFF_G_C, q3, (ah, al), bias="b_g", wait=(o3_out, NH // 2))
    mx = residual(w["w_out_c_2"], (ah, al), last=True)
    final_norm(mx)
    assert count["item"] == TOTAL_ITEMS, count
    ctx.close()


def kernel(**inputs):
    import concourse.bacc as _bacc
    from concourse.bass_utils import run_bass_kernel_spmd as _run

    nc = _bacc.Bacc("TRN2", target_bir_lowering=False, num_devices=1)
    arrays = {"x": np.asarray(inputs["x"])[0], "par": pack_params(inputs), "con": make_consts(),
              "bvc": np.asarray(inputs["b_in_c_2"])[:, OFF_KV_C + P:OFF_G_C]}
    for name in WEIGHTS:
        arrays[name] = np.asarray(inputs[name])[0]
    arrays = {f"in_{name}_dram": np.ascontiguousarray(a) for name, a in arrays.items()}
    aps = [nc.dram_tensor(name, a.shape, mybir.dt.from_np(a.dtype), kind="ExternalInput").ap()
           for name, a in arrays.items()]
    out = nc.dram_tensor("out_0_dram", (S, D), F32, kind="ExternalOutput").ap()
    two_blocks(nc, *aps[:4], dict(zip(WEIGHTS, aps[4:])), out)
    r = _run(nc, [arrays], core_ids=[0])
    return r.results[0]["out_0_dram"].reshape(1, S, D)
```

```python
from contextlib import ExitStack

import numpy as np

import concourse.bass as bass
from concourse import mybir

F32 = mybir.dt.float32
F32R = mybir.dt.float32r
ACT = mybir.ActivationFunctionType
ALU = mybir.AluOpType
AX = mybir.AxisListType.X

P = 128
S = 512
D = 1024
TT = S // P
KT = D // P
IC = 256
NEG = -1e30

POOL_W = 512
POOL_WINDOWS = (2, 4, 8, 16)
HD = 64
NH = 16
OFF_Q = POOL_W
OFF_KV = OFF_Q + NH * HD
OFF_G = OFF_KV + 3 * 2 * 2 * HD
OFF_MG = OFF_G + 3 * NH
DFF = 2752
FT = DFF // P
FREST = DFF - FT * P
CMP_BLOCK, CMP_STRIDE = 32, 16
NCMP = (S - CMP_BLOCK) // CMP_STRIDE + 1
EPS1, EPS2 = 1e-6, 1e-5
SCALE = HD ** -0.5
DA_H = 8
OFF_K2, OFF_V2, OFF_GA, OFF_Z, OFF_XBC, OFF_DT = 1024, 2048, 3072, 4096, 5120, 6656
SSD_H = 16
CH = S // P
LAMBDA_INIT = 0.8 - 0.6 * float(np.exp(-0.3 * 0))
WIN2 = 128
OFF_KV_C, OFF_G_C = 1024, 1280


def slopes(n):
    return [float(np.float32(2.0 ** (-8.0 * (i + 1) / n))) for i in range(n)]


def high_part(v):
    m, e = np.frexp(np.float64(v))
    return float(np.ldexp(np.round(m * 4096) / 4096, e))


PARAMS = [("attn_norm", 8), ("ffn_norm", 8), ("q_norm", 1), ("k_norm", 3), ("pool_scale", 4), ("cmp_b1", 2),
          ("pos", 64), ("convw_g", 66), ("convw_v", 66), ("convb_g", 22), ("convb_v", 22),
          ("norm_a", 8), ("conv_a", 48), ("convb_a", 12), ("dt_bias", 1), ("a_log", 1), ("d_skip", 8),
          ("ssd_norm", 8), ("lam", 4), ("subln", 1), ("norm_c", 8), ("b_q", 8), ("b_k", 1), ("b_g", 8),
          ("sinks", 16), ("final", 8)]
PCOL, _o = {}, 0
for _n, _c in PARAMS:
    PCOL[_n] = _o
    _o += _c
NPAR = _o


def pack_params(a):
    f = np.float32

    def tiles(v, n=None):
        v = np.asarray(v).reshape(-1)
        n = n or -(-v.size // P)
        out = np.zeros(n * P, f)
        out[:v.size] = v
        return out.reshape(n, P).T

    def rows(v):
        out = np.zeros((P, v.shape[1]), f)
        out[:v.shape[0]] = v
        return out

    def twice(v):
        return np.concatenate([v, v], axis=0)

    cw, cb = a["conv_w"][0], a["conv_b"][0]
    b_in = a["b_in_c_2"][0]
    got = {
        "attn_norm": tiles(a["attn_norm_w"]), "ffn_norm": tiles(a["ffn_norm_w"]),
        "q_norm": twice(a["q_norm_w"][0][:, None]),
        "k_norm": twice(a["k_norm_w"][0].T), "pool_scale": tiles(a["pool_scale"]),
        "cmp_b1": a["cmp_b1"][0].T,
        "pos": twice(np.concatenate([a["cmp_pos"][0, 0].T, a["cmp_pos"][0, 1].T], axis=1)),
        "convw_g": np.concatenate([tiles(cw[t, :DFF]) for t in range(3)], axis=1),
        "convw_v": np.concatenate([tiles(cw[t, DFF:]) for t in range(3)], axis=1),
        "convb_g": tiles(cb[:DFF]), "convb_v": tiles(cb[DFF:]),
        "norm_a": tiles(a["norm_a_2"]),
        "conv_a": np.concatenate([tiles(a["conv_w_a_2"][0, t]) for t in range(4)], axis=1),
        "convb_a": tiles(a["conv_b_a_2"]),
        "dt_bias": rows(a["dt_bias_a_2"].T), "a_log": rows(a["a_log_a_2"].T),
        "d_skip": tiles(np.repeat(a["d_skip_a_2"][0], HD)),
        "ssd_norm": tiles(a["ssd_norm_a_2"]),
        "lam": rows(np.stack([a["lambda_q1_a_2"][0], a["lambda_k1_a_2"][0],
                              a["lambda_q2_a_2"][0], a["lambda_k2_a_2"][0]], axis=1)),
        "subln": tiles(a["subln_a_2"]), "norm_c": tiles(a["norm_c_2"]),
        "b_q": tiles(b_in[:1024]), "b_k": tiles(b_in[1024:1152]), "b_g": tiles(b_in[OFF_G_C:]),
        "sinks": np.tile(a["sinks_c_2"][0][None, :], (P, 1)),
        "final": tiles(a["final_norm_2"]),
    }
    return np.ascontiguousarray(np.concatenate([got[n] for n, _ in PARAMS], axis=1), dtype=f)


CONSTS = [("ident", 128), ("ones", 128), ("eps1", 1), ("eps2", 1), ("halves", 2), ("maskc", 4 * NCMP), ("keepc", 4 * NCMP),
          ("cos", 512), ("sin", 512), ("perm", 128), ("blk", 128), ("dup0", 128), ("dup1", 128),
          ("causal", 128), ("rcnt", 4 * 16), ("causal_t", 512), ("sel", SSD_H * 128), ("selp", 8 * 128),
          ("dist", 512), ("dist2", 256)]
CCOL, _o = {}, 0
for _n, _c in CONSTS:
    CCOL[_n] = _o
    _o += _c
NCON = _o


def make_consts():
    f = np.float32
    i = np.arange(P)
    freqs = (f(10000.0) ** (-np.arange(32, dtype=f) / f(32))).astype(f)
    ang = (np.arange(S, dtype=f)[:, None] * freqs[None, :]).astype(f)
    cos = np.cos(ang.astype(np.float64)).T
    sin = np.sin(ang.astype(np.float64)).T
    perm = np.zeros((P, P), f)
    for j in range(P):
        perm[j ^ 32, j] = 1.0
    dup = []
    for g in range(2):
        m = np.zeros((P, P), f)
        for j in range(P):
            m[64 * g + j % 64, j] = 1.0
        dup.append(m)
    t = np.arange(S).reshape(TT, P).T
    end = np.arange(NCMP) * CMP_STRIDE + CMP_BLOCK - 1
    ok = end[None, None, :] <= t[:, :, None]
    rc = np.zeros((P, 4, 16), f)
    for g, w in enumerate(POOL_WINDOWS):
        rc[:, g, :] = 1.0 / np.minimum(np.arange(16) + 1, w)
    sel = np.zeros((P, SSD_H, P), f)
    selp = np.zeros((P, 8, P), f)
    for h in range(SSD_H):
        sel[h, h, :] = 1.0
        selp[h, h // 2, 64 * (h % 2):64 * (h % 2) + 64] = 1.0
    c = np.arange(512)
    rel = (c[None, :] - 384) - i[:, None]
    c2 = np.arange(256)
    rel2 = (c2[None, :] - 128) - i[:, None]
    got = {
        "ident": np.eye(P), "ones": np.ones((P, P)), "eps1": np.full((P, 1), EPS1), "eps2": np.full((P, 1), EPS2),
        "halves": (i[:, None] // 64 == np.arange(2)[None, :]).astype(f),
        "maskc": np.where(ok, 0.0, NEG).reshape(P, -1), "keepc": ok.reshape(P, -1).astype(f),
        "cos": np.concatenate([cos] * 4), "sin": np.concatenate([-sin, sin] * 2),
        "perm": perm, "blk": (i[:, None] // 64 == i[None, :] // 64).astype(f),
        "dup0": dup[0], "dup1": dup[1],
        "causal": np.where(i[None, :] <= i[:, None], 0.0, NEG),
        "rcnt": rc.reshape(P, -1),
        "causal_t": np.tile(np.where(i[None, :] >= i[:, None], 0.0, NEG), (1, 4)),
        "sel": sel.reshape(P, -1), "selp": selp.reshape(P, -1),
        "dist": np.where(rel <= 0, rel, NEG), "dist2": np.where((rel2 <= 0) & (rel2 > -WIN2), rel2, NEG),
    }
    return np.ascontiguousarray(np.concatenate([got[n] for n, _ in CONSTS], axis=1), dtype=f)


WEIGHTS = ["w_in", "pool_w", "cmp_w1", "cmp_w2", "w_pool_br", "w_attn_br", "w_o", "w_up", "w_down",
           "w_in_a_2", "w_out_a_2", "w_in_c_2", "w_out_c_2"]


AHEAD = 2
TOTAL_ITEMS = 112


def two_blocks(nc, x, par, con, bvc, w, out):
    ctx = ExitStack()
    K = 1024
    base = nc.sbuf_base
    base += -base % 64
    room = nc.sbuf_usable_end - base

    def at(name, offset, shape, dt=F32):
        size = 4 * int(np.prod(shape))
        assert offset + size <= room, (name, offset + size, room)
        return nc.alloc_sbuf_tensor_at(name, [P] + list(shape), dt, offset=base + offset)

    def sem(name):
        return ctx.enter_context(nc.semaphore(name))

    W_RAW, W_HI, W_LO, X_AT, H_HI, H_LO, Y, PAR_AT, CON_AT = (0, 16 * K, 32 * K, 48 * K, 64 * K, 80 * K, 96 * K,
                                                            184 * K, 186 * K)
    SC_AT = CON_AT + 1600
    SC_AT += -SC_AT % 64
    wraw = at("wraw", W_RAW, [2, KT, IC])
    whi = at("whi", W_HI, [2, KT, IC], F32R)
    wlo = at("wlo", W_LO, [2, KT, IC], F32R)
    xt = at("xt", X_AT, [KT, S])
    hh = at("hh", H_HI, [KT, S], F32R)
    hl = at("hl", H_LO, [KT, S], F32R)
    parm = at("parm", PAR_AT, [NPAR])
    ident = at("ident", CON_AT, [128])
    ones = at("ones", CON_AT + 512, [128])
    identr = at("identr", CON_AT + 1024, [128], F32R)
    eps = at("eps", CON_AT + 1536, [2])
    halves = at("halves", CON_AT + 1568, [2])

    causf = at("causf", Y + 80 * K, [128])

    def pcol(name, t=0, rows=P, n=1):
        return parm[0:rows, PCOL[name] + t:PCOL[name] + t + n]

    def pcol_at(name, t, rows=P):
        return parm[0:rows, bass.ds(PCOL[name] + t, 1)]

    bank = [ctx.enter_context(nc.psum_tensor(f"bank{i}", [P, S], F32)) for i in range(8)]

    block = ctx.enter_context(nc.Block())

    w_landed = [sem("w_landed0"), sem("w_landed1")]
    w_hi_done = sem("w_hi_done")
    w_lo_done = sem("w_lo_done")
    tiles = sem("tiles")
    drained = sem("drained")
    count = {"item": 0, "tile": 0}

    def new_items(n):
        n0 = count["item"]
        count["item"] += n
        return n0

    def new_tiles(n):
        m0 = count["tile"]
        count["tile"] += n
        return m0

    def load_item(sp, b, i, pairs):
        assert len(pairs) == 2
        if b >= 2:
            sp.wait_ge(w_lo_done, b - 1 + 2 * i)
            sp.sem_inc(w_free, 1)
        for dst, src in pairs:
            sp.dma_start(dst, src).then_inc(w_landed[b % 2], 16)

    def full_item(b, mat, r0, c0):
        v = mat[r0:r0 + D, :].rearrange("(k p) n -> p k n", p=P)
        s = wraw[:, b % 2]
        return [(s[:, 0:4, :], v[:, 0:4, bass.ds(c0, IC)]), (s[:, 4:8, :], v[:, 4:8, bass.ds(c0, IC)])]

    def split_hi(act, b, i=0):
        if isinstance(i, int) and b + 2 * i >= TOTAL_ITEMS:
            return
        p = b % 2
        act.wait_ge(w_landed[p], 32 * (b // 2 + 1) + 32 * i)
        if b >= 2:
            act.wait_ge(tiles, 2 * (b - 1) + 4 * i)
        act.activation(whi[:, p], wraw[:, p], ACT.Copy).then_inc(w_hi_done, 1)

    def split_lo(dve, b, i=0):
        if isinstance(i, int) and b + 2 * i >= TOTAL_ITEMS:
            return
        p = b % 2
        dve.wait_ge(w_hi_done, b + 1 + 2 * i)
        dve.tensor_tensor(wlo[:, p], wraw[:, p], whi[:, p].bitcast(F32), ALU.subtract).then_inc(w_lo_done, 1)

    def item_ready(pe, b, i=0):
        pe.wait_ge(w_lo_done, b + 1 + 2 * i)

    def passes(pe, out, ws, hs, first, last):
        pe.matmul(out, ws[0], hs[0], start=first, stop=False)
        pe.matmul(out, ws[0], hs[1], start=False, stop=False)
        return pe.matmul(out, ws[1], hs[0], start=False, stop=last)

    def tile_of(pe, b, t, out, rhs, kts=KT, k0=0, w0=0, cols=P, c0=None, first=True, last=True, ready=None):
        p = b % 2
        c0 = P * t if c0 is None else c0
        for k in range(kts):
            if ready:
                pe.wait_ge(ready[0], ready[1] + k + 1)
            mm = passes(pe, out, (whi[:, p, w0 + k, c0:c0 + cols], wlo[:, p, w0 + k, c0:c0 + cols]),
                        (rhs[0][:, k0 + k, :], rhs[1][:, k0 + k, :]), first and k == 0, last and k == kts - 1)
        return mm

    def rows_of(pe, b, tt, out, cols, c0=0):
        p = b % 2
        for k in range(KT):
            mm = passes(pe, out, (hh[:, k, P * tt:P * tt + P], hl[:, k, P * tt:P * tt + P]),
                        (whi[:, p, k, c0:c0 + cols], wlo[:, p, k, c0:c0 + cols]), k == 0, k == KT - 1)
        return mm

    class Chain:

        def __init__(self, name):
            self.sem, self.n, self.off = sem(name), 0, 0

        def __call__(self, eng, ins):
            ins.then_inc(self.sem, 1)
            self.n += 1
            eng.wait_ge(self.sem, self.n + self.off)

        def loop(self, i, per, times):
            self.n0, self.off, self.per, self.times = self.n, per * i, per, times

        def done(self):
            assert self.n - self.n0 == self.per, (self.n - self.n0, self.per)
            self.n, self.off = self.n0 + self.per * self.times, 0

    dch = Chain("dve_own")
    ach = Chain("act_own")

    xr = at("xr", Y, [TT, D])
    CON1 = 16 * 6
    CON_K, CON_P = CON1 + 16 * 13, CON1 + 16 * 16
    CON2, CON3, CON4 = CON_P + 16, CON_P + 16 * 4, CON_P + 16 * 7
    w_free = sem("w_free")
    got_x, got_con, con_ready = sem("got_x"), sem("got_con"), sem("con_ready")
    x_turned = sem("x_turned")

    def load_x():
        n0 = 0

        @block.sync
        def _(sp):
            v = x.rearrange("(t p) n -> p t n", p=P)
            for t in range(TT):
                sp.dma_start(xr[:, t, :], v[:, t, :]).then_inc(got_x, 16)

        @block.scalar
        def _(act):
            act.dma_start(parm[:, :], par).then_inc(got_con, 16)
            act.dma_start(ident[:, :], con[:, CCOL["ident"]:CCOL["ident"] + 128]).then_inc(got_con, 16)
            act.dma_start(ones[:, :], con[:, CCOL["ones"]:CCOL["ones"] + 128]).then_inc(got_con, 16)
            act.dma_start(eps[:, :], con[:, CCOL["eps1"]:CCOL["eps1"] + 2]).then_inc(got_con, 16)
            act.dma_start(halves[:, :], con[:, CCOL["halves"]:CCOL["halves"] + 2]).then_inc(got_con, 16)
            act.dma_start(causf[:, :], con[:, CCOL["causal"]:CCOL["causal"] + 128]).then_inc(got_con, 16)
            for early in (g_sig, b_silu):
                act.sem_inc(early, AHEAD)
            act.wait_ge(got_con, CON1)
            act.activation(identr[:, :], ident[:, :], ACT.Copy).then_inc(con_ready, 1)
            split_hi(act, 0)
            split_hi(act, 1)

        @block.tensor
        def _(pe):
            pe.wait_ge(got_con, CON1)
            pe.wait_ge(got_x, 16 * TT)
            pe.wait_ge(con_ready, 1)
            for k in range(KT):
                if k >= 4:
                    pe.wait_ge(drained, k - 3)
                for t in range(TT):
                    mm = pe.transpose(bank[k % 4][:, P * t:P * t + P], xr[:, t, P * k:P * k + P], ident[:, :])
                mm.then_inc(x_turned, 1)

        @block.vector
        def _(dve):
            for early in (g_pool, g_full, g_low, f_act, f_low, e_prod, e_low):
                dve.sem_inc(early, AHEAD)
            for k in range(KT):
                dve.wait_ge(x_turned, k + 1)
                dve.tensor_copy(xt[:, k, :], bank[k % 4][:, :]).then_inc(drained, 1)

        return new_tiles(KT)

    sqn = at("sqn", SC_AT, [2, S])
    ssn = at("ssn", SC_AT + 4 * K, [S])
    rtn = at("rtn", SC_AT + 6 * K, [TT])
    rrn = at("rrn", SC_AT + 6 * K + 64, [TT])
    hfn = at("hfn", SC_AT + 7 * K, [2, S])
    n_sq, n_add, n_sum, n_root, n_rec = sem("n_sq"), sem("n_add"), sem("n_sum"), sem("n_root"), sem("n_rec")
    n_spread, n_full, n_high, n_low = sem("n_spread"), sem("n_full"), sem("n_high"), sem("n_low")
    norms = [0]

    def norm(m0, weight, eps_col, late=None):
        c = norms[0]
        norms[0] += 1

        def norm_low(dve, c, k):
            dve.wait_ge(n_high, KT * c + k + 1)
            dve.tensor_tensor(hl[:, k, :], hfn[:, k % 2, :], hh[:, k, :].bitcast(F32),
                              ALU.subtract).then_inc(n_low, 1)

        @block.scalar
        def _(act):
            for k in range(KT):
                act.wait_ge(drained, m0 + k + 1)
                if k >= 2 or c:
                    act.wait_ge(n_add, KT * c + k - 1)
                act.activation(sqn[:, k % 2, :], xt[:, k, :], ACT.Square).then_inc(n_sq, 1)
            act.wait_ge(n_sum, c + 1)
            act.activation(rtn[:, :], bank[4][:, 0:TT], ACT.Sqrt, bias=eps[:, eps_col:eps_col + 1],
                           scale=1.0 / D).then_inc(n_root, 1)
            if late:
                split_hi(act, late)
            for k in range(KT):
                act.wait_ge(n_full, KT * c + k + 1)
                act.activation(hh[:, k, :], hfn[:, k % 2, :], ACT.Copy).then_inc(n_high, 1)

        @block.vector
        def _(dve):
            dve.wait_ge(n_sq, KT * c + 1)
            if c:
                dve.wait_ge(n_sum, c)
            dve.tensor_copy(ssn[:, :], sqn[:, 0, :]).then_inc(n_add, 1)
            for k in range(1, KT):
                dve.wait_ge(n_sq, KT * c + k + 1)
                dve.wait_ge(n_add, KT * c + k)
                dve.tensor_tensor(ssn[:, :], ssn[:, :], sqn[:, k % 2, :], ALU.add).then_inc(n_add, 1)
            dve.wait_ge(n_root, c + 1)
            dve.reciprocal(rrn[:, :], rtn[:, :]).then_inc(n_rec, 1)
            if late:
                split_lo(dve, late)
            if c == 0:
                split_lo(dve, 0)
                split_lo(dve, 1)
            dve.wait_ge(n_spread, c + 1)
            for k in range(KT):
                if k >= 2:
                    dve.wait_ge(n_low, KT * c + k - 1)
                dve.scalar_tensor_tensor(out=hfn[:, k % 2, :], in0=xt[:, k, :], scalar=pcol(weight, k),
                                         in1=bank[5][:, :], op0=ALU.mult, op1=ALU.mult).then_inc(n_full, 1)
                if k >= 1:
                    norm_low(dve, c, k - 1)
            norm_low(dve, c, KT - 1)

        @block.tensor
        def _(pe):
            pe.wait_ge(n_add, KT * c + KT)
            pe.wait_ge(drained, m0 + KT)
            for t in range(TT):
                mm = pe.matmul(bank[4][:, t:t + 1], ssn[:, P * t:P * t + P], ones[:, 0:1], start=True, stop=True)
            mm.then_inc(n_sum, 1)
            pe.wait_ge(n_rec, c + 1)
            spread(pe, bank[5], lambda t: rrn[:, t:t + 1].to_broadcast([P, P])).then_inc(n_spread, 1)

        return (n_low, KT * c)

    def spread(pe, out, col):
        for t in range(TT):
            mm = pe.matmul(out[:, P * t:P * t + P], col(t), ident[:, :], start=True, stop=True)
        return mm

    H = (hh, hl)

    cosr = at("cosr", Y + 66 * K, [S])
    sinr = at("sinr", Y + 68 * K, [S])
    perm = at("perm", Y + 70 * K, [128])
    dup = at("dup", Y + 71 * K, [2, 128])
    kr = at("kr", Y + 72 * K, [3, S])
    vcz = at("vcz", Y + 78 * K, [S])
    qt = at("qt", Y + 32 * K, [KT, S])
    kdh = at("kdh", Y + 48 * K, [2, 2, S], F32R)
    kdl = at("kdl", Y + 16 * K, [2, 2, S], F32R)
    qs = at("qs", Y + 24 * K, [2, 2, S], F32R)
    vp = at("vp", Y + 56 * K, [TT, 2, 320])
    pt = at("pt", Y + 66 * K, [2, TT, S])
    gt = at("gt", Y + 82 * K, [TT, 3 * NH])
    kc = at("kc", Y + 83 * K, [2, NCMP])
    mc = at("mc", Y + 83 * K + 256, [TT, NCMP])
    keep = at("keep", Y + 83 * K + 768, [TT, NCMP])
    SM = Y + 84 * K + 512
    rtq = at("rtq", SM, [TT, 22])
    rq = at("rq", SM + 352, [TT, 22])
    cmx = at("cmx", SM + 704, [TT, NH])
    csm = at("csm", SM + 960, [TT, NH])
    crs = at("crs", SM + 1216, [TT, NH])
    nm = at("nm", SM + 1472, [2, TT])
    sm = at("sm", SM + 1504, [2, TT])
    rs = at("rs", SM + 1536, [2, TT])
    gel = at("gel", SM + 1600, [2, 2, NCMP])
    w2d = at("w2d", SM + 2112, [128])
    w2v = at("w2v", SM + 2624, [64])
    caus = at("caus", SM + 2880, [128], F32R)
    w1 = at("w1", Y, [2, 32, 128])
    hs = at("hs", Y + 66 * K, [2 * P])
    oh = at("oh", Y + 32 * K, [KT, S], F32R)
    ol = at("ol", Y, [KT, S], F32R)
    kw = at("kw", SC_AT, [2, S])
    sq = at("sq", SC_AT + 4 * K, [2, S])
    ta = at("ta", SC_AT + 8 * K, [S])
    tb = at("tb", SC_AT + 10 * K, [S])
    rwide = at("rwide", SC_AT, [2, TT, P])
    f_wide = sem("f_wide")
    win = at("win", SC_AT + 4 * K, [2, 32, 2 * NCMP])
    sc = at("sc", SC_AT + 8 * K, [TT, NH, 32])
    pct = at("pct", SC_AT, [4, S])
    pr = at("pr", SC_AT + 8 * K, [2, 1280])
    vc = at("vc", SC_AT + 18 * K, [2, 2, 128])
    r_z, r_mm, r_done = sem("r_z"), sem("r_mm"), sem("r_done")

    def rope_in(act, r, src, weight):
        n, p = r
        if not (isinstance(n, int) and n < 2):
            act.wait_ge(r_done, n - 1)
        act.activation(kw[:, p, :], src, ACT.Copy, scale=weight)
        act.activation(sq[:, p, :], src, ACT.Square).then_inc(r_z, 1)

    def rope_mm(pe, r):
        n, p = r
        pe.wait_ge(r_z, n + 1)
        if not (isinstance(n, int) and n < 2):
            pe.wait_ge(r_done, n - 1)
        for t in range(TT):
            out = bank[6][:, 44 * t + 2 * n:44 * t + 2 * n + 2] if isinstance(n, int) else \
                bank[6][:, bass.ds(44 * t + 2 * n, 2)]
            pe.matmul(out, sq[:, p, P * t:P * t + P], halves[:, :], start=True, stop=True)
        pe.matmul(bank[4 + p][:, :], perm[:, :], kw[:, p, :], start=True, stop=True).then_inc(r_mm, 1)

    def rope_out(dve, r, dst):
        n, p = r
        dve.wait_ge(r_mm, n + 1)
        if not (isinstance(n, int) and n < 1):
            dve.wait_ge(r_done, n)
        dve.tensor_tensor(ta[:, :], kw[:, p, :], cosr[:, :], ALU.mult)
        dch(dve, dve.tensor_tensor(tb[:, :], bank[4 + p][:, :], sinr[:, :], ALU.mult))
        dve.tensor_tensor(dst, ta[:, :], tb[:, :], ALU.add).then_inc(r_done, 1)

    vcz_ready, gates_ready = sem("vcz_ready"), sem("gates_ready")
    pads_ready = sem("pads_ready")

    def block1_kv(ready):
        n0, m0 = new_items(4), new_tiles(7)
        w_in = w["w_in"]
        v = w_in.rearrange("(k p) n -> p k n", p=P)

        @block.sync
        def _(sp):
            load_item(sp, n0, 0, full_item(n0, w_in, 0, OFF_KV))
            for b, (c0, c1) in ((n0 + 1, (256, 512)), (n0 + 2, (384, 640))):
                s = wraw[:, b % 2]
                load_item(sp, b, 0, [(s[:, :, 0:P], v[:, :, OFF_KV + c0:OFF_KV + c0 + P]),
                                     (s[:, :, P:IC], v[:, :, OFF_KV + c1:OFF_KV + c1 + P])])
            b = n0 + 3
            s = wraw[:, b % 2]
            g = 3 * NH
            load_item(sp, b, 0, [(s[:, 0:4, 0:g], v[:, 0:4, OFF_G:OFF_G + g]),
                                 (s[:, 4:8, 0:g], v[:, 4:8, OFF_G:OFF_G + g])])
            sp.wait_ge(x_turned, KT)
            for dst, name in ((cosr, "cos"), (sinr, "sin"), (perm, "perm")):
                n = dst.shape[1]
                sp.dma_start(dst[:, :], con[:, CCOL[name]:CCOL[name] + n]).then_inc(got_con, 16)
            sp.dma_start(dup[:, :, :], con[:, CCOL["dup0"]:CCOL["dup0"] + 256].rearrange(
                "p (g n) -> p g n", g=2)).then_inc(got_con, 16)
            for dst, name in ((mc, "maskc"), (keep, "keepc")):
                sp.dma_start(dst[:, :, :], con[:, CCOL[name]:CCOL[name] + TT * NCMP].rearrange(
                    "p (t n) -> p t n", t=TT)).then_inc(got_con, 16)
            w1v = w["cmp_w1"].rearrange("a (l d) h -> d a l h", d=HD)
            for half in range(2):
                for a in range(2):
                    sp.dma_start(w1[HD * half:HD * half + HD, a], w1v[:, a]).then_inc(got_con, 16)
                sp.dma_start(w2d[:, HD * half:HD * half + HD], w["cmp_w2"][0]).then_inc(got_con, 16)
            sp.dma_start(w2v[:, :], w["cmp_w2"][1]).then_inc(got_con, 16)

        @block.gpsimd
        def _(pool):
            pool.wait_ge(x_turned, KT)
            pool.memset(vp[:, :, :, :], 0.0).then_inc(pads_ready, 1)

        @block.tensor
        def _(pe):
            item_ready(pe, n0)
            tile_of(pe, n0, 0, bank[0][:, :], H, ready=ready).then_inc(tiles, 1)
            tile_of(pe, n0, 1, bank[1][:, :], H).then_inc(tiles, 1)
            item_ready(pe, n0 + 1)
            tile_of(pe, n0 + 1, 0, bank[2][:, :], H).then_inc(tiles, 1)
            pe.wait_ge(got_con, CON_K)
            rope_mm(pe, (0, 0))
            tile_of(pe, n0 + 1, 1, bank[3][:, :], H).then_inc(tiles, 1)
            rope_mm(pe, (1, 1))
            item_ready(pe, n0 + 2)
            for half in range(2):
                pe.wait_ge(drained, m0 + 1 + half)
                for j in range(2):
                    mm = rows_of(pe, n0 + 2, 2 * half + j, bank[half][:, IC * j:IC * j + IC], IC)
                mm.then_inc(tiles, 1)
            rope_mm(pe, (2, 0))
            item_ready(pe, n0 + 3)
            g = 3 * NH
            pe.wait_ge(drained, m0 + 3)
            for half in range(2):
                for j in range(2):
                    tt = 2 * half + j
                    mm = rows_of(pe, n0 + 3, tt, bank[2][:, g * tt:g * tt + g], g)
                mm.then_inc(tiles, 1)

        @block.scalar
        def _(act):
            act.wait_ge(tiles, 2 * n0 + 1)
            rope_in(act, (0, 0), bank[0][:, :], pcol("k_norm", 0))
            act.wait_ge(tiles, 2 * n0 + 2)
            act.wait_ge(x_turned, KT)
            act.activation(vcz[:, :], bank[1][:, :], ACT.Copy).then_inc(vcz_ready, 1)
            split_hi(act, n0 + 2)
            act.wait_ge(tiles, 2 * n0 + 3)
            rope_in(act, (1, 1), bank[2][:, :], pcol("k_norm", 1))
            act.wait_ge(tiles, 2 * n0 + 4)
            rope_in(act, (2, 0), bank[3][:, :], pcol("k_norm", 2))
            split_hi(act, n0 + 3)
            split_hi(act, n0 + 4)
            act.wait_ge(tiles, 2 * n0 + 8)
            act.activation(gt[:, :, :], bank[2][:, 0:TT * 3 * NH].rearrange("p (t g) -> p t g", t=TT),
                           ACT.Sigmoid).then_inc(gates_ready, 1)
            split_hi(act, n0 + 5)

        @block.vector
        def _(dve):
            dve.wait_ge(r_z, 1)
            dve.sem_inc(drained, 1)
            dve.wait_ge(vcz_ready, 1)
            dve.sem_inc(drained, 1)
            split_lo(dve, n0 + 2)
            dve.wait_ge(got_con, 16 * 13)
            rope_out(dve, (0, 0), kr[:, 0, :])
            dve.wait_ge(r_z, 2)
            dve.sem_inc(drained, 1)
            rope_out(dve, (1, 1), kr[:, 1, :])
            dve.wait_ge(r_z, 3)
            dve.sem_inc(drained, 1)
            split_lo(dve, n0 + 3)
            dve.wait_ge(pads_ready, 1)
            for half in range(2):
                dve.wait_ge(tiles, 2 * n0 + 5 + half)
                for j in range(2):
                    tt = 2 * half + j
                    src = bank[half][:, IC * j:IC * j + IC].rearrange("p (b g d) -> p b g d", b=2, g=2)
                    dst = vp[:, tt, :, HD:HD + 256].rearrange("p b (g e) -> p b g e", g=2)[:, :, :, 0:HD]
                    ins = dve.tensor_copy(dst, src)
                ins.then_inc(drained, 1)
            split_lo(dve, n0 + 4)
            rope_out(dve, (2, 0), kr[:, 2, :])
            dve.wait_ge(gates_ready, 1)
            dve.sem_inc(drained, 1)
            split_lo(dve, n0 + 5)

    def block1_q():
        n0, m0, r0 = new_items(4), new_tiles(8), 3

        @block.sync
        def _(sp):
            with sp.Fori(0, 2) as i:
                for j in range(2):
                    load_item(sp, n0 + j, i, full_item(n0 + j, w["w_in"], 0, OFF_Q + IC * j + 2 * IC * i))

        @block.tensor
        def _(pe):
            pe.wait_ge(drained, m0)
            with pe.Fori(0, 2) as i:
                for t in range(4):
                    if t % 2 == 0:
                        item_ready(pe, n0 + t // 2, i)
                    pe.wait_ge(drained, m0 - 4 + t + 1 + 4 * i)
                    tile_of(pe, n0 + t // 2, t % 2, bank[t][:, :], H).then_inc(tiles, 1)
                    if t:
                        rope_mm(pe, (r0 + t - 1 + 4 * i, (r0 + t - 1) % 2))
                rope_mm(pe, (r0 + 3 + 4 * i, (r0 + 3) % 2))

        @block.scalar
        def _(act):
            with act.Fori(0, 2) as i:
                for t in range(4):
                    act.wait_ge(tiles, 2 * n0 + t + 1 + 4 * i)
                    rope_in(act, (r0 + t + 4 * i, (r0 + t) % 2), bank[t][:, :], pcol("q_norm"))
                    if t % 2:
                        split_hi(act, n0 + 2 + t // 2, i)

        @block.vector
        def _(dve):
            with dve.Fori(0, 2) as i:
                dch.loop(i, 4, 2)
                for t in range(4):
                    dve.wait_ge(r_z, r0 + t + 1 + 4 * i)
                    dve.sem_inc(drained, 1)
                    if t % 2:
                        split_lo(dve, n0 + 2 + t // 2, i)
                    rope_out(dve, (r0 + t + 4 * i, (r0 + t) % 2), flat(qt[:, bass.ds(4 * i + t, 1), :]))
            dch.done()
        return m0 + 8

    def flat(ap):
        return ap.rearrange("p a n -> p (a n)")

    f_root, f_rec, f_spread, f_used, kd_mm, kd_done = (sem("f_root"), sem("f_rec"), sem("f_spread"), sem("f_used"),
                                                       sem("kd_mm"), sem("kd_done"))
    c_win, c_mm1, c_gelu, c_mm2, c_out = sem("c_win"), sem("c_mm1"), sem("c_gelu"), sem("c_mm2"), sem("c_out")
    kd_low, q_hi, q_lo = sem("kd_low"), sem("q_hi"), sem("q_lo")
    c_pad, c_s, c_sub, c_exp, c_p, c_t, c_done = (sem("c_pad"), sem("c_s"), sem("c_sub"), sem("c_exp"), sem("c_p"),
                                                  sem("c_t"), sem("c_done"))

    def block1_finish_qk(m1):

        @block.scalar
        def _(act):
            act.wait_ge(r_mm, 11)
            act.activation(rtq[:, :, :], bank[6][:, 0:44 * TT].rearrange("p (t g) -> p t g", t=TT)[:, :, 0:22],
                           ACT.Sqrt, bias=eps[:, 0:1], scale=1.0 / HD).then_inc(f_root, 1)
            act.wait_ge(f_rec, 1)
            act.wait_ge(r_done, 11)
            for n in range(11):
                if n >= 2:
                    act.wait_ge(f_spread, n - 1)
                act.activation(rwide[:, n % 2, :, :].rearrange("p t (h d) -> p t h d", h=2),
                               rq[:, :, 2 * n:2 * n + 2].unsqueeze(3).to_broadcast([P, TT, 2, HD]),
                               ACT.Copy).then_inc(f_wide, 1)
            act.activation(caus[:, :], causf[:, :], ACT.Copy).then_inc(kd_done, 1)
            act.wait_ge(c_mm1, 2)
            act.activation(hs[0:2 * NCMP, :], bank[0][0:2 * NCMP, 0:2 * P], ACT.Copy).then_inc(c_gelu, 1)
            act.wait_ge(c_mm1, 3)
            for a in range(2):
                ins = act.activation(gel[:, a, :, :], bank[1][:, 64 * a:64 * a + 2 * NCMP].rearrange(
                    "p (g n) -> p g n", g=2), ACT.Gelu_apprx_tanh, bias=pcol("cmp_b1", a))
            ins.then_inc(c_gelu, 1)
            for b in range(2):
                for g in range(2):
                    n = 2 * b + g
                    act.wait_ge(kd_mm, n + 1)
                    act.activation(kdh[:, b, g, :], bank[4 + n][:, :], ACT.Copy).then_inc(kd_done, 1)

        @block.vector
        def _(dve):
            dve.wait_ge(f_root, 1)
            dve.reciprocal(rq[:, :, :], rtq[:, :, :]).then_inc(f_rec, 1)
            for n in range(11):
                dve.wait_ge(f_spread, n + 1)
                dst = kr[:, n, :] if n < 3 else qt[:, n - 3, :]
                dve.scalar_tensor_tensor(out=dst, in0=dst, scalar=1.0 if n < 3 else SCALE, in1=bank[4 + n % 2][:, :],
                                         op0=ALU.mult, op1=ALU.mult).then_inc(f_used, 1)
            dve.wait_ge(f_used, 11)
            dve.wait_ge(vcz_ready, 1)
            for a, src in ((0, kr[:, 0, :]), (1, vcz[:, :])):
                v = src.rearrange("p (m b) -> p b m", b=CMP_STRIDE)
                for half in range(2):
                    for g in range(2):
                        rows = slice(HD * g, HD * g + HD)
                        pos = parm[rows, PCOL["pos"] + 32 * a + 16 * half:PCOL["pos"] + 32 * a + 16 * half + 16]
                        dve.tensor_tensor(win[rows, a, 16 * half:16 * half + 16, NCMP * g:NCMP * g + NCMP],
                                          v[rows, :, half:half + NCMP],
                                          pos.unsqueeze(2).to_broadcast([HD, 16, NCMP]), ALU.add).then_inc(c_win, 1)
            for n in range(4):
                dve.wait_ge(kd_done, n + 2)
                dve.tensor_tensor(kdl[:, n // 2, n % 2, :], bank[4 + n][:, :], kdh[:, n // 2, n % 2, :].bitcast(F32),
                                  ALU.subtract).then_inc(kd_low, 1)
            dve.wait_ge(c_mm2, 1)
            dve.wait_ge(c_pad, 3)
            dve.tensor_copy(kc[:, :, :], bank[2][:, 0:2 * NCMP].rearrange("p (g n) -> p g n", g=2))
            for g in range(2):
                for hq in range(4):
                    ins = dve.tensor_copy(vc[32 * hq:32 * hq + NCMP, g, hq // 2, HD * (hq % 2):HD * (hq % 2) + HD],
                                          bank[3][0:NCMP, HD * g:HD * g + HD])
            dch(dve, ins)
            dve.sem_inc(c_out, 1)
            for b in range(4):
                i2, e = b // 2, b % 2
                view = sc[:, 2 * i2:2 * i2 + 2, e::2, 0:NCMP]
                src = bank[b][:, :].rearrange("p (i h n) -> p i h n", i=2, h=8)[:, :, :, 0:NCMP]
                dve.wait_ge(c_s, b + 1)
                for ii in range(2):
                    i = 2 * i2 + ii
                    v1 = sc[:, i, e::2, 0:NCMP]
                    dve.tensor_tensor(v1, src[:, ii], mc[:, i:i + 1, :].to_broadcast([P, 8, NCMP]), ALU.add) \
                        .then_inc(c_sub, 1)
            dve.wait_ge(c_sub, 8)
            dch(dve, dve.tensor_reduce(cmx[:, :, :], sc[:, :, :, 0:NCMP], AX, ALU.max))
            for i in range(TT):
                dve.tensor_tensor(sc[:, i, :, 0:NCMP], sc[:, i, :, 0:NCMP],
                                  cmx[:, i, :].unsqueeze(2).to_broadcast([P, NH, NCMP]), ALU.subtract) \
                    .then_inc(c_sub, 1)
            dve.wait_ge(c_exp, TT)
            dch(dve, dve.tensor_reduce(csm[:, :, :], sc[:, :, :, 0:NCMP], AX, ALU.add))
            dch(dve, dve.reciprocal(crs[:, :, :], csm[:, :, :]))
            dch(dve, dve.tensor_tensor(crs[:, :, :], crs[:, :, :],
                                       gt[:, :, :].rearrange("p t (h b) -> p t h b", b=3)[:, :, :, 0], ALU.mult))
            for i in range(TT):
                v1 = sc[:, i, :, 0:NCMP]
                dch(dve, dve.tensor_tensor(v1, v1, crs[:, i, :].unsqueeze(2).to_broadcast([P, NH, NCMP]), ALU.mult))
                dve.tensor_tensor(v1, v1, keep[:, i:i + 1, :].to_broadcast([P, NH, NCMP]), ALU.mult) \
                    .then_inc(c_p, 1)
            for q4 in range(4):
                dve.wait_ge(c_t, q4 + 1)
                dve.tensor_copy(pct[:, q4, :], bank[4 + q4 % 2][:, :]).then_inc(c_done, 1)

        @block.gpsimd
        def _(pool):
            pool.wait_ge(r_done, 11)
            pool.wait_ge(r_mm, 11)
            for g in range(2):
                ins = pool.memset(win[HD * g:HD * g + HD, :, :, NCMP * (1 - g):NCMP * (2 - g)], 0.0)
            ins.then_inc(c_pad, 1)
            pool.wait_ge(c_mm1, 2)
            pool.memset(vc[:, :, :, :], 0.0).then_inc(c_pad, 1)
            pool.memset(sc[:, :, :, :], 0.0).then_inc(c_pad, 1)

        @block.scalar
        def _(act):
            for i in range(TT):
                act.wait_ge(c_sub, 8 + i + 1)
                act.activation(sc[:, i, :, 0:NCMP], sc[:, i, :, 0:NCMP], ACT.Exp).then_inc(c_exp, 1)

        @block.tensor
        def _(pe):
            pe.wait_ge(f_rec, 1)
            pe.wait_ge(r_done, 11)
            for n in range(11):
                if n >= 2:
                    pe.wait_ge(f_used, n - 1)
                pe.wait_ge(f_wide, n + 1)
                spread(pe, bank[4 + n % 2], lambda t: rwide[:, n % 2, t, :]).then_inc(f_spread, 1)
            pe.wait_ge(drained, m1)
            pe.wait_ge(c_pad, 1)
            for a in range(2):
                pe.wait_ge(c_win, 4 * a + 4)
                for pos in range(CMP_BLOCK):
                    mm = pe.matmul(bank[0][0:2 * NCMP, P * a:P * a + P], win[:, a, pos, :], w1[:, a, pos, :],
                                   start=(pos == 0), stop=(pos == CMP_BLOCK - 1))
                mm.then_inc(c_mm1, 1)
            pe.wait_ge(f_used, 11)
            for b in range(2):
                for g in range(2):
                    pe.matmul(bank[4 + 2 * b + g][:, :], dup[:, g, :], kr[:, 1 + b, :], start=True, stop=True) \
                        .then_inc(kd_mm, 1)
            pe.wait_ge(c_gelu, 1)
            for a in range(2):
                mm = pe.transpose(bank[1][:, 64 * a:64 * a + 2 * NCMP], hs[0:2 * NCMP, P * a:P * a + P],
                                  ident[0:2 * NCMP, 0:2 * NCMP])
            mm.then_inc(c_mm1, 1)
            pe.wait_ge(c_gelu, 2)
            pe.matmul(bank[2][:, 0:2 * NCMP], w2d[:, :], gel[:, 0, :, :].rearrange("p g n -> p (g n)"),
                      start=True, stop=True)
            for g in range(2):
                mm = pe.matmul(bank[3][0:NCMP, HD * g:HD * g + HD], gel[:, 1, g, :], w2v[:, :], start=True, stop=True)
            mm.then_inc(c_mm2, 1)
            pe.wait_ge(c_out, 1)
            for b in range(4):
                i2, e = b // 2, b % 2
                for ii in range(2):
                    i = 2 * i2 + ii
                    for hp in range(8):
                        mm = pe.matmul(bank[b][:, 256 * ii + 32 * hp:256 * ii + 32 * hp + NCMP],
                                       qt[HD * e:HD * e + HD, hp, P * i:P * i + P],
                                       kc[HD * e:HD * e + HD, hp // 4, :], start=True, stop=True)
                mm.then_inc(c_s, 1)
            pe.wait_ge(c_p, TT)
            pe.wait_ge(kd_low, 4)
            for q4 in range(4):
                if q4 >= 2:
                    pe.wait_ge(c_done, q4 - 1)
                for i in range(TT):
                    mm = pe.transpose(bank[4 + q4 % 2][:, P * i:P * i + P],
                                      sc[:, i, 4 * q4:4 * q4 + 4, :].rearrange("p h n -> p (h n)"), ident[:, :])
                mm.then_inc(c_t, 1)

    s_done, s_max, p_exp, p_scaled = sem("s_done"), sem("s_max"), sem("p_exp"), sem("p_scaled")
    t_done, t_act, t_dve, pv_done = sem("t_done"), sem("t_act"), sem("t_dve"), sem("pv_done")
    o_high, o_out = sem("o_high"), sem("o_out")
    UNITS = 4 * (NH // 2)
    POFF = [0, 128, 384, 768]

    PV_T, GATE_T = 4, 2 * KT
    aside = nc.dram_tensor("aside", (PV_T + GATE_T, P, S), F32, kind="Internal").ap()
    stage = at("stage", Y + 14 * K, [S])
    spilled = sem("spilled")
    PIECES = 4 * (PV_T + GATE_T)

    def block1_attention():
        n0, m0 = new_items((PV_T + GATE_T) // 2), new_tiles(PV_T + GATE_T)

        SHARE = (2, 2, 2, 2, 4, 2, 2, 4)

        def done_pieces(u):
            return sum(SHARE[v % len(SHARE)] for v in range(min(u + 1, UNITS)))

        assert done_pieces(UNITS) == PIECES

        def done_tiles(u):
            return done_pieces(u) // 4

        @block.sync
        def _(sp):
            for j in range(2):
                load_item(sp, n0 + j, 0, full_item(n0 + j, w["w_in"], 0, IC * j))
            with sp.Fori(0, KT // 2) as i:
                for j in range(2):
                    load_item(sp, n0 + 2 + j, i, full_item(n0 + 2 + j, w["w_in"], 0, OFF_MG + IC * j + 2 * IC * i))

        @block.gpsimd
        def _(pool):
            for t in range(PV_T + GATE_T):
                pool.wait_ge(drained, m0 + t + 1)
                pool.dma_start(aside[t], stage[:, :]).then_inc(spilled, 16)

        def pieces(pe, u):
            for q in range(done_pieces(u - 1), done_pieces(u)):
                t, part = q // 4, q % 4
                if part == 0:
                    if t % 2 == 0:
                        item_ready(pe, n0 + t // 2)
                    pe.wait_ge(drained, m0 + t)
                mm = tile_of(pe, n0 + t // 2, t % 2, bank[7][:, :], H, kts=2, k0=2 * part, w0=2 * part,
                             first=part == 0, last=part == 3)
                if part == 3:
                    mm.then_inc(tiles, 1)

        def scores(pe, u):
            p, e, b = u // 4, u // 2 % 2, u % 2
            if u % 4 == 0:
                pe.wait_ge(q_lo, p + 1)
            for i in range(TT):
                wd = P * (i + 1)
                if u:
                    pe.wait_ge(p_exp, 4 * (u - 1) + i + 1)
                for part in (kdh, kdl):
                    pe.matmul(bank[i][:, 0:wd], qs[:, p % 2, e, P * i:P * i + P], part[:, b, p // 4, 0:wd],
                              start=(part is kdh), stop=False)
                pe.matmul(bank[i][:, P * i:wd], identr[:, :], caus[:, :], start=False, stop=True).then_inc(s_done, 1)

        def turn(pe, u):
            for i in range(TT):
                pe.wait_ge(p_scaled, 4 * u + i + 1)
                if i >= 2:
                    pe.wait_ge(t_dve, 3 * u + i - 1)
                elif u:
                    pe.wait_ge(t_dve if i else t_act, 3 * u if i else u)
                for j in range(i + 1):
                    mm = pe.transpose(bank[4 + i % 2][:, P * j:P * j + P],
                                      pr[:, u % 2, POFF[i] + P * j:POFF[i] + P * j + P], ident[:, :])
                mm.then_inc(t_done, 1)

        def values(pe, u):
            p, e, b = u // 4, u // 2 % 2, u % 2
            out = bank[6]
            if u % 4 == 0:
                if p:
                    pe.wait_ge(o_out, p)
                pe.matmul(out[:, :], vc[:, p // 4, p % 2, :], pct[:, p // 2, :], start=True, stop=False)
            pe.wait_ge(t_act, u + 1)
            pe.wait_ge(t_dve, 3 * u + 3)
            g = p // 4
            c0 = HD + P * g if e == 0 else P * g
            for j in range(TT):
                mm = pe.matmul(out[:, P * j:S], vp[:, j, b, c0:c0 + P], pt[:, u % 2, j, P * j:S],
                               start=False, stop=(u % 4 == 3 and j == TT - 1))
            mm.then_inc(pv_done, 1)

        @block.tensor
        def _(pe):
            pe.wait_ge(c_done, 4)
            pe.wait_ge(kd_done, 5)
            scores(pe, 0)
            for u in range(UNITS + 1):
                if u:
                    turn(pe, u - 1)
                if u + 1 < UNITS:
                    scores(pe, u + 1)
                if u < UNITS:
                    pieces(pe, u)
                if u:
                    values(pe, u - 1)

        def turned(eng, u, i, signal, copy):
            eng.wait_ge(t_done, 4 * u + i + 1)
            if u >= 2:
                eng.wait_ge(pv_done, u - 1)
            copy(pt[:, u % 2, 0:i + 1, P * i:P * i + P],
                 bank[4 + i % 2][:, 0:P * (i + 1)].rearrange("p (j q) -> p j q", j=i + 1)).then_inc(signal, 1)

        @block.scalar
        def _(act):
            def expo(u, i):
                wd = P * (i + 1)
                act.wait_ge(s_max, 4 * u + i + 1)
                if u >= 2 and i == 0:
                    act.wait_ge(t_done, 4 * (u - 1))
                act.activation(pr[:, u % 2, POFF[i]:POFF[i] + wd], bank[i][:, 0:wd], ACT.Exp,
                               bias=nm[:, u % 2, i:i + 1], accum_out=sm[:, u % 2, i:i + 1]).then_inc(p_exp, 1)

            def queries_high(p):
                if p >= 2:
                    act.wait_ge(s_done, 16 * (p - 1))
                for e in range(2):
                    rows = slice(HD * e, HD * e + HD)
                    ins = act.activation(qs[rows, p % 2, e, :], qt[rows, p, :], ACT.Copy)
                ins.then_inc(q_hi, 1)

            queries_high(0)
            act.wait_ge(c_t, 4)
            for u in range(UNITS + 2):
                if u >= 2 and u % 4 == 1:
                    p = u // 4 - 1
                    act.wait_ge(pv_done, u - 1)
                    act.activation(oh[:, p, :], bank[6][:, :], ACT.Copy).then_inc(o_high, 1)
                if u < UNITS:
                    for i in range(TT):
                        expo(u, i)
                ended = range(done_tiles(u - 2), done_tiles(u - 1))
                for t in ended:
                    act.wait_ge(tiles, 2 * n0 + t + 1)
                    if t:
                        act.wait_ge(spilled, 16 * t)
                    act.activation(stage[:, :], bank[7][:, :], ACT.Copy).then_inc(drained, 1)
                if 1 <= u <= UNITS:
                    turned(act, u - 1, 2, t_act, lambda o, s: act.activation(o, s, ACT.Copy))
                if u % 4 == 1 and u // 4 + 1 < NH // 2:
                    queries_high(u // 4 + 1)
                for t in ended:
                    if t % 2:
                        split_hi(act, n0 + 2 + t // 2)

        @block.vector
        def _(dve):
            def queries_low(p):
                dve.wait_ge(q_hi, p + 1)
                for e in range(2):
                    rows, other = slice(HD * e, HD * e + HD), slice(HD - HD * e, P - HD * e)
                    ins = dve.tensor_tensor(qs[other, p % 2, e, :], qt[rows, p, :],
                                            qs[rows, p % 2, e, :].bitcast(F32), ALU.subtract)
                ins.then_inc(q_lo, 1)

            queries_low(0)
            for u in range(UNITS + 2):
                if u % 4 == 2 and u // 4 + 1 < NH // 2:
                    queries_low(u // 4 + 1)
                if u < UNITS:
                    for i in range(TT):
                        dve.wait_ge(s_done, 4 * u + i + 1)
                        if u >= 2:
                            dve.wait_ge(p_exp, 4 * (u - 1) - 3 + i)
                        dve.tensor_reduce(nm[:, u % 2, i:i + 1], bank[i][:, 0:P * (i + 1)], AX, ALU.max,
                                          negate=True).then_inc(s_max, 1)
                if 1 <= u <= UNITS:
                    v = u - 1
                    h, b = v // 2, v % 2
                    dve.wait_ge(p_exp, 4 * v + 4)
                    if v >= 2:
                        dve.wait_ge(p_scaled, 4 * (v - 1))
                    dch(dve, dve.reciprocal(rs[:, v % 2, :], sm[:, v % 2, :]))
                    dch(dve, dve.tensor_tensor(rs[:, v % 2, :], rs[:, v % 2, :], gt[:, :, 3 * h + 1 + b], ALU.mult))
                    for i in range(TT):
                        part = pr[:, v % 2, POFF[i]:POFF[i] + P * (i + 1)]
                        dve.tensor_scalar(part, part, rs[:, v % 2, i:i + 1], None, ALU.mult).then_inc(p_scaled, 1)
                if 1 <= u <= UNITS:
                    for i in (0, 1, 3):
                        turned(dve, u - 1, i, t_dve, dve.tensor_copy)
                for t in range(done_tiles(u - 3), done_tiles(u - 2)):
                    if t % 2:
                        split_lo(dve, n0 + 2 + t // 2)
                if u >= 2 and u % 4 == 1:
                    p = u // 4 - 1
                    if p == NH // 2 - 1:
                        dve.wait_ge(spilled, 16 * (PV_T + GATE_T))
                    dve.wait_ge(o_high, p + 1)
                    dve.tensor_tensor(ol[:, p, :], bank[6][:, :], oh[:, p, :].bitcast(F32),
                                      ALU.subtract).then_inc(o_out, 1)

    pu = at("pu", Y + 16 * K, [4, 16 + S])
    pa = at("pa", Y + 25 * K, [2, 16 + S])
    pm = at("pm", Y + 48 * K, [4, S])
    pmh = at("pmh", Y + 64 * K, [4, S], F32R)
    pml = at("pml", Y + 72 * K, [4, S], F32R)
    pw = at("pw", Y + 80 * K, [4, P])
    rc = at("rc", Y + 82 * K, [4, 16])
    p_pad, p_mean, p_mm, p_high, p_out = (sem("p_pad"), sem("p_mean"), sem("p_mm"),
                                                  sem("p_high"), sem("p_out"))

    mh = at("mh", Y + 16 * K, [KT, S], F32R)
    ml = at("ml", Y + 48 * K, [KT, S], F32R)
    gs = at("gs", SC_AT, [4, S])
    mt = at("mt", SC_AT + 8 * K, [2, S])
    mu = at("mu", SC_AT + 12 * K, [2, S])
    g_sig, g_pool, g_full, g_high, g_low = sem("g_sig"), sem("g_pool"), sem("g_full"), sem("g_high"), sem("g_low")
    MI = D // IC

    def block1_merge():
        n0 = new_items(2 * MI)

        @block.sync
        def _(sp):
            def items(i):
                load_item(sp, n0 + 2 * i, 0, full_item(n0 + 2 * i, w["w_attn_br"], 0, IC * i))
                b = n0 + 2 * i + 1
                v = w["w_pool_br"].rearrange("(k p) n -> p k n", p=P)
                s = wraw[:, b % 2]
                load_item(sp, b, 0, [(s[:, k:k + 2, :], v[:, k:k + 2, IC * i:IC * i + IC]) for k in (0, 2)])

            def gates(i):
                if i:
                    sp.wait_ge(g_full, AHEAD + 4 * i)
                for part in range(2):
                    t0 = PV_T + KT * part + 2 * i
                    sp.dma_start(gs[:, 2 * part:2 * part + 2, :], aside[t0:t0 + 2].rearrange("t p n -> p t n")) \
                        .then_inc(got_x, 16)

            items(0)
            sp.wait_ge(spilled, 16 * (PV_T + GATE_T))
            sp.wait_ge(pv_done, UNITS)
            sp.dma_start(pu[:, :, 16:16 + S], aside[0:PV_T].rearrange("t p n -> p t n")).then_inc(got_con, 16)
            sp.dma_start(pw[:, :, :], w["pool_w"].rearrange("g c d -> c g d")).then_inc(got_con, 16)
            sp.dma_start(rc[:, :, :], con[:, CCOL["rcnt"]:CCOL["rcnt"] + 64].rearrange(
                "p (g n) -> p g n", g=4)).then_inc(got_con, 16)
            gates(0)
            for i in range(1, MI):
                items(i)
                gates(i)

        @block.gpsimd
        def _(pool):
            pool.wait_ge(pv_done, UNITS)
            pool.memset(pu[:, :, 0:16], 0.0)
            pool.memset(pa[:, :, 0:16], 0.0).then_inc(p_pad, 1)

        @block.tensor
        def _(pe):
            for i in range(MI):
                c = 4 * (i % 2)
                a, b = n0 + 2 * i, n0 + 2 * i + 1
                if i == 0:
                    pe.wait_ge(p_exp, 4 * UNITS)
                elif i == 1:
                    pe.wait_ge(t_act, UNITS)
                    pe.wait_ge(t_dve, 3 * UNITS)
                else:
                    pe.wait_ge(g_pool, AHEAD + 2 * (i - 1))
                item_ready(pe, a)
                for t in range(2):
                    for k in range(KT):
                        if i == 0 and t == 0:
                            pe.wait_ge(o_out, k + 1)
                        mm = passes(pe, bank[c + t][:, :], (whi[:, a % 2, k, P * t:P * t + P],
                                                            wlo[:, a % 2, k, P * t:P * t + P]),
                                    (oh[:, k, :], ol[:, k, :]), k == 0, k == KT - 1)
                    mm.then_inc(tiles, 1)
                if i == 0:
                    pe.wait_ge(got_con, CON_P)
                    pe.wait_ge(t_act, UNITS)
                    pe.wait_ge(t_dve, 3 * UNITS)
                    for g in range(4):
                        pe.wait_ge(p_mean, g + 1)
                        if g >= 2:
                            pe.wait_ge(p_out, g - 1)
                        pe.matmul(bank[4 + g % 2][:, :], pw[:, g, :], pm[:, g, :], start=True, stop=True) \
                            .then_inc(p_mm, 1)
                item_ready(pe, b)
                pe.wait_ge(p_out, 4)
                if i >= 2:
                    pe.wait_ge(g_full, AHEAD + 4 * (i - 1))
                for t in range(2):
                    tile_of(pe, b, t, bank[c + 2 + t][:, :], (pmh, pml), kts=4).then_inc(tiles, 1)

        @block.scalar
        def _(act):
            for i in range(MI):
                act.wait_ge(got_x, 16 * TT + 32 * (i + 1))
                act.activation(gs[:, :, :], gs[:, :, :], ACT.Sigmoid).then_inc(g_sig, 1)
                split_hi(act, n0 + 2 * i + 2)
                if i == 0:
                    for g in range(4):
                        act.wait_ge(p_mm, g + 1)
                        act.activation(pmh[:, g, :], bank[4 + g % 2][:, :], ACT.Copy,
                                       scale=pcol("pool_scale", g)).then_inc(p_high, 1)
                split_hi(act, n0 + 2 * i + 3)
                for t in range(2):
                    act.wait_ge(g_full, AHEAD + 2 * t + 2 + 4 * i)
                    act.activation(mh[:, 2 * i + t, :], mt[:, t, :], ACT.Copy).then_inc(g_high, 1)

        @block.vector
        def _(dve):
            dve.wait_ge(p_pad, 1)
            dve.wait_ge(got_con, CON_P)
            for g, wd in enumerate(POOL_WINDOWS):
                src, step, flip = pu[:, g, :], 1, 0
                while step < wd:
                    dst = pa[:, flip, :]
                    dch(dve, dve.tensor_tensor(dst[:, 16:16 + S], src[:, 16:16 + S], src[:, 16 - step:16 + S - step],
                                               ALU.add))
                    src, step, flip = dst, 2 * step, 1 - flip
                dch(dve, dve.tensor_tensor(pm[:, g, 0:16], src[:, 16:32], rc[:, g, :], ALU.mult))
                dch(dve, dve.tensor_tensor(pm[:, g, 0:16], pm[:, g, 0:16], pu[:, g, 16:32], ALU.subtract))
                dch(dve, dve.scalar_tensor_tensor(out=pm[:, g, 16:S], in0=src[:, 32:16 + S], scalar=1.0 / wd,
                                                  in1=pu[:, g, 32:16 + S], op0=ALU.mult, op1=ALU.subtract))
                dve.sem_inc(p_mean, 1)
            for i in range(MI):
                c = 4 * (i % 2)
                a, b = n0 + 2 * i, n0 + 2 * i + 1
                if i == 0:
                    for g in range(4):
                        dve.wait_ge(p_high, g + 1)
                        dve.scalar_tensor_tensor(out=pml[:, g, :], in0=bank[4 + g % 2][:, :],
                                                 scalar=pcol("pool_scale", g), in1=pmh[:, g, :].bitcast(F32),
                                                 op0=ALU.mult, op1=ALU.subtract).then_inc(p_out, 1)
                split_lo(dve, a + 2)
                dve.wait_ge(g_sig, AHEAD + i + 1)
                for t in range(2):
                    dve.wait_ge(tiles, 2 * a + t + 1)
                    dve.tensor_tensor(mu[:, t, :], gs[:, 2 + t, :], bank[c + t][:, :], ALU.mult).then_inc(g_pool, 1)
                split_lo(dve, b + 2)
                if i:
                    dve.wait_ge(g_low, AHEAD + 2 * i)
                for t in range(2):
                    dve.wait_ge(tiles, 2 * b + t + 1)
                    dve.tensor_tensor(mt[:, t, :], gs[:, t, :], bank[c + 2 + t][:, :], ALU.mult).then_inc(g_full, 1)
                    dve.wait_ge(g_full, AHEAD + 2 * t + 1 + 4 * i)
                    dve.wait_ge(g_pool, AHEAD + 2 * i + t + 1)
                    dve.tensor_tensor(mt[:, t, :], mt[:, t, :], mu[:, t, :], ALU.add).then_inc(g_full, 1)
                for t in range(2):
                    dve.wait_ge(g_high, 2 * i + t + 1)
                    dve.tensor_tensor(ml[:, 2 * i + t, :], mt[:, t, :], mh[:, 2 * i + t, :].bitcast(F32),
                                      ALU.subtract).then_inc(g_low, 1)
        return (g_low, AHEAD)

    def residual(mat, rhs, r0=0, last=False, ready=None, late=False):
        n0, m0 = new_items(4), new_tiles(KT)

        @block.sync
        def _(sp):
            with sp.Fori(0, 2) as i:
                for j in range(2):
                    load_item(sp, n0 + j, i, full_item(n0 + j, mat, r0, IC * j + 2 * IC * i))

        @block.tensor
        def _(pe):
            pe.wait_ge(drained, m0)
            with pe.Fori(0, 2) as i:
                for t in range(4):
                    if t % 2 == 0:
                        item_ready(pe, n0 + t // 2, i)
                    pe.wait_ge(drained, m0 - 4 + t + 1 + 4 * i)
                    tile_of(pe, n0 + t // 2, t % 2, bank[t][:, :], rhs, ready=ready if t == 0 else None) \
                        .then_inc(tiles, 1)

        @block.scalar
        def _(act):
            if last:
                split_hi(act, n0 + 2)
                split_hi(act, n0 + 3)
                return
            if late:
                for j in range(3):
                    split_hi(act, n0 + 2 + j)
                return
            with act.Fori(0, 2) as i:
                for j in range(2):
                    split_hi(act, n0 + 2 + j, i)

        @block.vector
        def _(dve):
            def part(i):
                for t in range(4):
                    dve.wait_ge(tiles, 2 * n0 + t + 1 + 4 * i)
                    x_t = flat(xt[:, bass.ds(4 * i + t, 1), :])
                    dve.tensor_tensor(x_t, x_t, bank[t][:, :], ALU.add).then_inc(drained, 1)
                    if t % 2 and not (late and isinstance(i, int) and i and t == 3):
                        split_lo(dve, n0 + 2 + t // 2, i)

            if last or late:
                part(0)
                part(1)
                return
            with dve.Fori(0, 2) as i:
                part(i)
        return m0

    yh = at("yh", Y, [FT + 1, S], F32R)
    yl = at("yl", Y + 44 * K, [FT + 1, S], F32R)
    cg = at("cg", SC_AT, [2, S])
    cv = at("cv", SC_AT + 4 * K, [2, S])
    fa = at("fa", SC_AT + 8 * K, [2, S])
    f_id, f_conv, f_silu, f_act, f_high, f_low = (sem("f_id"), sem("f_conv"), sem("f_silu"), sem("f_act"),
                                                  sem("f_high"), sem("f_low"))

    def ffn_up(ready):
        n0, m0 = new_items(FT + 1), new_tiles(2 * (FT + 1))
        v = w["w_up"].rearrange("(k p) n -> p k n", p=P)
        LOOPS = FT // 2
        rest = [FT - 1, FT] if FT % 2 else [FT]

        def pairs(b, c0, cols):
            s = wraw[:, b % 2]
            return [(s[:, :, 0:cols], v[:, :, bass.ds(c0, cols)]), (s[:, :, P:P + cols], v[:, :, bass.ds(c0 + DFF, cols)])]

        @block.sync
        def _(sp):
            with sp.Fori(0, LOOPS) as i:
                for j in range(2):
                    load_item(sp, n0 + j, i, pairs(n0 + j, P * j + IC * i, P))
            for f in rest:
                load_item(sp, n0 + f, 0, pairs(n0 + f, P * f, P if f < FT else FREST))

        def products(pe, b, j, i, f, cols):
            item_ready(pe, b, i)
            for t in range(2):
                pe.wait_ge(drained, m0 - 4 + 2 * f + t + 1)
                tile_of(pe, b, t, bank[2 * j + t][0:cols, :], H, cols=cols, ready=ready if t + j == 0 else None) \
                    .then_inc(tiles, 1)

        def straight(act, b, j, i, f, n):
            for t, (wn, bn, dst) in enumerate((("convw_g", "convb_g", cg), ("convw_v", "convb_v", cv))):
                act.wait_ge(tiles, 2 * b + 4 * i + t + 1)
                if not (isinstance(f, int) and f < 2):
                    act.wait_ge(f_act, AHEAD + f - 1)
                act.activation(dst[0:n, j, :], bank[2 * j + t][0:n, :], ACT.Identity,
                               scale=pcol_at(wn, 2 * (FT + 1) + f, n), bias=pcol_at(bn, f, n)).then_inc(f_id, 1)

        def conv(dve, b, j, i, f, n):
            for t, (wn, dst) in enumerate((("convw_g", cg), ("convw_v", cv))):
                src = bank[2 * j + t]
                dve.wait_ge(f_id, 2 * f + t + 1)
                dve.scalar_tensor_tensor(out=dst[0:n, j, 1:S], in0=src[0:n, 0:S - 1],
                                         scalar=pcol_at(wn, FT + 1 + f, n), in1=dst[0:n, j, 1:S],
                                         op0=ALU.mult, op1=ALU.add).then_inc(f_conv, 1)
                dve.wait_ge(f_conv, 4 * f + 2 * t + 1)
                dve.scalar_tensor_tensor(out=dst[0:n, j, 2:S], in0=src[0:n, 0:S - 2],
                                         scalar=pcol_at(wn, f, n), in1=dst[0:n, j, 2:S],
                                         op0=ALU.mult, op1=ALU.add).then_inc(f_conv, 1)
                dve.wait_ge(f_conv, 4 * f + 2 * t + 2)
                dve.sem_inc(drained, 1)

        def gate(act, j, f, n):
            act.wait_ge(f_conv, 4 * f + 2)
            act.activation(cg[0:n, j, :], cg[0:n, j, :], ACT.Silu).then_inc(f_silu, 1)

        def product(dve, j, f, n):
            dve.wait_ge(f_silu, f + 1)
            if not (isinstance(f, int) and f < 2):
                dve.wait_ge(f_low, AHEAD + f - 1)
            dve.tensor_tensor(fa[0:n, j, :], cg[0:n, j, :], cv[0:n, j, :], ALU.mult).then_inc(f_act, 1)

        def high(act, j, f, n):
            act.wait_ge(f_act, AHEAD + f + 1)
            act.activation(flat(yh[0:n, bass.ds(f, 1), :]), fa[0:n, j, :], ACT.Copy).then_inc(f_high, 1)

        def low(dve, j, f, n):
            dve.wait_ge(f_high, f + 1)
            dve.tensor_tensor(flat(yl[0:n, bass.ds(f, 1), :]), fa[0:n, j, :],
                              flat(yh[0:n, bass.ds(f, 1), :]).bitcast(F32), ALU.subtract).then_inc(f_low, 1)

        def each(loop, eng, body):
            with eng.Fori(0, LOOPS) as i:
                for j in range(2):
                    body(n0 + j, j, i, 2 * i + j, P)
            for f in rest:
                body(n0 + f, f % 2, 0, f, P if f < FT else FREST)

        @block.tensor
        def _(pe):
            pe.wait_ge(drained, m0)
            each(None, pe, lambda b, j, i, f, n: products(pe, b, j, i, f, n))

        @block.scalar
        def _(act):
            def body(b, j, i, f, n):
                straight(act, b, j, i, f, n)
                split_hi(act, b + 2, i)
                gate(act, j, f, n)
                high(act, j, f, n)
            act.wait_ge(g_low, AHEAD + KT)
            each(None, act, body)

        @block.vector
        def _(dve):
            def body(b, j, i, f, n):
                conv(dve, b, j, i, f, n)
                product(dve, j, f, n)
                split_lo(dve, b + 2, i)
                low(dve, j, f, n)
            each(None, dve, body)

    def ffn_down():
        PER = 3
        n0, m0 = new_items(PER * MI), new_tiles(KT)
        mat = w["w_down"]
        v = mat[0:FT * P, :].rearrange("(k p) n -> p k n", p=P)

        @block.sync
        def _(sp):
            with sp.Fori(0, MI // 2) as i:
                for c in range(2):
                    for part in range(PER):
                        b = n0 + PER * c + part
                        s = wraw[:, b % 2]
                        cols = bass.ds(IC * c + 2 * IC * i, IC)
                        if part < 2:
                            pr_ = [(s[:, 0:4, :], v[:, 8 * part:8 * part + 4, cols]),
                                   (s[:, 4:8, :], v[:, 8 * part + 4:8 * part + 8, cols])]
                        else:
                            pr_ = [(s[:, 0:FT - 16, :], v[:, 16:FT, cols]),
                                   (s[0:FREST, FT - 16, :], mat[FT * P:DFF, cols])]
                        load_item(sp, b, PER * i, pr_)

        @block.tensor
        def _(pe):
            pe.wait_ge(f_low, AHEAD + FT + 1)
            pe.wait_ge(drained, m0)
            with pe.Fori(0, MI // 2) as i:
                for c in range(2):
                    for part in range(PER):
                        b = n0 + PER * c + part
                        item_ready(pe, b, PER * i)
                        p = b % 2
                        for t in range(2):
                            if part == 0:
                                pe.wait_ge(drained, m0 - 4 + 2 * c + t + 1 + 4 * i)
                            out = bank[2 * c + t][:, :]
                            if part < 2:
                                mm = tile_of(pe, b, t, out, (yh, yl), k0=8 * part, first=part == 0, last=False)
                            else:
                                tile_of(pe, b, t, out, (yh, yl), kts=FT - 16, k0=16, first=False, last=False)
                                k, cs = FT - 16, slice(P * t, P * t + P)
                                mm = passes(pe, out, (whi[0:FREST, p, k, cs], wlo[0:FREST, p, k, cs]),
                                            (yh[0:FREST, FT, :], yl[0:FREST, FT, :]), False, True)
                            mm.then_inc(tiles, 1)

        @block.scalar
        def _(act):
            for j in range(PER * MI - 1):
                split_hi(act, n0 + 2 + j)

        @block.vector
        def _(dve):
            for c in range(MI):
                for part in range(PER):
                    b = n0 + PER * c + part
                    if part == PER - 1:
                        for t in range(2):
                            dve.wait_ge(tiles, 2 * b + t + 1)
                            x_t = xt[:, 2 * c + t, :]
                            dve.tensor_tensor(x_t, x_t, bank[2 * (c % 2) + t][:, :], ALU.add).then_inc(drained, 1)
                    if b + 2 < n0 + PER * MI + 1:
                        split_lo(dve, b + 2)
        return m0

    def project(mat, c0, dst, scale=1.0, bias=None, ready=None):
        n0, m0 = new_items(4), new_tiles(KT)

        @block.sync
        def _(sp):
            with sp.Fori(0, 2) as i:
                for j in range(2):
                    load_item(sp, n0 + j, i, full_item(n0 + j, mat, 0, c0 + IC * j + 2 * IC * i))

        @block.tensor
        def _(pe):
            pe.wait_ge(drained, m0)
            with pe.Fori(0, 2) as i:
                for t in range(4):
                    if t % 2 == 0:
                        item_ready(pe, n0 + t // 2, i)
                    pe.wait_ge(drained, m0 - 4 + t + 1 + 4 * i)
                    tile_of(pe, n0 + t // 2, t % 2, bank[t][:, :], H, ready=ready if t == 0 else None) \
                        .then_inc(tiles, 1)

        @block.scalar
        def _(act):
            with act.Fori(0, 2) as i:
                for j in range(2):
                    split_hi(act, n0 + 2 + j, i)

        @block.vector
        def _(dve):
            with dve.Fori(0, 2) as i:
                for t in range(4):
                    dve.wait_ge(tiles, 2 * n0 + t + 1 + 4 * i)
                    out_t = flat(dst[:, bass.ds(4 * i + t, 1), :])
                    if bias:
                        ins = dve.tensor_scalar(out_t, bank[t][:, :], pcol_at(bias, 4 * i + t), scale,
                                                ALU.add, ALU.mult)
                    else:
                        ins = dve.tensor_scalar(out_t, bank[t][:, :], scale, None, ALU.mult)
                    ins.then_inc(drained, 1)
                    if t % 2:
                        split_lo(dve, n0 + 2 + t // 2, i)
        return m0

    e_silu, e_prod, e_high, e_low = sem("e_silu"), sem("e_prod"), sem("e_high"), sem("e_low")
    gated = [0]

    ah = at("ah", Y, [KT, S], F32R)
    al = at("al", Y + 16 * K, [KT, S], F32R)
    q2 = at("q2", Y + 32 * K, [KT, S])
    k2 = at("k2", Y + 48 * K, [KT, S])
    v2 = at("v2", Y + 64 * K, [TT, D])
    pt2 = [at("pt2a", Y + 80 * K, [TT, S]), at("pt2b", SC_AT + 8 * K, [TT, S])]
    pr2 = at("pr2", SC_AT, [2, 2, S])
    dist = at("dist", SC_AT + 16 * K, [S], F32R)
    dg2 = at("dg2", SC_AT + 18 * K, [2, P], F32R)
    S2 = SC_AT + 19 * K
    nm2 = at("nm2", S2, [2, 2])
    sm2 = at("sm2", S2 + 32, [2, 2])
    rs2 = at("rs2", S2 + 64, [2, 2])
    nlam = at("nlam", S2 + 96, [4])
    lprod = at("lprod", S2 + 128, [2])
    rta = at("rta", S2 + 160, [TT, DA_H])
    rra = at("rra", S2 + 288, [TT, DA_H])
    distf = at("distf", SC_AT, [S])
    d_ready, l_prod, l_sum, l_exp, l_lam = (sem("d_ready"), sem("l_prod"), sem("l_sum"),
                                                    sem("l_exp"), sem("l_lam"))
    dg_done, s2_done, s2_max, p2_exp, p2_done = sem("dg_done"), sem("s2_done"), sem("s2_max"), sem("p2_exp"), sem("p2_done")
    t2_done, t2_act, t2_dve, pv2_done, o2_out = (sem("t2_done"), sem("t2_act"), sem("t2_dve"), sem("pv2_done"),
                                                 sem("o2_out"))
    a_sq, a_used, a_root, a_rec, a_spread, a_out = (sem("a_sq"), sem("a_used"), sem("a_root"), sem("a_rec"),
                                                    sem("a_spread"), sem("a_out"))
    sqa = at("sqa", SC_AT, [2, S])

    def diff_values():
        n0, m0 = new_items(4), new_tiles(KT)
        mat = w["w_in_a_2"]

        @block.sync
        def _(sp):
            with sp.Fori(0, 2) as i:
                for j in range(2):
                    load_item(sp, n0 + j, i, full_item(n0 + j, mat, 0, OFF_V2 + IC * j + 2 * IC * i))

        @block.tensor
        def _(pe):
            pe.wait_ge(drained, m0)
            with pe.Fori(0, 2) as i:
                for j in range(2):
                    item_ready(pe, n0 + j, i)
                    for half in range(2):
                        pe.wait_ge(drained, m0 - 4 + 2 * j + half + 1 + 4 * i)
                        for t in range(2):
                            mm = rows_of(pe, n0 + j, 2 * half + t, bank[2 * j + half][:, IC * t:IC * t + IC], IC)
                        mm.then_inc(tiles, 1)

        @block.scalar
        def _(act):
            with act.Fori(0, 2) as i:
                for j in range(2):
                    split_hi(act, n0 + 2 + j, i)

        @block.vector
        def _(dve):
            with dve.Fori(0, 2) as i:
                for j in range(2):
                    for half in range(2):
                        dve.wait_ge(tiles, 2 * n0 + 2 * j + half + 1 + 4 * i)
                        dve.tensor_copy(v2[:, 2 * half:2 * half + 2, bass.ds(IC * j + 2 * IC * i, IC)],
                                        bank[2 * j + half][:, :].rearrange("p (t n) -> p t n", t=2)) \
                            .then_inc(drained, 1)
                    split_lo(dve, n0 + 2 + j, i)
        return m0

    STEPS = DA_H * TT
    k2r = at("k2r", Y + 48 * K, [KT, S], F32R)
    qs2 = at("qs2", Y + 16 * K, [2, 2, S], F32R)
    kh2 = at("kh2", Y + 24 * K, [2, 2, S], F32R)
    sga = at("sga", Y, [KT, S])

    def diff_attention(m1):
        sl = slopes(DA_H)
        n0, m0, q0 = new_items(4), new_tiles(KT), KT * gated[0]
        gated[0] += 1
        QB = NH // 2

        @block.sync
        def _(sp):
            with sp.Fori(0, 2) as i:
                for j in range(2):
                    load_item(sp, n0 + j, i, full_item(n0 + j, w["w_in_a_2"], 0, OFF_GA + IC * j + 2 * IC * i))

        @block.tensor
        def _(pe):
            pe.wait_ge(l_prod, 1)
            pe.matmul(bank[4][:, 0:2], ones[:, :], lprod[:, :], start=True, stop=True).then_inc(l_sum, 1)
            pe.wait_ge(l_lam, 1)
            pe.wait_ge(drained, m1)
            pe.wait_ge(d_ready, 1)

            def scores(u):
                h, i = u // TT, u % TT
                wd = P * (i + 1)
                if i == 0:
                    pe.wait_ge(dg_done, h + 1)
                    pe.wait_ge(q_lo, QB + h + 1)
                for m in range(2):
                    rows = slice(HD * m, HD * m + HD)
                    if u >= 2:
                        pe.wait_ge(p2_exp, 2 * (u - 2) + m + 1)
                    out = bank[2 * (u % 2) + m][:, 0:wd]
                    pe.matmul(out, qs2[:, h % 2, m, P * i:P * i + P], kh2[:, h % 2, m, 0:wd], start=True, stop=False)
                    pe.matmul(out, qs2[rows, h % 2, m, P * i:P * i + P], k2r[rows, h, 0:wd], start=False, stop=False)
                    pe.matmul(out, dg2[:, h % 2, :], dist[:, S - wd:S], start=False, stop=True).then_inc(s2_done, 1)

            def turn(u):
                i = u % TT
                pe.wait_ge(p2_done, u + 1)
                if u >= 2:
                    pe.wait_ge(t2_dve if u % 2 else t2_act, u // 2)
                for j in range(i + 1):
                    mm = pe.transpose(bank[4 + u % 2][:, P * j:P * j + P], pr2[:, u % 2, 0, P * j:P * j + P],
                                      ident[:, :])
                mm.then_inc(t2_done, 1)

            def values(h):
                pe.wait_ge(t2_act, 2 * h + 2)
                pe.wait_ge(t2_dve, 2 * h + 2)
                if h:
                    pe.wait_ge(o2_out, h)
                for j in range(TT):
                    mm = pe.matmul(bank[6][:, P * j:S], v2[:, j, P * h:P * h + P], pt2[h % 2][:, j, P * j:S],
                                   start=(j == 0), stop=(j == TT - 1))
                mm.then_inc(pv2_done, 1)

            def gate_part(u):
                h, i = u // TT, u % TT
                if i == 0:
                    if h % 2 == 0:
                        item_ready(pe, n0 + h // 2)
                    pe.wait_ge(drained, m0 + h)
                mm = tile_of(pe, n0 + h // 2, h % 2, bank[7][:, :], H, kts=2, k0=2 * i, w0=2 * i, first=i == 0,
                             last=i == TT - 1)
                if i == TT - 1:
                    mm.then_inc(tiles, 1)

            scores(0)
            for u in range(STEPS + 1):
                if u:
                    turn(u - 1)
                if u + 1 < STEPS:
                    scores(u + 1)
                if u < STEPS:
                    gate_part(u)
                if u > TT and (u - 2) % TT == TT - 1:
                    values((u - 2) // TT)
            values(DA_H - 1)

        def turned(eng, u, signal, copy):
            h, i = u // TT, u % TT
            eng.wait_ge(t2_done, u + 1)
            if h >= 2:
                eng.wait_ge(pv2_done, h - 1)
            copy(pt2[h % 2][:, 0:i + 1, P * i:P * i + P],
                 bank[4 + u % 2][:, 0:P * (i + 1)].rearrange("p (j q) -> p j q", j=i + 1)).then_inc(signal, 1)

        @block.scalar
        def _(act):
            act.wait_ge(drained, m1)
            act.dma_start(distf[:, :], con[:, CCOL["dist"]:CCOL["dist"] + S]).then_inc(got_con, 16)
            act.wait_ge(got_con, CON2)
            act.activation(dist[:, :], distf[:, :], ACT.Copy).then_inc(d_ready, 1)
            act.wait_ge(l_sum, 1)
            act.activation(nlam[:, 0:2], bank[4][:, 0:2], ACT.Exp).then_inc(l_exp, 1)

            def diag(h):
                if h >= 2:
                    act.wait_ge(s2_done, 8 * (h - 1))
                act.activation(dg2[:, h % 2, :], ident[:, :], ACT.Copy, scale=sl[h]).then_inc(dg_done, 1)

            def high(h, m, what):
                rows, other = slice(HD * m, HD * m + HD), slice(HD - HD * m, P - HD * m)
                if what == "q":
                    return act.activation(qs2[rows, h % 2, m, :], q2[rows, h, :], ACT.Copy)
                return act.activation(kh2[rows if what == "k" else other, h % 2, m, :], k2[rows, h, :], ACT.Copy)

            def high_parts(h, step):
                if step == 0:
                    if h >= 2:
                        act.wait_ge(s2_done, 8 * (h - 1))
                    high(h, 0, "q")
                    high(h, 1, "q")
                    high(h, 0, "k")
                else:
                    high(h, 0, "other")
                    high(h, 1, "k")
                    high(h, 1, "other").then_inc(q_hi, 1)

            def out_head(h):
                act.wait_ge(pv2_done, h + 1)
                act.activation(q2[:, h, :], bank[6][:, :], ACT.Copy).then_inc(o2_out, 1)

            diag(0)
            act.wait_ge(d_ready, 1)
            high_parts(0, 0)
            high_parts(0, 1)
            for u in range(STEPS + 3):
                h, i = u // TT, u % TT
                if u < STEPS:
                    wd = P * (i + 1)
                    for m in range(2):
                        act.wait_ge(s2_max, 2 * u + m + 1)
                        if u >= 2:
                            act.wait_ge(t2_done, u - 1)
                        act.activation(pr2[:, u % 2, m, 0:wd], bank[2 * (u % 2) + m][:, 0:wd], ACT.Exp,
                                       bias=nm2[:, u % 2, m:m + 1],
                                       accum_out=sm2[:, u % 2, m:m + 1]).then_inc(p2_exp, 1)
                if 1 <= u <= STEPS and (u - 1) % 2 == 0:
                    turned(act, u - 1, t2_act, lambda o, s_: act.activation(o, s_, ACT.Copy))
                if u < STEPS:
                    if i < 2 and h + 1 < DA_H:
                        high_parts(h + 1, i)
                        if i == 0:
                            diag(h + 1)
                    if i == 2 and h % 2 == 0 and h:
                        split_hi(act, n0 + h // 2 + 1)
                if 0 < u <= STEPS and i == 0:
                    act.wait_ge(tiles, 2 * n0 + h)
                    act.activation(sga[:, h - 1, :], bank[7][:, :], ACT.Copy).then_inc(drained, 1)
                if u > TT and (u - 3) % TT == TT - 1:
                    out_head((u - 3) // TT)
            split_hi(act, n0 + 5)

        @block.vector
        def _(dve):
            lamc = pcol("lam", 0, n=4).rearrange("p (a b) -> p a b", b=2)
            dve.tensor_tensor(lprod[:, :], lamc[:, :, 0], lamc[:, :, 1], ALU.mult).then_inc(l_prod, 1)
            dve.wait_ge(l_exp, 1)
            dve.scalar_tensor_tensor(out=nlam[:, 2:3], in0=nlam[:, 1:2], scalar=-LAMBDA_INIT, in1=nlam[:, 0:1],
                                     op0=ALU.add, op1=ALU.subtract).then_inc(l_lam, 1)
            dve.wait_ge(l_lam, 1)

            def low(h, m, what):
                rows, other = slice(HD * m, HD * m + HD), slice(HD - HD * m, P - HD * m)
                if what == "q":
                    return dve.tensor_tensor(qs2[other, h % 2, m, :], q2[rows, h, :],
                                             qs2[rows, h % 2, m, :].bitcast(F32), ALU.subtract)
                return dve.tensor_tensor(k2r[rows, h, :], k2[rows, h, :], kh2[rows, h % 2, m, :].bitcast(F32),
                                         ALU.subtract)

            def low_parts(h, what):
                dve.wait_ge(q_hi, QB + h + 1)
                low(h, 0, what)
                ins = low(h, 1, what)
                if what == "k":
                    ins.then_inc(q_lo, 1)

            low_parts(0, "q")
            low_parts(0, "k")
            for u in range(STEPS + 2):
                if u < STEPS:
                    wd = P * (u % TT + 1)
                    for m in range(2):
                        dve.wait_ge(s2_done, 2 * u + m + 1)
                        if u >= 2:
                            dve.wait_ge(p2_exp, 2 * (u - 2) + m + 1)
                        dve.tensor_reduce(nm2[:, u % 2, m:m + 1], bank[2 * (u % 2) + m][:, 0:wd], AX, ALU.max,
                                          negate=True).then_inc(s2_max, 1)
                if 1 <= u <= STEPS:
                    v = u - 1
                    wd = P * (v % TT + 1)
                    dve.wait_ge(p2_exp, 2 * v + 2)
                    r = rs2[:, v % 2, :]
                    if v:
                        dve.wait_ge(p2_done, v)
                    dch(dve, dve.reciprocal(r, sm2[:, v % 2, :]))
                    dch(dve, dve.tensor_scalar(rs2[:, v % 2, 1:2], rs2[:, v % 2, 1:2], nlam[:, 2:3], None, ALU.mult))
                    a, b = pr2[:, v % 2, 0, 0:wd], pr2[:, v % 2, 1, 0:wd]
                    dch(dve, dve.tensor_scalar(a, a, rs2[:, v % 2, 0:1], None, ALU.mult))
                    dve.scalar_tensor_tensor(out=a, in0=b, scalar=rs2[:, v % 2, 1:2], in1=a, op0=ALU.mult,
                                             op1=ALU.add).then_inc(p2_done, 1)
                if u >= 1 and (u - 1) % 2 and u <= STEPS:
                    turned(dve, u - 1, t2_dve, dve.tensor_copy)
                if u < STEPS:
                    h, i = u // TT, u % TT
                    if h + 1 < DA_H and i in (2, 3):
                        low_parts(h + 1, "q" if i == 2 else "k")
                    if i == 3 and h % 2 == 0 and h:
                        split_lo(dve, n0 + h // 2 + 1)
            split_lo(dve, n0 + 5)

        @block.scalar
        def _(act):
            act.wait_ge(t2_done, STEPS)
            act.wait_ge(o2_out, DA_H)
            act.wait_ge(drained, m0 + KT)
            for h in range(DA_H):
                act.activation(sga[:, h, :], sga[:, h, :], ACT.Silu).then_inc(e_silu, 1)
                if h >= 2:
                    act.wait_ge(a_used, h - 1)
                act.activation(sqa[:, h % 2, :], q2[:, h, :], ACT.Square).then_inc(a_sq, 1)
            act.wait_ge(a_used, DA_H)
            act.activation(rta[:, :, :], bank[4][:, 0:TT * DA_H].rearrange("p (t h) -> p t h", t=TT), ACT.Sqrt,
                           bias=eps[:, 1:2], scale=1.0 / P).then_inc(a_root, 1)
            for h in range(DA_H):
                act.wait_ge(e_prod, AHEAD + q0 + h + 1)
                act.activation(ah[:, h, :], q2[:, h, :], ACT.Copy).then_inc(e_high, 1)

        @block.tensor
        def _(pe):
            pe.wait_ge(t2_act, STEPS // 2)
            for h in range(DA_H):
                pe.wait_ge(a_sq, h + 1)
                for t in range(TT):
                    mm = pe.matmul(bank[4][:, DA_H * t + h:DA_H * t + h + 1], sqa[:, h % 2, P * t:P * t + P],
                                   ones[:, 0:1], start=True, stop=True)
                mm.then_inc(a_used, 1)
            pe.wait_ge(a_rec, 2)
            pe.wait_ge(t2_dve, STEPS // 2)
            for h in range(DA_H):
                if h >= 3:
                    pe.wait_ge(e_prod, AHEAD + q0 + h - 2)
                spread(pe, bank[5 + h % 3], lambda t: rra[:, t, h:h + 1].to_broadcast([P, P])).then_inc(a_spread, 1)

        @block.vector
        def _(dve):
            for h in range(DA_H):
                dve.wait_ge(e_silu, q0 + h + 1)
                dve.wait_ge(a_sq, h + 1)
                dve.scalar_tensor_tensor(out=q2[:, h, :], in0=q2[:, h, :], scalar=pcol("subln"), in1=sga[:, h, :],
                                         op0=ALU.mult, op1=ALU.mult).then_inc(a_out, 1)
            dve.wait_ge(a_root, 1)
            dve.reciprocal(rra[:, :, :], rta[:, :, :]).then_inc(a_rec, 1)
            dve.wait_ge(a_rec, 1)
            dve.tensor_scalar(rra[:, :, :], rra[:, :, :], 1.0 - LAMBDA_INIT, None, ALU.mult).then_inc(a_rec, 1)

            def low_out(h):
                dve.wait_ge(e_high, h + 1)
                dve.tensor_tensor(al[:, h, :], q2[:, h, :], ah[:, h, :].bitcast(F32), ALU.subtract).then_inc(e_low, 1)

            for h in range(DA_H):
                dve.wait_ge(a_spread, h + 1)
                dve.wait_ge(a_out, h + 1)
                dve.tensor_tensor(q2[:, h, :], q2[:, h, :], bank[5 + h % 3][:, :], ALU.mult).then_inc(e_prod, 1)
                if h:
                    low_out(h - 1)
            low_out(DA_H - 1)
        return (e_low, AHEAD + q0)

    xbc = at("xbc", Y + 32 * K, [12, S])
    xtok = at("xtok", Y + 56 * K, [CH, D])
    btok = at("btok", Y + 72 * K, [CH, 2, P])
    cbt = at("cbt", Y + 76 * K, [2, S])
    xpad = at("xpad", Y + 80 * K, [2, 2, CH, P])
    sel = at("sel", Y, [SSD_H, P])
    selp = at("selp", Y + 8 * K, [8, P])
    cx = at("cx", SC_AT, [2, S])
    csf = at("csf", Y + 12 * K, [S])
    dtf = at("dtf", Y + 14 * K, [S])
    caut = at("caut", Y + 16 * K, [S], F32R)
    cautf = at("cautf", Y + 18 * K, [S])
    xdec = at("xdec", Y + 20 * K, [2, D])
    daf = at("daf", Y + 28 * K, [S])
    spx = at("spx", Y + 30 * K, [S])
    prevt = at("prevt", SC_AT, [CH - 1, D])
    lm = at("lm", SC_AT + 12 * K, [2, S])
    eb = at("eb", SC_AT + 16 * K, [S])
    S3 = SC_AT + 18 * K
    cst = at("cst", S3, [CH, SSD_H])
    dtt = at("dtt", S3 + 256, [CH, SSD_H])
    ncst = at("ncst", S3 + 512, [CH, SSD_H])
    dec = at("dec", S3 + 768, [CH, SSD_H])
    wdec = at("wdec", S3 + 1024, [CH, SSD_H])
    na = at("na", S3 + 1280, [1])
    mtt = at("mtt", Y + 20 * K, [2, S])
    yo = at("yo", Y + 24 * K, [S])
    b_id, b_conv, b_silu = sem("b_id"), sem("b_conv"), sem("b_silu")
    dt_v, dt_a, cs_done, cs_t, cs_tok, cl_mm, cl_exp = (
        sem("dt_v"), sem("dt_a"), sem("cs_done"), sem("cs_t"), sem("cs_tok"), sem("cl_mm"),
        sem("cl_exp"))
    x_t, x_tok, st_w, st_mm, st_done, cb_mm, cb_done, s3_pad = (
        sem("x_t"), sem("x_tok"), sem("st_w"), sem("st_mm"), sem("st_done"), sem("cb_mm"), sem("cb_done"),
        sem("s3_pad"))
    cs_mm, cs_exp, m_done, xp_done, y_mm, y_out = (sem("cs_mm"), sem("cs_exp"), sem("m_done"), sem("xp_done"),
                                                   sem("y_mm"), sem("y_out"))

    def ssd_inputs():
        n0, m0 = new_items(7), new_tiles(13)
        mat = w["w_in_a_2"]
        v = mat.rearrange("(k p) n -> p k n", p=P)

        @block.sync
        def _(sp):
            with sp.Fori(0, 3) as i:
                for j in range(2):
                    load_item(sp, n0 + j, i, full_item(n0 + j, mat, 0, OFF_XBC + IC * j + 2 * IC * i))
            b = n0 + 6
            s_ = wraw[:, b % 2]
            load_item(sp, b, 0, [(s_[:, 0:4, 0:SSD_H], v[:, 0:4, OFF_DT:OFF_DT + SSD_H]),
                                 (s_[:, 4:8, 0:SSD_H], v[:, 4:8, OFF_DT:OFF_DT + SSD_H])])

        @block.tensor
        def _(pe):
            pe.wait_ge(drained, m0)
            with pe.Fori(0, 3) as i:
                for t in range(4):
                    if t % 2 == 0:
                        item_ready(pe, n0 + t // 2, i)
                    pe.wait_ge(drained, m0 - 4 + t + 1 + 4 * i)
                    tile_of(pe, n0 + t // 2, t % 2, bank[t][:, :], H).then_inc(tiles, 1)
            item_ready(pe, n0 + 6)
            pe.wait_ge(drained, m0 + 9)
            tile_of(pe, n0 + 6, 0, bank[0][0:SSD_H, :], H, cols=SSD_H).then_inc(tiles, 2)

        @block.scalar
        def _(act):
            act.wait_ge(tiles, 2 * n0)
            for dst, name, n in ((sel, "sel", SSD_H * P), (selp, "selp", 8 * P)):
                act.dma_start(dst[:, :, :], con[:, CCOL[name]:CCOL[name] + n].rearrange("p (h n) -> p h n", n=P)) \
                    .then_inc(got_con, 16)
            act.dma_start(cautf[:, :], con[:, CCOL["causal_t"]:CCOL["causal_t"] + S]).then_inc(got_con, 16)
            with act.Fori(0, 3) as i:
                for t in range(4):
                    act.wait_ge(tiles, 2 * n0 + t + 1 + 4 * i)
                    if t >= 2:
                        act.wait_ge(b_silu, AHEAD + t - 1 + 4 * i)
                    else:
                        act.wait_ge(b_silu, AHEAD + 4 * i)
                    act.activation(cx[:, t % 2, :], bank[t][:, :], ACT.Identity, scale=pcol_at("conv_a", 36 + t + 4 * i),
                                   bias=pcol_at("convb_a", t + 4 * i)).then_inc(b_id, 1)
                    if t % 2:
                        split_hi(act, n0 + 2 + t // 2, i)
                    act.wait_ge(b_conv, 3 * t + 3 + 12 * i)
                    act.activation(flat(xbc[:, bass.ds(4 * i + t, 1), :]), cx[:, t % 2, :],
                                   ACT.Silu).then_inc(b_silu, 1)
            split_hi(act, n0 + 8)
            act.wait_ge(got_con, CON3)
            act.activation(caut[:, :], cautf[:, :], ACT.Copy)
            act.wait_ge(dt_v, 1)
            ach(act, act.activation(spx[0:SSD_H, :], daf[0:SSD_H, :], ACT.Abs))
            ach(act, act.activation(spx[0:SSD_H, :], spx[0:SSD_H, :], ACT.Exp, scale=-1.0))
            ach(act, act.activation(spx[0:SSD_H, :], spx[0:SSD_H, :], ACT.Ln, bias=ones[0:SSD_H, 0:1]))
            act.activation(na[0:SSD_H, :], pcol("a_log", rows=SSD_H), ACT.Exp).then_inc(dt_a, 1)

        @block.vector
        def _(dve):
            with dve.Fori(0, 3) as i:
                for t in range(4):
                    dve.wait_ge(b_id, t + 1 + 4 * i)
                    for tap in range(1, 4):
                        d_ = cx[:, t % 2, tap:S]
                        dve.scalar_tensor_tensor(out=d_, in0=bank[t][:, 0:S - tap],
                                                 scalar=pcol_at("conv_a", 12 * (3 - tap) + t + 4 * i), in1=d_,
                                                 op0=ALU.mult, op1=ALU.add).then_inc(b_conv, 1)
                        dve.wait_ge(b_conv, 3 * t + tap + 12 * i)
                    dve.sem_inc(drained, 1)
                    if t % 2:
                        split_lo(dve, n0 + 2 + t // 2, i)
            split_lo(dve, n0 + 8)
            dve.wait_ge(tiles, 2 * (n0 + 7))
            dve.tensor_scalar(daf[0:SSD_H, :], bank[0][0:SSD_H, :], pcol("dt_bias", rows=SSD_H), None,
                              ALU.add).then_inc(drained, 1)
            dve.wait_ge(drained, m0 + 13)
            dve.sem_inc(dt_v, 1)
            dve.wait_ge(dt_a, 1)
            dch(dve, dve.scalar_tensor_tensor(out=dtf[0:SSD_H, :], in0=daf[0:SSD_H, :], scalar=0.0,
                                              in1=spx[0:SSD_H, :], op0=ALU.max, op1=ALU.add))
            dch(dve, dve.tensor_scalar(daf[0:SSD_H, :], dtf[0:SSD_H, :], na[0:SSD_H, :], -1.0, ALU.mult, ALU.mult))
            for c in range(CH):
                cs = slice(P * c, P * c + P)
                ins = dve.tensor_tensor_scan(csf[0:SSD_H, cs], ones[0:SSD_H, :], daf[0:SSD_H, cs], 0.0,
                                             ALU.mult, ALU.add)
            dch(dve, ins)
            dve.sem_inc(cs_done, 1)
        return m0 + 13

    bh, bl = ah, al
    sz = at("sz", Y + 26 * K, [S])
    sqb = at("sqb", Y + 28 * K, [S])
    ssb = [at("ssb0", Y + 18 * K, [S]), at("ssb1", Y + 30 * K, [S])]
    rtb = at("rtb", SC_AT + 12 * K, [2, TT])
    rrb = at("rrb", SC_AT + 12 * K + 64, [2, TT])
    hfb = at("hfb", SC_AT + 14 * K, [2, S])
    z_silu, z_prod, z_sq, z_add, z_sum, z_root, z_rec, z_spread, z_full, z_high, z_low = (
        sem(n_) for n_ in ("z_silu", "z_prod", "z_sq", "z_add", "z_sum", "z_root", "z_rec", "z_spread", "z_full",
                           "z_high", "z_low"))

    def ssd_core(m1):
        n0, m0 = new_items(4), new_tiles(KT)

        @block.sync
        def _(sp):
            with sp.Fori(0, 2) as i:
                for j in range(2):
                    load_item(sp, n0 + j, i, full_item(n0 + j, w["w_in_a_2"], 0, OFF_Z + IC * j + 2 * IC * i))

        @block.tensor
        def _(pe):
            pe.wait_ge(drained, m1)
            pe.wait_ge(b_silu, AHEAD + 12)
            for t in range(10):
                if t >= 3:
                    pe.wait_ge(x_tok, t - 2)
                for c in range(CH):
                    mm = pe.transpose(bank[5 + t % 3][:, P * c:P * c + P], xbc[:, t, P * c:P * c + P], ident[:, :])
                mm.then_inc(x_t, 1)
            for g in range(2):
                for c in range(CH):
                    cs = slice(P * c, P * c + P)
                    mm = pe.matmul(bank[2 + g][:, cs], xbc[:, 8 + g, cs], xbc[:, 10 + g, cs], start=True, stop=True)
                mm.then_inc(cb_mm, 1)
            pe.wait_ge(cs_done, 1)
            for c in range(CH):
                cs = slice(P * c, P * c + P)
                pe.transpose(bank[4][:, SSD_H * c:SSD_H * c + SSD_H], csf[0:SSD_H, cs], ident[0:SSD_H, 0:SSD_H])
                mm = pe.transpose(bank[4][:, 64 + SSD_H * c:64 + SSD_H * c + SSD_H], dtf[0:SSD_H, cs],
                                  ident[0:SSD_H, 0:SSD_H])
            mm.then_inc(cs_t, 1)
            pe.wait_ge(cs_tok, 1)
            pe.matmul(bank[4][:, 128:192], ident[:, P - 1:P].to_broadcast([P, P]),
                      cst[:, :, :].rearrange("p c h -> p (c h)"), start=True, stop=True).then_inc(cl_mm, 1)
            pe.wait_ge(x_tok, 10)
            for c in range(CH - 1):
                pe.wait_ge(st_w, c + 2)
                for g in range(2):
                    n = 2 * c + g
                    if n >= 2:
                        pe.wait_ge(st_done, n - 1)
                    pe.matmul(bank[g][:, :], btok[:, c, g, :], xdec[:, c % 2, 512 * g:512 * g + 512],
                              start=True, stop=True).then_inc(st_mm, 1)
            pe.wait_ge(got_con, CON3)
            pe.wait_ge(st_done, 6)
            pe.wait_ge(cb_done, 2)

            def sums(t):
                if t:
                    pe.wait_ge(cs_exp, 9 * t)
                for e in range(2):
                    pe.matmul(bank[e][:, :], sel[0:SSD_H, 2 * t + e, :], csf[0:SSD_H, :], start=True, stop=False)
                    pe.matmul(bank[e][:, :], identr[:, :], caut[:, :], start=False, stop=True)
                pe.matmul(bank[2][:, :], selp[0:SSD_H, t, :], csf[0:SSD_H, :], start=True, stop=True) \
                    .then_inc(cs_mm, 1)

            def outputs(t):
                pe.wait_ge(m_done, 2 * t + 2)
                pe.wait_ge(xp_done, 2 * t + 2)
                if t >= 2:
                    pe.wait_ge(y_out, t - 1)
                a, b = bank[4 + t % 2], bank[6 + t % 2]
                for c in range(CH):
                    cs = slice(P * c, P * c + P)
                    for e in range(2):
                        pe.matmul(a[:, cs], xpad[:, t % 2, e, c, :], mtt[:, e, cs], start=(e == 0), stop=(e == 1))
                for c in range(1, CH):
                    cs = slice(P * c, P * c + P)
                    mm = pe.matmul(b[:, cs], prevt[:, c - 1, P * t:P * t + P], xbc[:, 10 + t // 4, cs],
                                   start=True, stop=True)
                mm.then_inc(y_mm, 1)

            sums(0)
            for t in range(8):
                if t % 2 == 0:
                    item_ready(pe, n0 + t // 2)
                pe.wait_ge(drained, m0 + t)
                tile_of(pe, n0 + t // 2, t % 2, bank[3][:, :], H).then_inc(tiles, 1)
                if t + 1 < 8:
                    sums(t + 1)
                outputs(t)

        @block.scalar
        def _(act):
            for t in range(10):
                act.wait_ge(x_t, t + 1)
                src = bank[5 + t % 3][:, :].rearrange("p (c n) -> p c n", c=CH)
                dst = xtok[:, :, P * t:P * t + P] if t < 8 else btok[:, :, t - 8, :]
                act.activation(dst, src, ACT.Copy).then_inc(x_tok, 1)
            act.wait_ge(st_w, 1)
            act.activation(dec[:, :, :], bank[4][:, 128:192].rearrange("p (c h) -> p c h", c=CH), ACT.Exp) \
                .then_inc(cl_exp, 1)
            ach(act, act.activation(wdec[:, :, :], wdec[:, :, :], ACT.Exp))
            act.sem_inc(cl_exp, 1)

            def square(t):
                act.wait_ge(z_prod, t + 1)
                if t:
                    act.wait_ge(z_add, t)
                act.activation(sqb[:, :], xbc[:, t, :], ACT.Square).then_inc(z_sq, 1)

            for t in range(8):
                act.wait_ge(cs_mm, t + 1)
                if t:
                    act.wait_ge(m_done, 2 * t)
                for e in range(2):
                    for c in range(CH):
                        cs = slice(P * c, P * c + P)
                        act.activation(lm[:, e, cs], bank[e][:, cs], ACT.Exp,
                                       bias=ncst[:, c, 2 * t + e:2 * t + e + 1]).then_inc(cs_exp, 1)
                if t:
                    act.wait_ge(y_out, t)
                act.activation(eb[:, :], bank[2][:, :], ACT.Exp).then_inc(cs_exp, 1)
                act.wait_ge(tiles, 2 * n0 + t + 1)
                if t:
                    act.wait_ge(z_prod, t)
                act.activation(sz[:, :], bank[3][:, :], ACT.Silu).then_inc(z_silu, 1)
                if t % 2:
                    split_hi(act, n0 + 2 + t // 2)
                if t:
                    square(t - 1)
            square(7)

        @block.gpsimd
        def _(pool):
            pool.wait_ge(y_free_for_pad[0], y_free_for_pad[1])
            pool.memset(xpad[:, :, :, :, :], 0.0).then_inc(s3_pad, 1)
            pool.wait_ge(s3_pad, 1)
            pool.wait_ge(cs_tok, 1)
            pool.wait_ge(x_tok, 8)
            for t in range(8):
                if t >= 2:
                    pool.wait_ge(y_mm, t - 1)
                for e in range(2):
                    h = 2 * t + e
                    pool.tensor_tensor(xpad[:, t % 2, e, :, HD * e:HD * e + HD], xtok[:, :, HD * h:HD * h + HD],
                                       dtt[:, :, h:h + 1].to_broadcast([P, CH, HD]), ALU.mult).then_inc(xp_done, 1)

        @block.vector
        def _(dve):
            for g in range(2):
                dve.wait_ge(cb_mm, g + 1)
                dve.tensor_copy(cbt[:, g, :], bank[2 + g][:, :]).then_inc(cb_done, 1)
            dve.wait_ge(cs_t, 1)
            t4 = lambda a: bank[4][:, a:a + 64].rearrange("p (c h) -> p c h", c=CH)
            dve.tensor_copy(cst[:, :, :], t4(0))
            dve.tensor_copy(dtt[:, :, :], t4(64))
            dch(dve, dve.tensor_scalar(ncst[:, :, :], t4(0), -1.0, None, ALU.mult))
            dve.sem_inc(cs_tok, 1)
            dve.wait_ge(cl_mm, 1)
            dch(dve, dve.tensor_tensor(wdec[:, :, :], t4(128), ncst[:, :, :], ALU.add))
            dve.sem_inc(st_w, 1)
            dve.wait_ge(cl_exp, 2)
            dch(dve, dve.tensor_tensor(wdec[:, :, :], wdec[:, :, :], dtt[:, :, :], ALU.mult))
            dve.wait_ge(x_tok, 8)

            def weighted(c):
                if c >= 2:
                    dve.wait_ge(st_mm, 2 * (c - 1))
                hv = lambda a: a.rearrange("p (h d) -> p h d", d=HD)
                dve.tensor_tensor(hv(xdec[:, c % 2, :]), hv(xtok[:, c, :]),
                                  wdec[:, c, :].unsqueeze(2).to_broadcast([P, SSD_H, HD]), ALU.mult) \
                    .then_inc(st_w, 1)

            weighted(0)
            for c in range(CH - 1):
                if c + 1 < CH - 1:
                    weighted(c + 1)
                for g in range(2):
                    gs_ = slice(512 * g, 512 * g + 512)
                    dve.wait_ge(st_mm, 2 * c + g + 1)
                    if c:
                        hv = lambda a: a.rearrange("p (h d) -> p h d", d=HD)
                        dch(dve, dve.tensor_tensor(hv(prevt[:, c, gs_]), hv(prevt[:, c - 1, gs_]),
                                                   dec[:, c, 8 * g:8 * g + 8].unsqueeze(2).to_broadcast([P, 8, HD]),
                                                   ALU.mult))
                        dve.tensor_tensor(prevt[:, c, gs_], prevt[:, c, gs_], bank[g][:, :], ALU.add) \
                            .then_inc(st_done, 1)
                    else:
                        dve.tensor_copy(prevt[:, 0, gs_], bank[g][:, :]).then_inc(st_done, 1)
                dve.wait_ge(st_done, 2 * c + 2)
            dve.wait_ge(st_mm, 6)

            def masked(t):
                for e in range(2):
                    dve.wait_ge(cs_exp, 9 * t + 4 * e + 4)
                    if t:
                        dve.wait_ge(y_mm, t)
                    dve.tensor_tensor(mtt[:, e, :], lm[:, e, :], cbt[:, t // 4, :], ALU.mult).then_inc(m_done, 1)

            def combine(t):
                dve.wait_ge(y_mm, t + 1)
                dve.wait_ge(cs_exp, 9 * t + 9)
                a, b = bank[4 + t % 2], bank[6 + t % 2]
                if t:
                    dve.wait_ge(y_out, t)
                dve.tensor_tensor(yo[:, P:S], b[:, P:S], eb[:, P:S], ALU.mult)
                dch(dve, dve.scalar_tensor_tensor(out=xbc[:, t, :], in0=xbc[:, t, :], scalar=pcol("d_skip", t),
                                                  in1=a[:, :], op0=ALU.mult, op1=ALU.add))
                dve.tensor_tensor(xbc[:, t, P:S], xbc[:, t, P:S], yo[:, P:S], ALU.add).then_inc(y_out, 1)

            def add(t):
                g = t // 4
                dve.wait_ge(z_sq, t + 1)
                if t % 4 == 0:
                    dve.tensor_copy(ssb[g][:, :], sqb[:, :]).then_inc(z_add, 1)
                else:
                    dve.wait_ge(z_add, t)
                    dve.tensor_tensor(ssb[g][:, :], ssb[g][:, :], sqb[:, :], ALU.add).then_inc(z_add, 1)

            for t in range(8):
                masked(t)
                combine(t)
                dve.wait_ge(z_silu, t + 1)
                dve.sem_inc(drained, 1)
                dve.wait_ge(y_out, t + 1)
                dve.tensor_tensor(xbc[:, t, :], xbc[:, t, :], sz[:, :], ALU.mult).then_inc(z_prod, 1)
                if t % 2:
                    split_lo(dve, n0 + 2 + t // 2)
                if t:
                    add(t - 1)
            add(7)

    def ssd_norm():
        @block.tensor
        def _(pe):
            pe.wait_ge(z_add, KT)
            for g in range(2):
                for t in range(TT):
                    mm = pe.matmul(bank[4][:, TT * g + t:TT * g + t + 1], ssb[g][:, P * t:P * t + P], ones[:, 0:1],
                                   start=True, stop=True)
            mm.then_inc(z_sum, 1)
            pe.wait_ge(z_rec, 1)
            for g in range(2):
                spread(pe, bank[5 + g], lambda t: rrb[:, g, t:t + 1].to_broadcast([P, P])).then_inc(z_spread, 1)

        @block.scalar
        def _(act):
            act.wait_ge(z_sum, 1)
            act.activation(rtb[:, :, :], bank[4][:, 0:2 * TT].rearrange("p (g t) -> p g t", g=2), ACT.Sqrt,
                           bias=eps[:, 1:2], scale=2.0 / D).then_inc(z_root, 1)
            for k in range(KT):
                act.wait_ge(z_full, k + 1)
                act.activation(bh[:, k, :], hfb[:, k % 2, :], ACT.Copy).then_inc(z_high, 1)

        @block.vector
        def _(dve):
            dve.wait_ge(z_root, 1)
            dve.reciprocal(rrb[:, :, :], rtb[:, :, :]).then_inc(z_rec, 1)

            def low(k):
                dve.wait_ge(z_high, k + 1)
                dve.tensor_tensor(bl[:, k, :], hfb[:, k % 2, :], bh[:, k, :].bitcast(F32),
                                  ALU.subtract).then_inc(z_low, 1)

            for k in range(KT):
                dve.wait_ge(z_spread, k // 4 + 1)
                if k >= 2:
                    dve.wait_ge(z_low, k - 1)
                dve.scalar_tensor_tensor(out=hfb[:, k % 2, :], in0=xbc[:, k, :], scalar=pcol("ssd_norm", k),
                                         in1=bank[5 + k // 4][:, :], op0=ALU.mult, op1=ALU.mult).then_inc(z_full, 1)
                if k:
                    low(k - 1)
            low(KT - 1)
        return (z_low, 0)

    q3 = at("q3", Y + 32 * K, [KT, S])
    kdh3 = at("kdh3", Y + 48 * K, [2, S], F32R)
    kdl3 = at("kdl3", Y + 24 * K, [2, S], F32R)
    qs3 = at("qs3", Y + 16 * K, [2, 2, S], F32R)
    sg3 = at("sg3", Y, [KT, S])
    vp3 = at("vp3", Y + 52 * K, [TT, 320])
    pt3 = at("pt3", Y + 58 * K, [2, 7 * P])
    bv3 = at("bv3", Y + 66 * K, [P])
    dup3 = at("dup3", Y + 67 * K, [2, P])
    k3 = at("k3", Y + 68 * K, [S])
    dist3 = at("dist3", Y + 70 * K, [2 * P], F32R)
    dist3f = at("dist3f", Y + 71 * K, [2 * P])
    dg3 = at("dg3", Y + 72 * K, [2, 2, P], F32R)
    pr3 = at("pr3", Y + 74 * K, [2, TT, 2 * P])
    S4 = Y + 82 * K
    nm3 = at("nm3", S4, [2, TT])
    sm3 = at("sm3", S4 + 32, [2, TT])
    es3 = at("es3", S4 + 64, [2, TT])
    rs3 = at("rs3", S4 + 96, [2, TT])
    nsink = at("nsink", S4 + 128, [NH])
    k3_done, kd3_mm, kd3_done, v3_pad, c4_ready, ns_done = (
        sem(n_) for n_ in ("k3_done", "kd3_mm", "kd3_done", "v3_pad", "c4_ready", "ns_done"))
    dg3_done, s3_done, s3_max, p3_exp, p3_done, t3_done, t3_act, t3_dve, pv3_done, o3_out = (
        sem(n_) for n_ in ("dg3_done", "s3_done", "s3_max", "p3_exp", "p3_done", "t3_done", "t3_act", "t3_dve",
                           "pv3_done", "o3_out"))

    def window_kv(ready):
        n0, m0 = new_items(1), new_tiles(2)

        @block.sync
        def _(sp):
            load_item(sp, n0, 0, full_item(n0, w["w_in_c_2"], 0, OFF_KV_C))
            sp.wait_ge(z_low, KT)
            sp.dma_start(bv3[:, :], bvc.to_broadcast([P, P])).then_inc(got_con, 16)
            sp.dma_start(dup3[:, :, :], con[:, CCOL["dup0"]:CCOL["dup0"] + 256].rearrange(
                "p (g n) -> p g n", g=2)).then_inc(got_con, 16)
            sp.dma_start(dist3f[:, :], con[:, CCOL["dist2"]:CCOL["dist2"] + 256]).then_inc(got_con, 16)

        @block.gpsimd
        def _(pool):
            pool.wait_ge(z_low, KT)
            pool.memset(vp3[:, :, :], 0.0).then_inc(v3_pad, 1)

        @block.tensor
        def _(pe):
            item_ready(pe, n0)
            pe.wait_ge(drained, m0)
            tile_of(pe, n0, 0, bank[0][:, :], H, ready=ready).then_inc(tiles, 1)
            for tt in range(TT):
                mm = rows_of(pe, n0, tt, bank[1][:, P * tt:P * tt + P], P, c0=P)
            mm.then_inc(tiles, 1)
            pe.wait_ge(got_con, CON4)
            pe.wait_ge(k3_done, 1)
            for g in range(2):
                pe.matmul(bank[4 + g][:, :], dup3[:, g, :], k3[:, :], start=True, stop=True).then_inc(kd3_mm, 1)

        @block.scalar
        def _(act):
            split_hi(act, n0 + 2)
            act.wait_ge(got_con, CON4)
            act.activation(dist3[:, :], dist3f[:, :], ACT.Copy).then_inc(c4_ready, 1)
            for g in range(2):
                act.wait_ge(kd3_mm, g + 1)
                act.activation(kdh3[:, g, :], bank[4 + g][:, :], ACT.Copy).then_inc(kd3_done, 1)

        @block.vector
        def _(dve):
            dve.wait_ge(tiles, 2 * n0 + 1)
            dve.tensor_scalar(k3[:, :], bank[0][:, :], pcol("b_k"), None, ALU.add).then_inc(drained, 1)
            dve.wait_ge(drained, m0 + 1)
            dve.sem_inc(k3_done, 1)
            split_lo(dve, n0 + 2)
            dve.wait_ge(tiles, 2 * n0 + 2)
            dve.wait_ge(v3_pad, 1)
            dve.wait_ge(got_con, CON4)
            for tt in range(TT):
                dst = vp3[:, tt, HD:HD + 256].rearrange("p (g e) -> p g e", g=2)[:, :, 0:HD]
                ins = dve.tensor_tensor(dst, bank[1][:, P * tt:P * tt + P].rearrange("p (g d) -> p g d", g=2),
                                        bv3[:, :].rearrange("p (g d) -> p g d", g=2), ALU.add)
            ins.then_inc(drained, 1)
            dve.tensor_scalar(nsink[:, :], pcol("sinks", n=NH), -1.0, None, ALU.mult).then_inc(ns_done, 1)
            for g in range(2):
                dve.wait_ge(kd3_done, g + 1)
                dve.tensor_tensor(kdl3[:, g, :], bank[4 + g][:, :], kdh3[:, g, :].bitcast(F32),
                                  ALU.subtract).then_inc(kd_low, 1)

    def window_attention(m1):
        sl = slopes(NH)
        n0, m0, q0 = new_items(4), new_tiles(KT), KT * gated[0]
        gated[0] += 1
        QB = NH // 2 + DA_H

        @block.sync
        def _(sp):
            with sp.Fori(0, 2) as i:
                for j in range(2):
                    load_item(sp, n0 + j, i, full_item(n0 + j, w["w_in_c_2"], 0, OFF_G_C + IC * j + 2 * IC * i))

        @block.tensor
        def _(pe):
            pe.wait_ge(c4_ready, 1)
            pe.wait_ge(kd_low, 6)
            pe.wait_ge(drained, m1)

            def scores(h):
                e, hp, g = h % 2, h // 2, h // 8
                pe.wait_ge(dg3_done, h + 1)
                if e == 0:
                    pe.wait_ge(q_lo, QB + hp + 1)
                for i in range(TT):
                    lo = P if i == 0 else 0
                    if h >= 2:
                        pe.wait_ge(p3_exp, 5 * (h - 2) + i + 1)
                    out = bank[2 * (h % 2) + i // 2][:, 2 * P * (i % 2) + lo:2 * P * (i % 2) + 2 * P]
                    for part in (kdh3, kdl3):
                        pe.matmul(out, qs3[:, hp % 2, e, P * i:P * i + P], part[:, g, P * (i - 1) + lo:P * (i + 1)],
                                  start=(part is kdh3), stop=False)
                    pe.matmul(out, dg3[:, h % 2, 0, :], dist3[:, lo:2 * P], start=False, stop=False)
                    pe.matmul(out, dg3[:, h % 2, 1, :], dist3[:, lo:2 * P], start=False, stop=True).then_inc(s3_done, 1)

            def turn(h):
                pe.wait_ge(p3_done, 4 * h + 4)
                n = 0
                for i in range(TT):
                    if i % 2 == 0 and h:
                        pe.wait_ge(t3_dve if i else t3_act, h)
                    for j in ([0] if i == 0 else [i - 1, i]):
                        slot = n if n < 3 else n - 3
                        mm = pe.transpose(bank[4 + i // 2][:, P * slot:P * slot + P],
                                          pr3[:, h % 2, i, P * (j - i + 1):P * (j - i + 2)], ident[:, :])
                        n += 1
                    if i % 2:
                        mm.then_inc(t3_done, 1)

            def gate_part(h):
                t, part = h // 2, h % 2
                if part == 0:
                    if t % 2 == 0:
                        item_ready(pe, n0 + t // 2)
                    pe.wait_ge(drained, m0 + t)
                mm = tile_of(pe, n0 + t // 2, t % 2, bank[7][:, :], H, kts=4, k0=4 * part, w0=4 * part,
                             first=part == 0, last=part == 1)
                if part:
                    mm.then_inc(tiles, 1)

            def values(h):
                e, hp, g = h % 2, h // 2, h // 8
                pe.wait_ge(t3_act, h + 1)
                pe.wait_ge(t3_dve, h + 1)
                if e == 0 and hp:
                    pe.wait_ge(o3_out, hp)
                c0 = HD + P * g if e == 0 else P * g
                for j in range(TT):
                    n = 2 * P if j < TT - 1 else P
                    mm = pe.matmul(bank[6][:, P * j:P * j + n], vp3[:, j, c0:c0 + P],
                                   pt3[:, h % 2, 2 * P * j:2 * P * j + n], start=(e == 0 and j == 0),
                                   stop=(e == 1 and j == TT - 1), skip_group_check=True)
                mm.then_inc(pv3_done, 1)

            scores(0)
            for h in range(NH + 1):
                if h:
                    turn(h - 1)
                if h + 1 < NH:
                    scores(h + 1)
                if h < NH:
                    gate_part(h)
                if h:
                    values(h - 1)

        @block.scalar
        def _(act):
            def diag(h):
                if h >= 2:
                    act.wait_ge(s3_done, 4 * (h - 1))
                hi_ = high_part(sl[h])
                act.activation(dg3[:, h % 2, 0, :], ident[:, :], ACT.Copy, scale=hi_)
                act.activation(dg3[:, h % 2, 1, :], ident[:, :], ACT.Copy, scale=sl[h] - hi_).then_inc(dg3_done, 1)

            def queries_high(hp):
                if hp >= 2:
                    act.wait_ge(s3_done, 8 * (hp - 1))
                for e in range(2):
                    rows = slice(HD * e, HD * e + HD)
                    ins = act.activation(qs3[rows, hp % 2, e, :], q3[rows, hp, :], ACT.Copy)
                ins.then_inc(q_hi, 1)

            def out_pair(hp):
                act.wait_ge(pv3_done, 2 * hp + 2)
                act.activation(q3[:, hp, :], bank[6][:, :], ACT.Copy).then_inc(o3_out, 1)

            act.wait_ge(drained, m1)
            queries_high(0)
            diag(0)
            for h in range(NH + 2):
                if h + 1 < NH:
                    diag(h + 1)
                if h < NH:
                    act.wait_ge(s3_max, h + 1)
                    if h >= 2:
                        act.wait_ge(t3_done, 2 * (h - 1))
                    for i in range(TT):
                        lo = P if i == 0 else 0
                        act.activation(pr3[:, h % 2, i, lo:2 * P],
                                       bank[2 * (h % 2) + i // 2][:, 2 * P * (i % 2) + lo:2 * P * (i % 2) + 2 * P],
                                       ACT.Exp, bias=nm3[:, h % 2, i:i + 1],
                                       accum_out=sm3[:, h % 2, i:i + 1]).then_inc(p3_exp, 1)
                    act.activation(es3[:, h % 2, :], nm3[:, h % 2, :], ACT.Exp,
                                   bias=pcol("sinks", h)).then_inc(p3_exp, 1)
                t = h // 2 - 1
                if h % 2 == 0 and h:
                    act.wait_ge(tiles, 2 * n0 + t + 1)
                    act.activation(sg3[:, t, :], bank[7][:, :], ACT.Copy).then_inc(drained, 1)
                if 1 <= h <= NH:
                    v = h - 1
                    act.wait_ge(t3_done, 2 * v + 1)
                    if v >= 2:
                        act.wait_ge(pv3_done, v - 1)
                    act.activation(pt3[:, v % 2, 0:3 * P], bank[4][:, 0:3 * P], ACT.Copy).then_inc(t3_act, 1)
                if h % 2 and h >= 3:
                    out_pair(h // 2 - 1)
                if h % 2 == 0 and h // 2 + 1 < NH // 2:
                    queries_high(h // 2 + 1)
                if h % 4 == 0 and h:
                    split_hi(act, n0 + t // 2 + 2)

        @block.vector
        def _(dve):
            def queries_low(hp):
                dve.wait_ge(q_hi, QB + hp + 1)
                for e in range(2):
                    rows, other = slice(HD * e, HD * e + HD), slice(HD - HD * e, P - HD * e)
                    ins = dve.tensor_tensor(qs3[other, hp % 2, e, :], q3[rows, hp, :],
                                            qs3[rows, hp % 2, e, :].bitcast(F32), ALU.subtract)
                ins.then_inc(q_lo, 1)

            dve.wait_ge(ns_done, 1)
            queries_low(0)
            for h in range(NH + 2):
                if h < NH:
                    if h >= 2:
                        dve.wait_ge(p3_exp, 5 * (h - 1))
                    b0, b1 = bank[2 * (h % 2)], bank[2 * (h % 2) + 1]
                    dve.wait_ge(s3_done, 4 * h + 2)
                    dve.tensor_reduce(nm3[:, h % 2, 0:1], b0[:, P:2 * P], AX, ALU.max, negate=True)
                    dve.tensor_reduce(nm3[:, h % 2, 1:2], b0[:, 2 * P:4 * P], AX, ALU.max, negate=True)
                    dve.wait_ge(s3_done, 4 * h + 4)
                    dch(dve, dve.tensor_reduce(nm3[:, h % 2, 2:4], b1[:, :].rearrange("p (i n) -> p i n", i=2), AX,
                                               ALU.max, negate=True))
                    dve.tensor_scalar(nm3[:, h % 2, :], nm3[:, h % 2, :], nsink[:, h:h + 1], None,
                                      ALU.min).then_inc(s3_max, 1)
                if 1 <= h <= NH:
                    v = h - 1
                    dve.wait_ge(p3_exp, 5 * v + 5)
                    if v:
                        dve.wait_ge(p3_done, 4 * v)
                    dch(dve, dve.tensor_tensor(sm3[:, v % 2, :], sm3[:, v % 2, :], es3[:, v % 2, :], ALU.add))
                    dch(dve, dve.reciprocal(rs3[:, v % 2, :], sm3[:, v % 2, :]))
                    for i in range(TT):
                        part = pr3[:, v % 2, i, (P if i == 0 else 0):2 * P]
                        dve.tensor_scalar(part, part, rs3[:, v % 2, i:i + 1], None, ALU.mult).then_inc(p3_done, 1)
                    dve.wait_ge(t3_done, 2 * v + 2)
                    if v >= 2:
                        dve.wait_ge(pv3_done, v - 1)
                    dve.tensor_copy(pt3[:, v % 2, 3 * P:7 * P], bank[5][:, :]).then_inc(t3_dve, 1)
                if h % 2 == 0 and h // 2 + 1 < NH // 2:
                    queries_low(h // 2 + 1)
                if h % 4 == 1 and h > 1:
                    split_lo(dve, n0 + h // 4 + 1)

        @block.scalar
        def _(act):
            act.wait_ge(drained, m0 + KT)
            for k in range(KT):
                act.activation(sg3[:, k, :], sg3[:, k, :], ACT.Silu, bias=pcol("b_g", k)).then_inc(e_silu, 1)
            for k in range(KT):
                act.wait_ge(e_prod, AHEAD + q0 + k + 1)
                act.activation(ah[:, k, :], q3[:, k, :], ACT.Copy).then_inc(e_high, 1)

        @block.vector
        def _(dve):
            for k in range(KT + 1):
                if k < KT:
                    dve.wait_ge(e_silu, q0 + k + 1)
                    dve.wait_ge(o3_out, KT)
                    dve.tensor_tensor(q3[:, k, :], q3[:, k, :], sg3[:, k, :], ALU.mult).then_inc(e_prod, 1)
                if k:
                    dve.wait_ge(e_high, q0 + k)
                    dve.tensor_tensor(al[:, k - 1, :], q3[:, k - 1, :], ah[:, k - 1, :].bitcast(F32),
                                      ALU.subtract).then_inc(e_low, 1)
        return (e_low, AHEAD + q0)

    xw = at("xw", Y, [KT, S])
    orow = at("orow", Y + 16 * K, [TT, D])
    x_w, y_turned, y_row = sem("x_w"), sem("y_turned"), sem("y_row")

    def final_norm(m0):
        c = norms[0]

        @block.scalar
        def _(act):
            for k in range(KT):
                act.wait_ge(drained, m0 + k + 1)
                act.wait_ge(n_add, KT * c + k - 1)
                act.activation(sqn[:, k % 2, :], xt[:, k, :], ACT.Square).then_inc(n_sq, 1)
            act.wait_ge(n_sum, c + 1)
            act.activation(rtn[:, :], bank[4][:, 0:TT], ACT.Sqrt, bias=eps[:, 1:2], scale=1.0 / D).then_inc(n_root, 1)

        @block.gpsimd
        def _(pool):
            pool.wait_ge(tiles, 2 * TOTAL_ITEMS)
            for k in range(KT):
                pool.wait_ge(drained, m0 + k + 1)
                pool.tensor_scalar(xw[:, k, :], xt[:, k, :], pcol("final", k), 1.0, ALU.mult, ALU.mult) \
                    .then_inc(x_w, 1)

        @block.tensor
        def _(pe):
            pe.wait_ge(n_add, KT * c + KT)
            pe.wait_ge(drained, m0 + KT)
            for t in range(TT):
                mm = pe.matmul(bank[4][:, t:t + 1], ssn[:, P * t:P * t + P], ones[:, 0:1], start=True, stop=True)
            mm.then_inc(n_sum, 1)
            pe.wait_ge(x_w, KT)
            for t in range(TT):
                for half in range(2):
                    n = 2 * t + half
                    if n >= 4:
                        pe.wait_ge(y_row, n - 3)
                    for k in range(4):
                        mm = pe.transpose(bank[n % 4][:, P * k:P * k + P], xw[:, 4 * half + k, P * t:P * t + P],
                                          ident[:, :])
                    mm.then_inc(y_turned, 1)

        @block.vector
        def _(dve):
            dve.wait_ge(n_sq, KT * c + 1)
            dve.wait_ge(n_sum, c)
            dve.tensor_copy(ssn[:, :], sqn[:, 0, :]).then_inc(n_add, 1)
            for k in range(1, KT):
                dve.wait_ge(n_sq, KT * c + k + 1)
                dve.wait_ge(n_add, KT * c + k)
                dve.tensor_tensor(ssn[:, :], ssn[:, :], sqn[:, k % 2, :], ALU.add).then_inc(n_add, 1)
            dve.wait_ge(n_root, c + 1)
            dve.reciprocal(rrn[:, :], rtn[:, :]).then_inc(n_rec, 1)
            dve.wait_ge(n_rec, c + 1)
            for t in range(TT):
                for half in range(2):
                    n = 2 * t + half
                    dve.wait_ge(y_turned, n + 1)
                    dve.tensor_scalar(orow[:, t, 512 * half:512 * half + 512], bank[n % 4][:, :], rrn[:, t:t + 1],
                                      None, ALU.mult).then_inc(y_row, 1)

        @block.sync
        def _(sp):
            for t in range(TT):
                sp.wait_ge(y_row, 2 * t + 2)
                sp.dma_start(out[P * t:P * t + P, :], orow[:, t, :]).then_inc(stored, 16)
            sp.wait_ge(stored, 16 * TT)

    stored = sem("stored")

    mx = load_x()
    block1_kv(norm(mx, "attn_norm", 0))
    m1 = block1_q()
    block1_finish_qk(m1)
    block1_attention()
    ready = block1_merge()
    mx = residual(w["w_o"], (mh, ml), ready=ready, late=True)
    ffn_up(norm(mx, "ffn_norm", 0, late=count["item"] + 1))
    mx = ffn_down()
    wa = w["w_in_a_2"]
    project(wa, 0, q2, SCALE, ready=norm(mx, "norm_a", 1, late=count["item"] + 1))
    project(wa, OFF_K2, k2)
    m1 = diff_values() + KT
    ready = diff_attention(m1)
    mx = residual(w["w_out_a_2"], (ah, al), ready=ready)
    y_free_for_pad = (tiles, 2 * count["item"])
    ssd_core(ssd_inputs())
    mx = residual(w["w_out_a_2"], (bh, bl), r0=D, ready=ssd_norm(), late=True)
    window_kv(norm(mx, "norm_c", 1, late=count["item"] + 1))
    m1 = project(w["w_in_c_2"], 0, q3, SCALE, bias="b_q") + KT
    ready = window_attention(m1)
    mx = residual(w["w_out_c_2"], (ah, al), ready=ready, last=True)
    final_norm(mx)
    assert count["item"] == TOTAL_ITEMS, count
    ctx.close()


def kernel(**inputs):
    import concourse.bacc as _bacc
    from concourse.bass_utils import run_bass_kernel_spmd as _run

    nc = _bacc.Bacc("TRN2", target_bir_lowering=False, num_devices=1)
    arrays = {"x": np.asarray(inputs["x"])[0], "par": pack_params(inputs), "con": make_consts(),
              "bvc": np.asarray(inputs["b_in_c_2"])[:, OFF_KV_C + P:OFF_G_C]}
    for name in WEIGHTS:
        arrays[name] = np.asarray(inputs[name])[0]
    arrays = {f"in_{name}_dram": np.ascontiguousarray(a) for name, a in arrays.items()}
    aps = [nc.dram_tensor(name, a.shape, mybir.dt.from_np(a.dtype), kind="ExternalInput").ap()
           for name, a in arrays.items()]
    out = nc.dram_tensor("out_0_dram", (S, D), F32, kind="ExternalOutput").ap()
    two_blocks(nc, *aps[:4], dict(zip(WEIGHTS, aps[4:])), out)
    r = _run(nc, [arrays], core_ids=[0])
    return r.results[0]["out_0_dram"].reshape(1, S, D)
```
